# Optimizing a Trainium2 kernel written in Bass

```python
import jax, jax.numpy as jnp
from jax import lax
import numpy as np
import math

D_MODEL = 2048
BATCH = 1
SEQ = 256
DEPTH = 2

N_EVEN = (DEPTH + 1) // 2
N_ODD = DEPTH // 2

GLA_HEADS = 4
GLA_DK = 128
GLA_DV = 256
GLA_GATE_RANK = 16
GLA_TAU = 16.0
GLA_CHUNK = 64

DIL_PAIRS = ((128, 1), (512, 4), (2048, 16))
DIL_GROUPS = len(DIL_PAIRS)
DIL_HEADS = 4
DIL_HEAD_DIM = 128
DIL_BLOCK = 128

MLSTM_HEADS = 4
MLSTM_DQK = 128
MLSTM_DV = 256
MLSTM_CONV = 4
MLSTM_CHUNK = 64

MLA_HEADS = 8
MLA_Q_RANK = 512
MLA_KV_RANK = 512
MLA_NOPE = 128
MLA_ROPE = 64
MLA_DV = 128
ROPE_THETA = 10000.0
ATTN_BLOCK = 128

FFN_HIDDEN = -((-8 * D_MODEL) // (3 * 256)) * 256

DEEPNORM_ALPHA = (2.0 * DEPTH) ** 0.25
DEEPNORM_BETA = (8.0 * DEPTH) ** -0.25

GLA_QK_W = GLA_HEADS * GLA_DK
GLA_V_W = GLA_HEADS * GLA_DV
DIL_W = DIL_GROUPS * DIL_HEADS * DIL_HEAD_DIM
EVEN_SPLITS = (GLA_QK_W, GLA_QK_W, GLA_V_W, GLA_GATE_RANK, GLA_V_W, DIL_W, DIL_W, DIL_W)
EVEN_IN = sum(EVEN_SPLITS)
EVEN_OUT = GLA_V_W + DIL_HEADS * DIL_HEAD_DIM

MQK_W = MLSTM_HEADS * MLSTM_DQK
MV_W = MLSTM_HEADS * MLSTM_DV
ODD_SPLITS = (MQK_W, MQK_W, MV_W, MLSTM_HEADS, MLSTM_HEADS, MV_W, MLA_Q_RANK, MLA_KV_RANK, MLA_ROPE)
ODD_IN = sum(ODD_SPLITS)
ODD_OUT = MV_W + MLA_HEADS * MLA_DV


F32 = jnp.float32

def _split(y, sizes):
    return jnp.split(y, np.cumsum(sizes)[:-1].tolist(), axis=-1)

def layer_norm(x, g, b, eps=1e-5):
    xf = x.astype(F32)
    mu = jnp.mean(xf, -1, keepdims=True)
    var = jnp.mean(jnp.square(xf - mu), -1, keepdims=True)
    return ((xf - mu) * lax.rsqrt(var + eps) * g.astype(F32) + b.astype(F32)).astype(x.dtype)

def head_layer_norm(x, g, eps=1e-5):
    xf = x.astype(F32)
    mu = jnp.mean(xf, -1, keepdims=True)
    var = jnp.mean(jnp.square(xf - mu), -1, keepdims=True)
    return (xf - mu) * lax.rsqrt(var + eps) * g.astype(F32)

def rms_norm(x, g, eps=1e-6):
    xf = x.astype(F32)
    return (xf * lax.rsqrt(jnp.mean(xf * xf, -1, keepdims=True) + eps) * g.astype(F32)).astype(x.dtype)

def swiglu(x, w_gu, w_d):
    gate, up = jnp.split(x @ w_gu, 2, axis=-1)
    return (jax.nn.silu(gate) * up) @ w_d

def gla(q, k, v, g1, w_g2, b_g):
    B_, S_, H, dk = q.shape
    dv = v.shape[-1]
    L = GLA_CHUNK
    N = S_ // L
    log_a = jax.nn.log_sigmoid((g1 @ w_g2 + b_g).astype(F32)) / GLA_TAU
    log_a = log_a.reshape(B_, N, L, H, dk)
    q = (q.astype(F32) * dk ** -0.5).reshape(B_, N, L, H, dk)
    k = k.astype(F32).reshape(B_, N, L, H, dk)
    v = v.astype(F32).reshape(B_, N, L, H, dv)
    b = jnp.cumsum(log_a, axis=2)
    b_last = b[:, :, -1]
    q_dec = q * jnp.exp(b)
    k_inv = k * jnp.exp(-b)
    k_end = k * jnp.exp(b_last[:, :, None] - b)
    tril = jnp.tril(jnp.ones((L, L), dtype=bool))
    scores = jnp.where(tril, jnp.einsum('bnihd,bnjhd->bnhij', q_dec, k_inv), 0.0)
    o_intra = jnp.einsum('bnhij,bnjhe->bnihe', scores, v)
    s_loc = jnp.einsum('bnjhd,bnjhe->bnhde', k_end, v)

    def step(state, inp):
        decay, s_c = inp
        return state * decay[..., None] + s_c, state

    init = jnp.zeros((B_, H, dk, dv), F32)
    _, s_prev = lax.scan(step, init, (jnp.moveaxis(jnp.exp(b_last), 1, 0), jnp.moveaxis(s_loc, 1, 0)))
    s_prev = jnp.moveaxis(s_prev, 0, 1)
    o_inter = jnp.einsum('bnihd,bnhde->bnihe', q_dec, s_prev)
    return (o_intra + o_inter).reshape(B_, S_, H, dv)

def dilated_branch(q, k, v, window, dilation):
    B_, S_, H, Dh = q.shape
    span = window // dilation
    blk = DIL_BLOCK
    unit = dilation * blk
    S_pad = -((-S_) // unit) * unit
    nb = S_pad // unit

    def regroup(t):
        t = jnp.pad(t, ((0, 0), (0, S_pad - S_), (0, 0), (0, 0)))
        t = jnp.moveaxis(t.reshape(B_, S_pad // dilation, dilation, H, Dh), 2, 1)
        return t.reshape(B_, dilation, nb, blk, H, Dh)

    def with_prev(t):
        prev = jnp.pad(t, ((0, 0), (0, 0), (1, 0), (0, 0), (0, 0), (0, 0)))[:, :, :-1]
        return jnp.concatenate([prev, t], axis=3)

    qg = regroup(q)
    kb = with_prev(regroup(k))
    vb = with_prev(regroup(v))
    s = jnp.einsum('bdnihe,bdnjhe->bdnhij', qg, kb).astype(F32) * Dh ** -0.5
    qi = jnp.arange(blk)[:, None] + blk
    kj = jnp.arange(2 * blk)[None, :]
    rel = qi - kj
    band = (rel >= 0) & (rel <= span)
    no_prev = (jnp.arange(nb) == 0)[:, None, None] & (kj < blk)[None]
    valid = band[None] & ~no_prev
    s = jnp.where(valid[:, None], s, -jnp.inf)
    m = jnp.max(s, -1, keepdims=True)
    p = jnp.exp(s - m)
    den = jnp.sum(p, -1, keepdims=True)
    o = jnp.einsum('bdnhij,bdnjhe->bdnihe', p / den, vb.astype(F32))
    lse = jnp.swapaxes((m + jnp.log(den))[..., 0], 3, 4)

    def ungroup(t):
        t = t.reshape((B_, dilation, S_pad // dilation) + t.shape[4:])
        t = jnp.moveaxis(t, 1, 2)
        return t.reshape((B_, S_pad) + t.shape[3:])[:, :S_]

    return ungroup(o), ungroup(lse)

def causal_conv(u, w, b):
    C = u.shape[-1]
    K = w.shape[0]
    out = lax.conv_general_dilated(u, w[:, None, :].astype(u.dtype), window_strides=(1,),
                                   padding=[(K - 1, 0)], dimension_numbers=('NWC', 'WIO', 'NWC'),
                                   feature_group_count=C)
    return out + b

def mlstm(q, k, v, i_pre, f_pre):
    B_, S_, H, dk = q.shape
    dv = v.shape[-1]
    L = MLSTM_CHUNK
    N = S_ // L
    q = q.astype(F32).reshape(B_, N, L, H, dk)
    k = (k.astype(F32) * dk ** -0.5).reshape(B_, N, L, H, dk)
    v = v.astype(F32).reshape(B_, N, L, H, dv)
    log_f = jax.nn.log_sigmoid(f_pre.astype(F32)).reshape(B_, N, L, H)
    log_i = i_pre.astype(F32).reshape(B_, N, L, H)
    b = jnp.cumsum(log_f, axis=2)
    b_last = b[:, :, -1]
    a = b_last[:, :, None] - b + log_i
    m_loc = jnp.max(a, axis=2)
    w = jnp.exp(a - m_loc[:, :, None])
    c_loc = jnp.einsum('bnjh,bnjhd,bnjhe->bnhde', w, k, v)
    n_loc = jnp.einsum('bnjh,bnjhd->bnhd', w, k)

    def step(carry, inp):
        c, n, m = carry
        g, cl, nl, ml = inp
        m_new = jnp.maximum(g + m, ml)
        s_old = jnp.exp(g + m - m_new)
        s_new = jnp.exp(ml - m_new)
        c_new = c * s_old[..., None, None] + cl * s_new[..., None, None]
        n_new = n * s_old[..., None] + nl * s_new[..., None]
        return (c_new, n_new, m_new), (c, n, m)

    init = (jnp.zeros((B_, H, dk, dv), F32), jnp.zeros((B_, H, dk), F32), jnp.zeros((B_, H), F32))
    xs = (jnp.moveaxis(b_last, 1, 0), jnp.moveaxis(c_loc, 1, 0), jnp.moveaxis(n_loc, 1, 0), jnp.moveaxis(m_loc, 1, 0))
    _, (c_prev, n_prev, m_prev) = lax.scan(step, init, xs)
    c_prev = jnp.moveaxis(c_prev, 0, 1)
    n_prev = jnp.moveaxis(n_prev, 0, 1)
    m_prev = jnp.moveaxis(m_prev, 0, 1)

    inter_log = b + m_prev[:, :, None, :]
    d_log = b[:, :, :, None, :] - b[:, :, None, :, :] + log_i[:, :, None, :, :]
    tril = jnp.tril(jnp.ones((L, L), dtype=bool))
    d_log = jnp.where(tril[:, :, None], d_log, -jnp.inf)
    m_t = jnp.maximum(inter_log, jnp.max(d_log, axis=3))
    dmat = jnp.exp(d_log - m_t[:, :, :, None, :])
    qk = jnp.einsum('bnihd,bnjhd->bnijh', q, k) * dmat
    inter_scale = jnp.exp(inter_log - m_t)
    num = (jnp.einsum('bnijh,bnjhe->bnihe', qk, v)
           + inter_scale[..., None] * jnp.einsum('bnihd,bnhde->bnihe', q, c_prev))
    nq = jnp.sum(qk, axis=3) + inter_scale * jnp.einsum('bnihd,bnhd->bnih', q, n_prev)
    den = jnp.maximum(jnp.abs(nq), jnp.exp(-m_t))
    return (num / den[..., None]).reshape(B_, S_, H, dv)

def rope(x, cos, sin):
    half = x.shape[-1] // 2
    x1, x2 = x[..., :half], x[..., half:]
    return jnp.concatenate([x1 * cos - x2 * sin, x1 * sin + x2 * cos], axis=-1)

def causal_latent_attention(q_nope, q_rope, k_nope, k_rope, v):
    B_, S_, H, _ = q_nope.shape
    nb = S_ // ATTN_BLOCK
    scale = (MLA_NOPE + MLA_ROPE) ** -0.5
    k_pos = jnp.arange(S_)

    def blocks(t):
        return jnp.moveaxis(t.reshape((B_, nb, ATTN_BLOCK) + t.shape[2:]), 1, 0)

    def one_block(args):
        qn, qr, i = args
        s = (jnp.einsum('bihd,bjhd->bhij', qn, k_nope)
             + jnp.einsum('bihr,bjr->bhij', qr, k_rope)).astype(F32) * scale
        q_pos = i * ATTN_BLOCK + jnp.arange(ATTN_BLOCK)
        s = jnp.where(k_pos[None, :] <= q_pos[:, None], s, -jnp.inf)
        p = jax.nn.softmax(s, axis=-1)
        return jnp.einsum('bhij,bjhe->bihe', p.astype(v.dtype), v)

    o = lax.map(one_block, (blocks(q_nope), blocks(q_rope), jnp.arange(nb)))
    return jnp.moveaxis(o, 0, 1).reshape(B_, S_, H, v.shape[-1])

def mixer_even(x, w_in, gla_wg2, gla_bg, gla_norm_g, w_o):
    B_, S_, _ = x.shape
    gq, gk, gv, gg, gr, dq, dk, dv = _split(x @ w_in, EVEN_SPLITS)
    o_a = gla(gq.reshape(B_, S_, GLA_HEADS, GLA_DK), gk.reshape(B_, S_, GLA_HEADS, GLA_DK),
              gv.reshape(B_, S_, GLA_HEADS, GLA_DV), gg, gla_wg2, gla_bg)
    o_a = rms_norm(o_a, gla_norm_g) * jax.nn.silu(gr.reshape(B_, S_, GLA_HEADS, GLA_DV).astype(F32))
    grp = (B_, S_, DIL_GROUPS, DIL_HEADS, DIL_HEAD_DIM)
    dq, dk, dv = dq.reshape(grp), dk.reshape(grp), dv.reshape(grp)
    outs = []
    lses = []
    for g, (window, dilation) in enumerate(DIL_PAIRS):
        o_g, lse_g = dilated_branch(dq[:, :, g], dk[:, :, g], dv[:, :, g], window, dilation)
        outs.append(o_g)
        lses.append(lse_g)
    wts = jax.nn.softmax(jnp.stack(lses, 0), axis=0)
    o_b = jnp.sum(wts[..., None] * jnp.stack(outs, 0), axis=0)
    o = jnp.concatenate([o_a.reshape(B_, S_, -1), o_b.reshape(B_, S_, -1)], axis=-1)
    return o.astype(x.dtype) @ w_o

def mixer_odd(x, cos, sin, w_in, conv_w, conv_b, mlstm_bi, mlstm_bf, mlstm_norm_g,
              mla_qnorm_g, mla_kvnorm_g, mla_wuq, mla_wukv, w_o):
    B_, S_, _ = x.shape
    cq, ck, cv, ci, cf, co, mq, mkv, mkr = _split(x @ w_in, ODD_SPLITS)
    qk = jax.nn.silu(causal_conv(jnp.concatenate([cq, ck], -1), conv_w, conv_b))
    cq, ck = jnp.split(qk, 2, axis=-1)
    h = mlstm(cq.reshape(B_, S_, MLSTM_HEADS, MLSTM_DQK), ck.reshape(B_, S_, MLSTM_HEADS, MLSTM_DQK),
              cv.reshape(B_, S_, MLSTM_HEADS, MLSTM_DV), ci + mlstm_bi, cf + mlstm_bf)
    o_c = jax.nn.sigmoid(co.reshape(B_, S_, MLSTM_HEADS, MLSTM_DV).astype(F32)) * head_layer_norm(h, mlstm_norm_g)
    q = (rms_norm(mq, mla_qnorm_g) @ mla_wuq).reshape(B_, S_, MLA_HEADS, MLA_NOPE + MLA_ROPE)
    q_nope, q_rope = q[..., :MLA_NOPE], q[..., MLA_NOPE:]
    q_rope = rope(q_rope, cos[:, :, None, :], sin[:, :, None, :]).astype(q.dtype)
    kv = (rms_norm(mkv, mla_kvnorm_g) @ mla_wukv).reshape(B_, S_, MLA_HEADS, MLA_NOPE + MLA_DV)
    k_nope, v = kv[..., :MLA_NOPE], kv[..., MLA_NOPE:]
    k_rope = rope(mkr, cos, sin).astype(mkr.dtype)
    o_d = causal_latent_attention(q_nope, q_rope, k_nope, k_rope, v)
    o = jnp.concatenate([o_c.reshape(B_, S_, -1).astype(x.dtype), o_d.reshape(B_, S_, -1).astype(x.dtype)], axis=-1)
    return o @ w_o

def first_inputs(seed: int = 0) -> dict:
    key = jax.random.key(seed)
    ks = iter(jax.random.split(key, 32))

    def nrm(shape, fan_in, scale=1.0):
        return jax.random.normal(next(ks), shape, F32) * (scale * fan_in ** -0.5)

    def gain(shape):
        return 1.0 + 0.02 * jax.random.normal(next(ks), shape, F32)

    def small(shape, s=0.02):
        return s * jax.random.normal(next(ks), shape, F32)

    ne, no = N_EVEN, N_ODD
    x = jax.random.normal(next(ks), (BATCH, SEQ, D_MODEL), F32)
    positions = (jax.random.randint(next(ks), (BATCH, 1), 0, 1024, dtype=jnp.int32)
                 + jnp.arange(SEQ, dtype=jnp.int32)[None, :])
    return {
        'x': x,
        'positions': positions,
        'even_w_in': nrm((ne, D_MODEL, EVEN_IN), D_MODEL),
        'even_gla_wg2': nrm((ne, GLA_GATE_RANK, GLA_QK_W), GLA_GATE_RANK),
        'even_gla_bg': small((ne, GLA_QK_W), 0.1),
        'even_gla_norm_g': gain((ne, GLA_DV)),
        'even_w_o': nrm((ne, EVEN_OUT, D_MODEL), EVEN_OUT, DEEPNORM_BETA),
        'odd_w_in': nrm((no, D_MODEL, ODD_IN), D_MODEL),
        'odd_conv_w': nrm((no, MLSTM_CONV, 2 * MQK_W), MLSTM_CONV),
        'odd_conv_b': small((no, 2 * MQK_W)),
        'odd_mlstm_bi': small((no, MLSTM_HEADS), 0.1),
        'odd_mlstm_bf': jnp.linspace(3.0, 6.0, MLSTM_HEADS, dtype=F32)[None, :] + small((no, MLSTM_HEADS), 0.01),
        'odd_mlstm_norm_g': gain((no, MLSTM_DV)),
        'odd_mla_qnorm_g': gain((no, MLA_Q_RANK)),
        'odd_mla_kvnorm_g': gain((no, MLA_KV_RANK)),
        'odd_mla_wuq': nrm((no, MLA_Q_RANK, MLA_HEADS * (MLA_NOPE + MLA_ROPE)), MLA_Q_RANK),
        'odd_mla_wukv': nrm((no, MLA_KV_RANK, MLA_HEADS * (MLA_NOPE + MLA_DV)), MLA_KV_RANK),
        'odd_w_o': nrm((no, ODD_OUT, D_MODEL), ODD_OUT, DEEPNORM_BETA),
        'ln1_g': gain((DEPTH, D_MODEL)),
        'ln1_b': small((DEPTH, D_MODEL)),
        'ffn_wgu': nrm((DEPTH, D_MODEL, 2 * FFN_HIDDEN), D_MODEL),
        'ffn_wd': nrm((DEPTH, FFN_HIDDEN, D_MODEL), FFN_HIDDEN, DEEPNORM_BETA),
        'ln2_g': gain((DEPTH, D_MODEL)),
        'ln2_b': small((DEPTH, D_MODEL)),
    }

def first_block(x, positions, even_w_in, even_gla_wg2, even_gla_bg, even_gla_norm_g, even_w_o,
              odd_w_in, odd_conv_w, odd_conv_b, odd_mlstm_bi, odd_mlstm_bf, odd_mlstm_norm_g,
              odd_mla_qnorm_g, odd_mla_kvnorm_g, odd_mla_wuq, odd_mla_wukv, odd_w_o,
              ln1_g, ln1_b, ffn_wgu, ffn_wd, ln2_g, ln2_b):
    inv_freq = ROPE_THETA ** (-jnp.arange(0, MLA_ROPE, 2, dtype=F32) / MLA_ROPE)
    angles = positions.astype(F32)[..., None] * inv_freq
    cos, sin = jnp.cos(angles), jnp.sin(angles)
    for l in range(DEPTH):
        j = l // 2
        if l % 2 == 0:
            h = mixer_even(x, even_w_in[j], even_gla_wg2[j], even_gla_bg[j], even_gla_norm_g[j], even_w_o[j])
        else:
            h = mixer_odd(x, cos, sin, odd_w_in[j], odd_conv_w[j], odd_conv_b[j], odd_mlstm_bi[j],
                          odd_mlstm_bf[j], odd_mlstm_norm_g[j], odd_mla_qnorm_g[j], odd_mla_kvnorm_g[j],
                          odd_mla_wuq[j], odd_mla_wukv[j], odd_w_o[j])
        x = layer_norm(DEEPNORM_ALPHA * x + h, ln1_g[l], ln1_b[l])
        x = layer_norm(DEEPNORM_ALPHA * x + swiglu(x, ffn_wgu[l], ffn_wd[l]), ln2_g[l], ln2_b[l])
    return x


DEPTH_2 = 1

GRID_W = 64
WIN_H = 8
WIN_W = 16
Q_BLOCK = 128
HEAD_DIM = 128
NA_WIDTH = D_MODEL // 2
NA_HEADS = NA_WIDTH // HEAD_DIM
SSM_WIDTH = D_MODEL // 4
SSM_CH = 16
SSM_GROUPS = SSM_WIDTH // SSM_CH
SSM_STATE = 64
MEM_WIDTH = D_MODEL // 4
MEM_HEADS = 4
MEM_HEAD_DIM = MEM_WIDTH // MEM_HEADS
N_MEM = 256
MIX_WIDTH = NA_WIDTH + SSM_WIDTH + MEM_WIDTH
IN_WIDTH = 3 * NA_WIDTH + SSM_WIDTH + MEM_WIDTH
D_FF = 4 * D_MODEL
EPS = 1e-6
DT_MIN = 1e-3
DT_MAX = 1e-1
LAM_RE_MAX = -1e-4


def rmsnorm(x, g):
    xf = x.astype(jnp.float32)
    y = xf * lax.rsqrt(jnp.mean(xf * xf, axis=-1, keepdims=True) + EPS)
    return (y * g.astype(jnp.float32)).astype(x.dtype)

def neighbourhood_tables(S):
    rows = S // GRID_W
    kh = min(WIN_H, rows)
    kw = min(WIN_W, GRID_W)
    t = jnp.arange(S, dtype=jnp.int32)
    r = t // GRID_W
    c = t % GRID_W
    rs = jnp.clip(r - kh // 2, 0, rows - kh)
    cs = jnp.clip(c - kw // 2, 0, GRID_W - kw)
    kr = rs[:, None, None] + jnp.arange(kh, dtype=jnp.int32)[None, :, None]
    kc = cs[:, None, None] + jnp.arange(kw, dtype=jnp.int32)[None, None, :]
    nbr = (kr * GRID_W + kc).reshape(S, kh * kw)
    off = ((kr - r[:, None, None] + WIN_H - 1) * (2 * WIN_W - 1)
           + (kc - c[:, None, None] + WIN_W - 1)).reshape(S, kh * kw)
    return nbr, off

def neighbourhood_attention(q, k, v, rpb):
    B, S, H, Dh = q.shape
    nbr, off = neighbourhood_tables(S)
    nk = nbr.shape[1]
    nb = S // Q_BLOCK
    rpb_flat = rpb.reshape(H, -1).astype(jnp.float32)
    scale = Dh ** -0.5
    qb = q.reshape(B, nb, Q_BLOCK, H, Dh).transpose(1, 0, 2, 3, 4)

    def block(args):
        q_blk, idx, bidx = args
        k_g = k[:, idx]
        v_g = v[:, idx]
        s = jnp.einsum('bqhd,bqkhd->bhqk', q_blk, k_g,
                       preferred_element_type=jnp.float32) * scale + rpb_flat[:, bidx][None]
        p = jax.nn.softmax(s, axis=-1).astype(v.dtype)
        return jnp.einsum('bhqk,bqkhd->bqhd', p, v_g)

    out = lax.map(block, (qb, nbr.reshape(nb, Q_BLOCK, nk), off.reshape(nb, Q_BLOCK, nk)))
    return out.transpose(1, 0, 2, 3, 4).reshape(B, S, H * Dh)

def s5_direction(u, lam_re, lam_im, log_dt, b_re, b_im, c_re, c_im, reverse):
    lam = lax.complex(jnp.minimum(lam_re.astype(jnp.float32), LAM_RE_MAX),
                      lam_im.astype(jnp.float32))
    dt = jnp.exp(log_dt.astype(jnp.float32))[:, None]
    lam_bar = jnp.exp(lam * dt)
    b = lax.complex(b_re.astype(jnp.float32), b_im.astype(jnp.float32))
    b_bar = ((lam_bar - 1.0) / lam)[..., None] * b
    bu = jnp.einsum('bsgc,gpc->bsgp', u.astype(jnp.complex64), b_bar)
    a = jnp.broadcast_to(lam_bar, bu.shape)

    def combine(e1, e2):
        a1, x1 = e1
        a2, x2 = e2
        return a1 * a2, a2 * x1 + x2

    _, h = lax.associative_scan(combine, (a, bu), axis=1, reverse=reverse)
    c = lax.complex(c_re.astype(jnp.float32), c_im.astype(jnp.float32))
    return jnp.einsum('bsgp,gcp->bsgc', h, c).real

def s5_mixer(u_flat, lam_re, lam_im, log_dt, b_re, b_im, c_re, c_im, d, w_glu, b_glu):
    B, S, _ = u_flat.shape
    u = u_flat.reshape(B, S, SSM_GROUPS, SSM_CH).astype(jnp.float32)
    y_f = s5_direction(u, lam_re[0], lam_im[0], log_dt[0], b_re[0], b_im[0], c_re[0], c_im[0], False)
    y_b = s5_direction(u, lam_re[1], lam_im[1], log_dt[1], b_re[1], b_im[1], c_re[1], c_im[1], True)
    y = (y_f + y_b + d.astype(jnp.float32) * u).reshape(B, S, SSM_WIDTH)
    y = jax.nn.gelu(y)
    y = y * jax.nn.sigmoid(y @ w_glu.astype(jnp.float32) + b_glu.astype(jnp.float32))
    return y.astype(u_flat.dtype)

def memory_cross_attention(q_flat, mem, mem_norm, w_mem_kv):
    B, S, _ = q_flat.shape
    q = q_flat.reshape(B, S, MEM_HEADS, MEM_HEAD_DIM)
    kv = rmsnorm(mem, mem_norm) @ w_mem_kv
    M = kv.shape[1]
    k, v = jnp.split(kv, 2, axis=-1)
    k = k.reshape(B, M, MEM_HEADS, MEM_HEAD_DIM)
    v = v.reshape(B, M, MEM_HEADS, MEM_HEAD_DIM)
    s = jnp.einsum('bshd,bmhd->bhsm', q, k, preferred_element_type=jnp.float32) * MEM_HEAD_DIM ** -0.5
    p = jax.nn.softmax(s, axis=-1).astype(v.dtype)
    return jnp.einsum('bhsm,bmhd->bshd', p, v).reshape(B, S, MEM_WIDTH)

def second_inputs(seed: int = 0) -> dict:
    key = jax.random.key(seed)
    ks = jax.random.split(key, 32)
    L = DEPTH_2
    f32 = jnp.float32

    def dense(k, shape, fan_in):
        return jax.random.normal(k, shape, f32) * fan_in ** -0.5

    def gain(k, shape):
        return 1.0 + 0.02 * jax.random.normal(k, shape, f32)

    n = jnp.arange(SSM_STATE, dtype=f32)
    G, P, Cg = SSM_GROUPS, SSM_STATE, SSM_CH
    return {
        "x": jax.random.normal(ks[0], (BATCH, SEQ, D_MODEL), f32),
        "mem": jax.random.normal(ks[1], (BATCH, N_MEM, D_MODEL), f32),
        "norm_mix_pre": gain(ks[2], (L, D_MODEL)),
        "w_in": dense(ks[3], (L, D_MODEL, IN_WIDTH), D_MODEL),
        "na_rpb": 0.02 * jax.random.normal(ks[4], (L, NA_HEADS, 2 * WIN_H - 1, 2 * WIN_W - 1), f32),
        "ssm_lam_re": -0.5 + 0.01 * jax.random.normal(ks[5], (L, 2, G, P), f32),
        "ssm_lam_im": math.pi * n + 0.01 * jax.random.normal(ks[6], (L, 2, G, P), f32),
        "ssm_log_dt": jax.random.uniform(ks[7], (L, 2, G), f32, math.log(DT_MIN), math.log(DT_MAX)),
        "ssm_b_re": dense(ks[8], (L, 2, G, P, Cg), 2 * Cg),
        "ssm_b_im": dense(ks[9], (L, 2, G, P, Cg), 2 * Cg),
        "ssm_c_re": dense(ks[10], (L, 2, G, Cg, P), 2 * P),
        "ssm_c_im": dense(ks[11], (L, 2, G, Cg, P), 2 * P),
        "ssm_d": jax.random.normal(ks[12], (L, G, Cg), f32),
        "w_glu": dense(ks[13], (L, SSM_WIDTH, SSM_WIDTH), SSM_WIDTH),
        "b_glu": 0.01 * jax.random.normal(ks[14], (L, SSM_WIDTH), f32),
        "mem_norm": gain(ks[15], (L, D_MODEL)),
        "w_mem_kv": dense(ks[16], (L, D_MODEL, 2 * MEM_WIDTH), D_MODEL),
        "out_norm_na": gain(ks[17], (L, NA_WIDTH)),
        "out_norm_ssm": gain(ks[18], (L, SSM_WIDTH)),
        "out_norm_mem": gain(ks[19], (L, MEM_WIDTH)),
        "w_out": dense(ks[20], (L, MIX_WIDTH, D_MODEL), MIX_WIDTH),
        "norm_mix_post": gain(ks[21], (L, D_MODEL)),
        "norm_mlp_pre": gain(ks[22], (L, D_MODEL)),
        "w_ff1": dense(ks[23], (L, D_MODEL, D_FF), D_MODEL),
        "w_ff2": dense(ks[24], (L, D_FF, D_MODEL), D_FF),
        "norm_mlp_post": gain(ks[25], (L, D_MODEL)),
    }

def second_block(x, mem, norm_mix_pre, w_in, na_rpb, ssm_lam_re, ssm_lam_im, ssm_log_dt,
              ssm_b_re, ssm_b_im, ssm_c_re, ssm_c_im, ssm_d, w_glu, b_glu, mem_norm,
              w_mem_kv, out_norm_na, out_norm_ssm, out_norm_mem, w_out, norm_mix_post,
              norm_mlp_pre, w_ff1, w_ff2, norm_mlp_post):
    B, S, _ = x.shape
    for l in range(DEPTH_2):
        h = rmsnorm(x, norm_mix_pre[l])
        proj = h @ w_in[l]
        q_na, k_na, v_na, u_ssm, q_mem = jnp.split(
            proj, [NA_WIDTH, 2 * NA_WIDTH, 3 * NA_WIDTH, 3 * NA_WIDTH + SSM_WIDTH], axis=-1)
        hs = (B, S, NA_HEADS, HEAD_DIM)
        y_na = neighbourhood_attention(q_na.reshape(hs), k_na.reshape(hs), v_na.reshape(hs), na_rpb[l])
        y_ssm = s5_mixer(u_ssm, ssm_lam_re[l], ssm_lam_im[l], ssm_log_dt[l], ssm_b_re[l], ssm_b_im[l],
                         ssm_c_re[l], ssm_c_im[l], ssm_d[l], w_glu[l], b_glu[l])
        y_mem = memory_cross_attention(q_mem, mem, mem_norm[l], w_mem_kv[l])
        y = jnp.concatenate([rmsnorm(y_na, out_norm_na[l]),
                             rmsnorm(y_ssm, out_norm_ssm[l]),
                             rmsnorm(y_mem, out_norm_mem[l])], axis=-1)
        x = x + rmsnorm(y @ w_out[l], norm_mix_post[l])
        h = rmsnorm(x, norm_mlp_pre[l])
        f = jnp.square(jax.nn.relu(h @ w_ff1[l])) @ w_ff2[l]
        x = x + rmsnorm(f, norm_mlp_post[l])
    return x


_first_inputs = second_inputs


def second_inputs(seed=0):
    import zlib

    import numpy as np

    out = dict(_first_inputs(seed))
    spreads = {}
    factors = {}
    for name, (base, spread) in spreads.items():
        noise = np.random.default_rng([zlib.crc32(name.encode()), seed]).standard_normal(out[name].shape)
        drawn = base * np.exp(spread * noise) if base else spread * noise
        out[name] = __import__('jax').numpy.asarray(drawn.astype(out[name].dtype))
    for name, factor in factors.items():
        out[name] = (out[name] * factor).astype(out[name].dtype)
    return out


_narrow_inputs = second_inputs


def second_inputs(seed=0):

    out = dict(_narrow_inputs(seed))
    wider = {'norm_mix_pre': 3.01,
     'na_rpb': 6.47,
     'ssm_lam_re': 12.0,
     'b_glu': 12.0,
     'mem_norm': 5.88,
     'out_norm_na': 6.17,
     'out_norm_ssm': 8.79,
     'out_norm_mem': 9.28,
     'norm_mix_post': 4.21,
     'norm_mlp_pre': 4.79,
     'norm_mlp_post': 5.35}
    for name, times in wider.items():
        mean = out[name].mean()
        out[name] = (mean + times * (out[name] - mean)).astype(out[name].dtype)
    return out


def setup_inputs(seed=0):
    out = dict(first_inputs(seed))
    for name, value in second_inputs(seed + 1).items():
        if name != "x":
            out[name + "_2"] = value
    return out


def reference(
    x, positions, even_w_in, even_gla_wg2, even_gla_bg, even_gla_norm_g, even_w_o, odd_w_in,
    odd_conv_w, odd_conv_b, odd_mlstm_bi, odd_mlstm_bf, odd_mlstm_norm_g, odd_mla_qnorm_g,
    odd_mla_kvnorm_g, odd_mla_wuq, odd_mla_wukv, odd_w_o, ln1_g, ln1_b, ffn_wgu, ffn_wd, ln2_g,
    ln2_b, mem_2, norm_mix_pre_2, w_in_2, na_rpb_2, ssm_lam_re_2, ssm_lam_im_2, ssm_log_dt_2,
    ssm_b_re_2, ssm_b_im_2, ssm_c_re_2, ssm_c_im_2, ssm_d_2, w_glu_2, b_glu_2, mem_norm_2,
    w_mem_kv_2, out_norm_na_2, out_norm_ssm_2, out_norm_mem_2, w_out_2, norm_mix_post_2,
    norm_mlp_pre_2, w_ff1_2, w_ff2_2, norm_mlp_post_2,
):
    x = first_block(
        x, positions, even_w_in, even_gla_wg2, even_gla_bg, even_gla_norm_g, even_w_o, odd_w_in,
        odd_conv_w, odd_conv_b, odd_mlstm_bi, odd_mlstm_bf, odd_mlstm_norm_g, odd_mla_qnorm_g,
        odd_mla_kvnorm_g, odd_mla_wuq, odd_mla_wukv, odd_w_o, ln1_g, ln1_b, ffn_wgu, ffn_wd,
        ln2_g, ln2_b,
    )
    return second_block(
        x, mem_2, norm_mix_pre_2, w_in_2, na_rpb_2, ssm_lam_re_2, ssm_lam_im_2, ssm_log_dt_2,
        ssm_b_re_2, ssm_b_im_2, ssm_c_re_2, ssm_c_im_2, ssm_d_2, w_glu_2, b_glu_2, mem_norm_2,
        w_mem_kv_2, out_norm_na_2, out_norm_ssm_2, out_norm_mem_2, w_out_2, norm_mix_post_2,
        norm_mlp_pre_2, w_ff1_2, w_ff2_2, norm_mlp_post_2,
    )


_drawn_inputs = setup_inputs


def setup_inputs(seed=0):
    import zlib

    import numpy as np

    out = dict(_drawn_inputs(seed))
    spreads = {}
    factors = {'even_gla_bg': 6.011,
     'even_gla_norm_g': 8.0,
     'odd_conv_b': 8.0,
     'odd_mlstm_bi': 64.0,
     'odd_mlstm_norm_g': 111.268,
     'odd_mla_qnorm_g': 8.0,
     'odd_mla_kvnorm_g': 8.0,
     'ssm_lam_re_2': 200.0,
     'ssm_lam_im_2': 36.944,
     'ssm_log_dt_2': 42.504,
     'ssm_b_re_2': 51.008,
     'ssm_b_im_2': 51.752,
     'ssm_c_re_2': 50.016,
     'ssm_c_im_2': 51.064,
     'b_glu_2': 2.671,
     'na_rpb_2': 2.883}
    for name, (base, spread) in spreads.items():
        noise = np.random.default_rng([zlib.crc32(name.encode()), seed]).standard_normal(out[name].shape)
        drawn = base * np.exp(spread * noise) if base else spread * noise
        out[name] = __import__('jax').numpy.asarray(drawn.astype(out[name].dtype))
    for name, factor in factors.items():
        out[name] = (out[name] * factor).astype(out[name].dtype)
    return out
```

```python
from collections import Counter
from contextlib import ExitStack, contextmanager
import math

import numpy as np
import concourse.bass as bass
from concourse import mybir

F32 = mybir.dt.float32
F32R = mybir.dt.float32r
I32 = mybir.dt.int32
ACT = mybir.ActivationFunctionType
ALU = mybir.AluOpType
AX_X = mybir.AxisListType.X

P = 128
TOK = 256
TT = TOK // P
D = 2048
KT_D = D // P
BLK = 512
UNIT = 1024
RAW_SLOTS = 8
SPLIT_SLOTS = 4
CHUNK = 64
NEG = -1e30
TWO_PI = 2 * math.pi
ROUND = 12582912.0
TWO_PI_1 = 6.28125
TWO_PI_2 = round((TWO_PI - TWO_PI_1) * 2**20) / 2**20
TWO_PI_3 = TWO_PI - TWO_PI_1 - TWO_PI_2
PI_IN = 3.1415925
HALF_IN = 0.49999994
ALPHA = 4.0 ** 0.25

EVEN_N = 7696
ODD_N = 4168
SEC_N = 4096
HID = 5632
FF = 8192


class Count:

    def __init__(self):
        self.n = Counter()
        self.i = None
        self.per = {}
        self.end = 0

    def until(self, unit):
        return self.now("unit", unit - self.n["unit"])

    def freed(self, block):
        v = block // 2 + 1
        return v if self.i is None else v + self.i * (self.per["block"] // 2)

    def now(self, name, add=0, each=1, times=1):
        v = times * ((self.n[name] + add) // each)
        if self.i is None or not self.per.get(name):
            return v
        return v + self.i * (times * self.per[name] // each)

    @contextmanager
    def loop(self, eng, trips, per):
        start = Counter(self.n)
        with eng.Fori(0, trips) as i:
            self.i, self.per = i, per
            yield i
            self.i, self.per = None, {}
        for name in list(self.n):
            done = self.n[name] - start[name]
            assert done == per.get(name, 0), (name, done, per)
            self.n[name] += done * (trips - 1)
        self.end += per["unit"] * (trips - 1)


def units_of(kts, cols):
    most = max(1, UNIT // cols)
    n = -(-kts // most)
    size = -(-kts // n)
    return [(k, min(size, kts - k)) for k in range(0, kts, size)]


def build(nc, A, out, upto=99):
    ctx = ExitStack()
    base = -(-nc.sbuf_base // 64) * 64
    ctx.enter_context(nc.sbuf_tensor("all_sbuf", [P, (nc.sbuf_usable_end - base) // 4 - 16], F32))

    def at(name, word, shape, dt=F32):
        assert base + 4 * (word + int(np.prod(shape[1:]))) <= nc.sbuf_usable_end, name
        return nc.alloc_sbuf_tensor_at(name, shape, dt, offset=base + 4 * word)

    def sem(name):
        return ctx.enter_context(nc.semaphore(name))

    raw = at("weights_raw", 0, [P, RAW_SLOTS, UNIT])
    w_hi = at("weights_hi", 8192, [P, SPLIT_SLOTS, UNIT], F32R)
    w_lo = at("weights_lo", 12288, [P, SPLIT_SLOTS, UNIT], F32R)
    x = at("x", 16384, [P, TT, D])
    SCR = 20480
    aT_hi = at("act_hi", SCR, [P, KT_D, TOK], F32R)
    aT_lo = at("act_lo", SCR + 4096, [P, KT_D, TOK], F32R)
    hT_hi = at("hid_hi", SCR + 8192, [P, 8, TOK], F32R)
    hT_lo = at("hid_lo", SCR + 10240, [P, 8, TOK], F32R)
    CON = SCR + 12288
    ident = at("ident", CON, [P, P])
    smalls = at("smalls", CON + 128, [P, 128])
    BIG = CON + 256
    BIG_END = 53200
    n_view = [0]

    def scr(off, shape, dt=F32):
        n_view[0] += 1
        assert off + int(np.prod(shape[1:])) <= 12288
        return at(f"scratch_{n_view[0]}", SCR + off, shape, dt)

    def big(off, shape, dt=F32):
        n_view[0] += 1
        assert BIG + off + int(np.prod(shape[1:])) <= BIG_END
        return at(f"big_{n_view[0]}", BIG + off, shape, dt)

    psum = ctx.enter_context(nc.psum_tensor("psum", [P, 8, BLK], F32))

    def bank(i):
        return psum[:, i, :]

    landed = [sem(f"unit_landed{i}") for i in range(RAW_SLOTS)]
    hi_ready = sem("hi_ready")
    lo_ready = sem("lo_ready")
    w_used = sem("w_used")
    acc_free = [sem("acc_free0"), sem("acc_free1")]
    turned = sem("turned")
    turn_hi = sem("turn_hi")
    turn_free = [sem("turn_free0"), sem("turn_free1")]
    dve_step = sem("dve_step")
    act_step = sem("act_step")
    pool_step = sem("pool_step")
    att_scored = sem("att_scored")
    att_scaled = sem("att_scaled")
    att_maxed = sem("att_maxed")
    att_exped = sem("att_exped")
    att_turned = sem("att_turned")
    att_pt = sem("att_pt")
    att_pved = sem("att_pved")
    att_done = sem("att_done")
    named = {}

    def ready(name):
        if name not in named:
            named[name] = sem(name)
        return named[name]

    def unit_load(sp, c, src, cols):
        u = c.n["unit"]
        slot = u % RAW_SLOTS
        nk = src.shape[1]
        if u >= RAW_SLOTS:
            sp.wait_ge(lo_ready, c.now("unit", 1 - RAW_SLOTS))
        sp.dma_start(raw[:, slot, :nk * cols].rearrange("p (k n) -> p k n", n=cols), src).then_inc(landed[slot], 16)
        c.n["unit"] += 1

    def block_load(sp, c, w, row0, kts, col0, cols):
        for k, nk in units_of(kts, cols):
            src = w[bass.ds(row0 + k * P, nk * P), bass.ds(col0, cols)]
            unit_load(sp, c, src.rearrange("(k p) n -> p k n", p=P), cols)

    def unit_hi(act, c, size):
        u = c.n["unit"]
        act.wait_ge(landed[u % RAW_SLOTS], c.now("unit", RAW_SLOTS, RAW_SLOTS, 16))
        if u >= SPLIT_SLOTS:
            act.wait_ge(w_used, c.now("unit", 1 - SPLIT_SLOTS))
        nc.scalar.copy(w_hi[:, u % SPLIT_SLOTS, :size], raw[:, u % RAW_SLOTS, :size]).then_inc(hi_ready, 1)
        c.n["unit"] += 1

    def unit_lo(dve, c, size):
        u = c.n["unit"]
        dve.wait_ge(hi_ready, c.now("unit", 1))
        nc.vector.tensor_tensor(w_lo[:, u % SPLIT_SLOTS, :size], raw[:, u % RAW_SLOTS, :size],
                                w_hi[:, u % SPLIT_SLOTS, :size].bitcast(F32), ALU.subtract).then_inc(lo_ready, 1)
        c.n["unit"] += 1

    def block_split(one, eng, c, kts, cols, between=None):
        us = units_of(kts, cols)
        for j, (_, nk) in enumerate(us):
            if between is not None and j == (len(us) + 1) // 2:
                between()
                between = None
            one(eng, c, nk * cols)
        c.end = c.n["unit"]
        c.n["block"] += 1
        if between is not None:
            between()

    def block_mm(pe, c, kts, cols, hi, lo, k0=0):
        b = c.n["block"]
        pair = b % 2
        if b >= 2:
            pe.wait_ge(acc_free[pair], c.freed(b - 2))
        for k, nk in units_of(kts, cols):
            s = c.n["unit"] % SPLIT_SLOTS
            pe.wait_ge(lo_ready, c.now("unit", 1))
            for j in range(nk):
                wh = w_hi[:, s, j * cols:(j + 1) * cols]
                wl = w_lo[:, s, j * cols:(j + 1) * cols]
                for m in range(TT):
                    ah = hi[:, k0 + k + j, m * P:(m + 1) * P]
                    al = lo[:, k0 + k + j, m * P:(m + 1) * P]
                    o = psum[:, 2 * pair + m, :cols]
                    nc.tensor.matmul(o, ah, wh, start=(k + j == 0), stop=False)
                    nc.tensor.matmul(o, ah, wl, start=False, stop=False)
                    last = nc.tensor.matmul(o, al, wh, start=False, stop=(k + j == kts - 1))
            last.then_inc(w_used, 1)
            c.n["unit"] += 1
        c.n["block"] += 1

    def evac(eng, c, end, block, dst, do):
        eng.wait_ge(w_used, c.until(end))
        pair = block % 2
        for m in range(TT):
            last = do(m, dst(m), psum[:, 2 * pair + m, :])
        last.then_inc(acc_free[pair], 1)

    def wait_blocks(eng, c):
        b = c.n["block"]
        eng.wait_ge(acc_free[0], (b + 1) // 2)
        eng.wait_ge(acc_free[1], b // 2)

    def turn(pe, c, srcs):
        t = c.n["turn"]
        if t >= 2:
            pe.wait_ge(turn_free[t % 2], c.now("turn", 0, 2))
        at_col = 0
        for src in srcs:
            p, w = src.shape
            last = nc.tensor.transpose(psum[:w, 4 + t % 2, at_col:at_col + p], src, ident[:p, :p])
            at_col += p
        last.then_inc(turned, 1)
        c.n["turn"] += 1

    def turn_take_hi(act, c, dst):
        act.wait_ge(turned, c.now("turn", 1))
        t = c.n["turn"]
        nc.scalar.copy(dst, psum[:, 4 + t % 2, :]).then_inc(turn_hi, 1)
        c.n["turn"] += 1
        c.n["split_turn"] += 1

    def turn_take_lo(dve, c, dst, hi):
        dve.wait_ge(turn_hi, c.now("split_turn", 1))
        t = c.n["turn"]
        nc.vector.tensor_tensor(dst, psum[:, 4 + t % 2, :], hi.bitcast(F32), ALU.subtract).then_inc(turn_free[t % 2], 1)
        c.n["turn"] += 1
        c.n["split_turn"] += 1

    def turn_take(eng, c, mine, dst):
        t = c.n["turn"]
        if t % 2 == mine:
            w, n = dst.shape[0], int(np.prod(dst.shape[1:]))
            eng.wait_ge(turned, t + 1)
            src = psum[:w, 4 + t % 2, :n]
            (nc.scalar.copy if mine == 0 else nc.vector.tensor_copy)(dst, src).then_inc(turn_free[t % 2], 1)
        c.n["turn"] += 1

    def wait_turns(eng, c):
        t = c.n["turn"]
        eng.wait_ge(turn_free[0], c.now("turn", 1, 2))
        if t >= 2 or t == 2:
            eng.wait_ge(turn_free[1], c.now("turn", 0, 2))

    def turn_act(pe, c, src, kts):
        for k in range(0, kts, 2):
            turn(pe, c, [src(m, k + j) for j in range(2) for m in range(TT)])

    def take_act_hi(act, c, hi, kts, k0=0):
        for k in range(0, kts, 2):
            turn_take_hi(act, c, hi[:, k0 + k:k0 + k + 2, :].rearrange("p k t -> p (k t)"))

    def take_act_lo(dve, c, hi, lo, kts, k0=0):
        for k in range(0, kts, 2):
            turn_take_lo(dve, c, lo[:, k0 + k:k0 + k + 2, :].rearrange("p k t -> p (k t)"),
                         hi[:, k0 + k:k0 + k + 2, :].rearrange("p k t -> p (k t)"))

    def dve_link(c, ins):
        c.n["dve_step"] += 1
        ins.then_inc(dve_step, 1)
        nc.vector.wait_ge(dve_step, c.now("dve_step"))

    def act_link(c, ins):
        c.n["act_step"] += 1
        ins.then_inc(act_step, 1)
        nc.scalar.wait_ge(act_step, c.now("act_step"))

    def pool_link(c, ins):
        c.n["pool_step"] += 1
        ins.then_inc(pool_step, 1)
        nc.gpsimd.wait_ge(pool_step, c.now("pool_step"))

    def att_buf(c0):
        sc = scr(c0, [P, 2, 768])
        pb = scr(c0 + 1536, [P, 2, 768])
        pt = scr(c0 + 3072, [P, 2, 768])
        stat = scr(c0 + 4608, [P, 3, 4])
        return sc, pb, pt, stat

    def att_pe(pe, c, items):
        def scores(it, n):
            if n >= 2:
                pe.wait_ge(att_scaled, n - 1)
            flat = psum[:, 2 * (n % 2):2 * (n % 2) + 2, :].rearrange("p b n -> p (b n)")
            for col, pairs in it["parts"]:
                for j, (q, k) in enumerate(pairs):
                    last = nc.tensor.matmul(flat[:, col:col + k.shape[1]], q, k, start=(j == 0), stop=(j == len(pairs) - 1))
            last.then_inc(att_scored, 1)

        def rest(it, n):
            pe.wait_ge(att_exped, n + 1)
            if n >= 1:
                pe.wait_ge(att_pt, n)
            flat = psum[:, 4:6, :].rearrange("p b n -> p (b n)")
            for col in range(0, it["cols"], P):
                last = nc.tensor.transpose(flat[:, col:col + P], it["pb"][:, n % 2, col:col + P], ident[:])
            last.then_inc(att_turned, 1)
            pe.wait_ge(att_pt, n + 1)
            if n >= 2:
                pe.wait_ge(att_done, n - 1)
            nt = it["cols"] // P
            for j in range(nt):
                last = nc.tensor.matmul(psum[:, 6 + n % 2, :P], it["pt"][:, n % 2, j * P:(j + 1) * P], it["v"][j],
                                        start=(j == 0), stop=(j == nt - 1))
            last.then_inc(att_pved, 1)

        n0 = c.n["att"]
        scores(items[0], n0)
        for j, it in enumerate(items):
            if j + 1 < len(items):
                scores(items[j + 1], n0 + j + 1)
            rest(it, n0 + j)
        c.n["att"] += len(items)

    def att_act(act, c, items):
        def exp(it, n):
            act.wait_ge(att_maxed, n + 1)
            if n >= 2:
                act.wait_ge(att_turned, n - 1)
            nc.scalar.activation(it["pb"][:, n % 2, :it["cols"]], it["sc"][:, n % 2, :it["cols"]], ACT.Exp,
                                 bias=it["stat"][:, 0, n % 4:n % 4 + 1],
                                 accum_out=it["stat"][:, 1, n % 4:n % 4 + 1]).then_inc(att_exped, 1)

        def take(it, n):
            act.wait_ge(att_turned, n + 1)
            if n >= 2:
                act.wait_ge(att_pved, n - 1)
            flat = psum[:, 4:6, :].rearrange("p b n -> p (b n)")
            nc.scalar.copy(it["pt"][:, n % 2, :it["cols"]], flat[:, :it["cols"]]).then_inc(att_pt, 1)

        n0 = c.n["att"]
        exp(items[0], n0)
        for j, it in enumerate(items):
            if j + 1 < len(items):
                exp(items[j + 1], n0 + j + 1)
            take(it, n0 + j)
        c.n["att"] += len(items)

    def att_dve(dve, c, items):
        def scale(it, n):
            dve.wait_ge(att_scored, n + 1)
            if n >= 2:
                dve.wait_ge(att_exped, n - 1)
            flat = psum[:, 2 * (n % 2):2 * (n % 2) + 2, :].rearrange("p b n -> p (b n)")[:, :it["cols"]]
            sc = it["sc"][:, n % 2, :it["cols"]]
            if it["mask"] is None:
                nc.vector.tensor_scalar(sc, flat, it["scale"], None, ALU.mult).then_inc(att_scaled, 1)
            else:
                nc.vector.scalar_tensor_tensor(out=sc, in0=flat, scalar=it["scale"], in1=it["mask"], op0=ALU.mult,
                                               op1=ALU.add).then_inc(att_scaled, 1)
            dve.wait_ge(att_scaled, n + 1)
            top = it["stat"][:, 2, n % 4:n % 4 + 1]
            dve_link(c, nc.vector.reduce_max(top, sc, AX_X))
            nc.vector.tensor_scalar(it["stat"][:, 0, n % 4:n % 4 + 1], top, -1.0, None, ALU.mult).then_inc(att_maxed, 1)

        def finish(it, n):
            dve.wait_ge(att_pved, n + 1)
            inv = it["stat"][:, 2, n % 4:n % 4 + 1]
            dve_link(c, nc.vector.reciprocal(inv, it["stat"][:, 1, n % 4:n % 4 + 1]))
            nc.vector.tensor_scalar(it["out"], psum[:, 6 + n % 2, :P], inv, None, ALU.mult).then_inc(att_done, 1)

        n0 = c.n["att"]
        scale(items[0], n0)
        for j, it in enumerate(items):
            if j + 1 < len(items):
                scale(items[j + 1], n0 + j + 1)
            finish(it, n0 + j)
        c.n["att"] += len(items)

    proj_e = big(0, [P, TT, EVEN_N])
    dil_o = big(15392, [P, TT, 512])
    wg2 = big(16416, [16, 512])
    dil_mask = big(16928, [P, 1152])
    gla_bg = big(18080, [P, 4])
    gla_g = big(18088, [P, 256])
    chunk_pred = big(20048, [P, P], I32)
    restart = big(19024, [P, 1024])
    G_Q, G_K, G_V, G_G, G_R, D_Q, D_K, D_V = 0, 512, 1024, 2048, 2064, 3088, 4624, 6160

    vec = [big(10784, [P, D]), big(12832, [P, D])]
    eps = smalls[:, 0:1]
    one = smalls[:, 1:2]
    half_pi = smalls[:, 2:3]
    eps6 = smalls[:, 3:4]
    mean_var = smalls[:, 4:8].rearrange("p (m two) -> p m two", two=2)
    rstd = smalls[:, 8:10]
    shift = smalls[:, 10:12]
    sumsq = smalls[:, 16:24]
    rms = smalls[:, 24:32]
    stats = smalls[:, 32:80].rearrange("p (m c s) -> p m c s", m=2, s=6)

    gq = scr(0, [P, 4, TOK])
    gk = scr(1024, [P, 4, TOK])
    gke = scr(2048, [P, 1024])
    gb = scr(3072, [P, 1024])
    ge = scr(4096, [P, 1024])
    gkt = scr(5120, [P, TT, 512])
    gla_a = scr(6144, [P, 1024])
    gst = scr(7168, [P, 4, 3, 256])
    gsT = scr(10240, [P, 2, P])
    g1T = scr(10496, [16, TOK])
    gdec = scr(10752, [P, 16])
    g_o = scr(2048, [P, TT, 1024])
    gsq = scr(10768, [P, 256])
    dqT = scr(0, [P, 12, TOK])
    dkT = scr(3072, [P, 12, TOK])
    d_sc, d_pb, d_pt, d_stat = att_buf(6144)

    def att(sc, pb, pt, stat, parts, v, mask, scale, out, cols):
        return {"sc": sc, "pb": pb, "pt": pt, "stat": stat, "parts": parts, "v": v, "mask": mask, "scale": scale,
                "out": out, "cols": cols}

    def dil_items():
        items = []
        for h in range(4):
            for m in range(TT):
                nk = P * (m + 1)
                parts, vs = [], []
                for g in range(3):
                    s = 4 * g + h
                    parts.append((g * nk, [(dqT[:, s, m * P:(m + 1) * P], dkT[:, s, :nk])]))
                    vs += [proj_e[:, j, D_V + s * P:D_V + (s + 1) * P] for j in range(m + 1)]
                mask = dil_mask[:, 0:384] if m == 0 else dil_mask[:, 384:1152]
                items.append(att(d_sc, d_pb, d_pt, d_stat, parts, vs, mask, P ** -0.5,
                                 dil_o[:, m, h * P:(h + 1) * P], 3 * nk))
        return items

    proj_o = big(0, [P, TT, ODD_N])
    M_Q, M_K, M_V, M_I, M_F, M_O, L_Q, L_KV, L_KR = 0, 512, 1024, 2048, 2052, 2056, 3080, 3592, 4104
    qb = big(8336, [P, TT, 1536])
    kvb = big(11408, [P, TT, 2048])
    mla_o = big(15504, [P, TT, 1024])
    conv_w = big(17552, [P, 8, 4])
    conv_b = big(17584, [P, 8])
    gate_b = big(17592, [4, 2])
    mln_g = big(17600, [P, 256])
    qn_g = big(17856, [P, 512])
    kvn_g = big(18368, [P, 512])
    inv_freq = big(18880, [P, 32])
    mla_mask = big(18912, [P, 256])
    pos_i = big(19168, [P, TT], I32)
    pos_f = big(19176, [P, TT])
    rope_cs = big(19184, [P, 2, TT, 32])
    restart_o = big(19312, [4, 256])
    ang = big(19568, [P, 4, 64])
    lqT = scr(0, [P, 8, TOK])
    lkT = scr(2048, [P, 8, TOK])
    lqr = scr(4096, [64, 8, TOK])
    lkr = scr(6144, [64, TOK])
    l_sc, l_pb, l_pt, l_stat = att_buf(6400)
    rope_t = scr(11024, [P, 4, 256])

    def mla_items():
        items = []
        for h in range(8):
            for m in range(TT):
                nk = P * (m + 1)
                q = slice(m * P, (m + 1) * P)
                parts = [(0, [(lqT[:, h, q], lkT[:, h, :nk]), (lqr[:, h, q], lkr[:, :nk])])]
                vs = [kvb[:, j, 256 * h + 128:256 * h + 256] for j in range(m + 1)]
                mask = mla_mask[:, 128:256] if m == 0 else mla_mask[:, :]
                items.append(att(l_sc, l_pb, l_pt, l_stat, parts, vs, mask, 192 ** -0.5,
                                 mla_o[:, m, h * P:(h + 1) * P], nk))
        return items

    craw = scr(0, [P, 8, 260])
    qk = scr(2080, [P, 8, TOK])
    kw = scr(4128, [P, TT, 512])
    vaug = scr(5152, [P, TT, 4, 258])
    cst = scr(7216, [P, 4, 3, 258])
    eT = scr(10312, [P, 2, P])
    pT = scr(10568, [P, 2, P])
    qs = scr(10824, [P, 2, P])
    sE = scr(11080, [P, P])
    o257 = scr(11208, [P, 258])
    rows = big(8336, [4, 8, TOK])
    R_LI, R_LF, R_B, R_A, R_M, R_IS, R_W, R_E = range(8)
    zrow = big(10384, [4, 64])
    small4 = big(10448, [4, 32])
    m_prev, m_last, s_old, nm_last = small4[:, 0:5], small4[:, 8:12], small4[:, 16:20], small4[:, 24:28]
    head_row = big(10480, [4, 4, P])
    col6 = big(10992, [P, 6, 4])
    s_old_c = big(11016, [P, 4, 4])
    ml_mv = big(11032, [P, 8, 2])
    ml_rs = big(11048, [P, 8])
    ml_sh = big(11056, [P, 8])
    ml_st = big(11064, [P, 6])
    den = big(11072, [P, 2])
    m_o = big(11080, [P, TT, 1024])

    proj_s = big(0, [P, TT, SEC_N])
    kvm = big(8192, [P, TT, 1024])
    y = big(10240, [P, TT, D])
    pre = y
    bias = big(14336, [P, 16, 256])
    gain_a = big(14336, [P, D])
    gain_b = big(16384, [P, D])
    ssm_d = big(18432, [P, 512])
    b_glu = big(18944, [P, 512])
    mem_x = big(0, [P, TT, D])
    S_Q, S_K, S_V, S_U, S_MQ = 0, 1024, 2048, 3072, 3584
    nqT = scr(0, [P, 8, TOK])
    nkT = scr(2048, [P, 8, TOK])
    n_sc, n_pb, n_pt, n_stat = att_buf(4096)
    mqT = scr(8720, [P, 4, TOK])
    mkT = scr(9744, [P, 4, TOK])

    def second_items():
        items = []
        for h in range(8):
            for m in range(TT):
                parts = [(0, [(nqT[:, h, m * P:(m + 1) * P], nkT[:, h, :])])]
                vs = [proj_s[:, j, S_V + h * P:S_V + (h + 1) * P] for j in range(TT)]
                items.append(att(n_sc, n_pb, n_pt, n_stat, parts, vs, bias[:, 2 * h + m, :], P ** -0.5,
                                 y[:, m, h * P:(h + 1) * P], 256))
        for h in range(4):
            for m in range(TT):
                parts = [(0, [(mqT[:, h, m * P:(m + 1) * P], mkT[:, h, :])])]
                vs = [kvm[:, j, 512 + h * P:512 + (h + 1) * P] for j in range(TT)]
                items.append(att(n_sc, n_pb, n_pt, n_stat, parts, vs, None, P ** -0.5,
                                 y[:, m, 1536 + h * P:1536 + (h + 1) * P], 256))
        return items

    NDJ = 32
    uT = scr(0, [P, 4, TOK])
    bT = scr(1024, [P, 2, 2, 4, P])
    bbar = scr(3072, [P, 2, NDJ, 32])
    braw = scr(5120, [P, 2, NDJ, 32])
    cmat = scr(7168, [P, 2, NDJ, 32])
    par = scr(9216, [P, 22, NDJ])
    eb = scr(9920, [P, 2, NDJ, 16])
    fa = scr(3072, [P, NDJ, 4, 16])
    ph = [scr(5120 + 512 * j, [P, NDJ, 16]) for j in range(3)]
    steps16 = big(2048, [P, 2, NDJ, 16])
    bmul = scr(10944, [P, NDJ, 32])
    t_glu = big(0, [P, TT, BLK])
    wave = scr(5120, [P, 2, 2, TOK])
    t1 = scr(6144, [P, 2, TOK])
    t2 = scr(6656, [P, 2, TOK])
    q1 = scr(10944, [P, 2, TOK])
    q2 = scr(11456, [P, 2, TOK])
    xp = big(1024, [P, 2, TOK])
    gs = big(1536, [P, 2, TOK])
    hs = big(0, [P, 2, 2, TOK])

    ft_r = [big(0, [P, TT, BLK]), big(8192, [P, TT, BLK])]
    ft_h = [big(1024, [P, TT, 512]), big(9216, [P, TT, 1024])]
    acc_y = big(4096, [P, TT, D])
    mlp_g = [big(0, [P, D]), big(2048, [P, D])]

    def ffn(which):
        if which < 2:
            return A["ffn_wgu"][which], A["ffn_wd"][which], HID // 512, lambda ch: (ch * 512, ch * 512 + HID), 4
        return A["w_ff1_2"][0], A["w_ff2_2"][0], FF // 1024, lambda ch: (ch * 1024, ch * 1024 + 512), 8

    def ffn_body(kts):
        n = 16 + 4 * len(units_of(kts, 512))
        return {"unit": n, "block": 6, "turn": kts // 2, "split_turn": kts // 2, "hidden_h": 2 if kts == 8 else 0}

    block = ctx.enter_context(nc.Block())

    @block.sync
    def _(sp):
        c = Count()
        for m in range(TT):
            sp.dma_start(x[:, m, :], A["x"][0, m * P:(m + 1) * P, :]).then_inc(ready("x_in"), 16)

        def project(w, pairs, rest, kts=KT_D):
            block_load(sp, c, w, 0, kts, 0, BLK)
            if pairs:
                with c.loop(sp, pairs, {"unit": 16}) as i:
                    for j in range(2):
                        block_load(sp, c, w, 0, kts, (2 * i + 1 + j) * BLK, BLK)
            for col, cols in rest:
                block_load(sp, c, w, 0, kts, col, cols)

        def hidden(which):
            w1, w2, n, cols, kts = ffn(which)

            def step(ch, first=False):
                for col in cols(ch):
                    block_load(sp, c, w1, 0, KT_D, col, BLK)
                if not first:
                    for j in range(4):
                        block_load(sp, c, w2, (ch - 1) * kts * P, kts, j * BLK, BLK)
            step(0, True)
            step(1)
            with c.loop(sp, n - 2, {"unit": ffn_body(kts)["unit"]}) as i:
                step(i + 2)
            for j in range(4):
                block_load(sp, c, w2, (n - 1) * kts * P, kts, j * BLK, BLK)

        project(A["even_w_in"][0], 7, [(7680, 16)])
        project(A["even_w_o"][0], 0, [(BLK * j, BLK) for j in range(1, 4)], 12)
        if upto >= 2:
            hidden(0)
        if upto >= 3:
            project(A["odd_w_in"][0], 3, [(3584, BLK), (4096, 72)])
            project(A["odd_mla_wuq"][0], 0, [(BLK * j, BLK) for j in range(1, 3)], 4)
            project(A["odd_mla_wukv"][0], 0, [(BLK * j, BLK) for j in range(1, 4)], 4)
            project(A["odd_w_o"][0], 0, [(BLK * j, BLK) for j in range(1, 4)])
        if upto >= 4:
            hidden(1)
        if upto >= 5:
            project(A["w_mem_kv_2"][0], 0, [(BLK, BLK)])
            project(A["w_in_2"][0], 3, [(3584, BLK)])
            project(A["w_glu_2"][0], 0, [], 4)
            project(A["w_out_2"][0], 0, [(BLK * j, BLK) for j in range(1, 4)])
        if upto >= 6:
            hidden(2)
        sp.wait_ge(ready("x_out"), 1)
        for m in range(TT):
            sp.dma_start(out[0, m * P:(m + 1) * P, :], x[:, m, :]).then_inc(ready("stored"), 16)
        sp.wait_ge(ready("stored"), 16 * TT)

    @block.gpsimd
    def _(pool):
        pc = Count()

        def spread(dst, row):
            return pool.dma_start(dst, row.broadcast_to([P, row.shape[-1]]))

        for n, v in enumerate((1e-5, 1.0, math.pi / 2, 1e-6)):
            nc.gpsimd.memset(smalls[:, n:n + 1], v).then_inc(ready("consts"), 1)
        pool.dma_start(ident[:], A["c_ident"]).then_inc(ready("ident"), 16)
        for dst, src in ((chunk_pred[:], A["c_chunk_pred"]), (restart[:], A["c_restart"]), (dil_mask[:], A["c_dil_mask"]),
                         (wg2[:], A["even_gla_wg2"][0]), (gla_bg[:], A["l_gla_bg"])):
            pool.dma_start(dst, src).then_inc(ready("even_small"), 16)
        spread(gla_g[:], A["even_gla_norm_g"]).then_inc(ready("even_small"), 16)

        def vectors(name, which, layer):
            spread(vec[0][:], A[f"{which}_g"][layer:layer + 1, :]).then_inc(ready(name), 16)
            spread(vec[1][:], A[f"{which}_b"][layer:layer + 1, :]).then_inc(ready(name), 16)

        pool.wait_ge(att_done, 8)
        vectors("vec0", "ln1", 0)
        if upto >= 2:
            pool.wait_ge(ready("x_normed"), 1)
            vectors("vec1", "ln2", 0)
        if upto >= 3:
            for dst, src in ((conv_w[:], A["l_conv_w"]), (conv_b[:], A["l_conv_b"]), (gate_b[:], A["l_gate_b"]),
                             (inv_freq[:], A["c_inv_freq"]), (mla_mask[:], A["c_mla_mask"]),
                             (pos_i[:], A["l_pos"]), (restart_o[:], A["c_restart"][0:4, 0:256])):
                pool.dma_start(dst, src).then_inc(ready("odd_small"), 16)
            spread(mln_g[:], A["odd_mlstm_norm_g"]).then_inc(ready("odd_small"), 16)
            spread(qn_g[:], A["odd_mla_qnorm_g"]).then_inc(ready("odd_small"), 16)
            spread(kvn_g[:], A["odd_mla_kvnorm_g"]).then_inc(ready("odd_small"), 16)
            pool.wait_ge(ready("ml_done"), 1)
            vectors("vec2", "ln1", 1)
        if upto >= 4:
            pool.wait_ge(ready("x_normed"), 3)
            vectors("vec3", "ln2", 1)
        if upto >= 5:
            pool.wait_ge(ready("x_normed"), 4)
            for m in range(TT):
                pool.dma_start(mem_x[:, m, :], A["mem_2"][0, m * P:(m + 1) * P, :]).then_inc(ready("mem_in"), 16)
            spread(gain_a[:], A["mem_norm_2"]).then_inc(ready("mem_in"), 16)
            spread(gain_b[:], A["norm_mix_pre_2"]).then_inc(ready("mix_pre_g"), 16)
            spread(b_glu[:], A["b_glu_2"]).then_inc(ready("ssm_small"), 16)
            spread(ssm_d[:], A["l_ssm_d"]).then_inc(ready("ssm_small"), 16)
            pool.wait_ge(ready("pre_done"), 2)
            pool.dma_start(bias[:], A["l_bias"]).then_inc(ready("bias_in"), 16)
            pool.wait_ge(att_done, 8 + 16 + 24)
            for dst, src in ((braw[:], A["l_b"]), (cmat[:], A["l_c"]), (steps16[:], A["c_steps"]),
                             (par[:, 0:3, :], A["l_lam"])):
                pool.dma_start(dst, src).then_inc(ready("ssm_in"), 16)
            for j, name in enumerate(("out_norm_na_2", "out_norm_ssm_2", "out_norm_mem_2")):
                lo = (0, 1024, 1536)[j]
                spread(gain_a[:, lo:lo + (1024, 512, 512)[j]], A[name]).then_inc(ready("out_norms"), 16)
            spread(gain_b[:], A["norm_mix_post_2"]).then_inc(ready("mix_post_g"), 16)
            pool.wait_ge(ready("ssm_tab"), 2)
            for i in range(NDJ):
                dj = 16 * (i % 2) + i // 2
                if i >= 1:
                    pool.wait_ge(ready("ssm_wave"), i)
                if i >= 2:
                    pool.wait_ge(ready("ssm_h"), i - 1)
                for o, k, e in ((t1, 0, 0), (t2, 2, 1)):
                    last = nc.gpsimd.tensor_tensor(
                        o[:].rearrange("p r (a b) -> p r a b", b=16),
                        fa[:, dj, k:k + 2, :].unsqueeze(3).broadcast_to([P, 2, 16, 16]),
                        eb[:, e, dj, :].unsqueeze(1).unsqueeze(1).broadcast_to([P, 2, 16, 16]), ALU.mult)
                pool_link(pc, last)
                nc.gpsimd.tensor_tensor(wave[:, i % 2, :, :], t1[:], t2[:], ALU.add).then_inc(ready("ssm_wave"), 1)
            pool.wait_ge(ready("mix_turned"), 1)
            spread(mlp_g[0][:], A["norm_mlp_pre_2"]).then_inc(ready("mlp_pre_g"), 16)
            spread(mlp_g[1][:], A["norm_mlp_post_2"]).then_inc(ready("mlp_post_g"), 16)

    @block.scalar
    def _(act):
        c = Count()
        A_ = nc.scalar.activation
        act.wait_ge(ready("consts"), 4)

        def copy_out(col, dst, cols=BLK):
            end, b = c.end, c.n["block"] - 1

            def go():
                evac(act, c, end, b, lambda m: dst[:, m, bass.ds(col, cols)],
                     lambda m, o, s: nc.scalar.copy(o, s[:, :cols]))
            return go

        def project(dst, pairs, rest, kts=KT_D):
            block_split(unit_hi, act, c, kts, BLK)
            last, width = 0, BLK
            if pairs:
                with c.loop(act, pairs, {"unit": 16, "block": 2}) as i:
                    for j in range(2):
                        block_split(unit_hi, act, c, kts, BLK, copy_out((2 * i + j) * BLK, dst))
                last = 2 * pairs * BLK
            for col, cols in rest:
                block_split(unit_hi, act, c, kts, cols, copy_out(last, dst, width))
                last, width = col, cols
            copy_out(last, dst, width)()

        def blocks_only(n, kts):
            for _ in range(n):
                block_split(unit_hi, act, c, kts, BLK)

        def layer_norm(n):
            act.wait_ge(ready("ln_stats"), n)
            A_(rstd, mean_var[:, :, 1], ACT.Sqrt, bias=eps).then_inc(ready("ln_std"), 1)

        def hidden(which):
            w1, w2, n, cols, kts = ffn(which)
            r, h = ft_r[which // 2], ft_h[which // 2]

            def take_block(end, b, col, before):
                if which < 2:
                    if before is not None:
                        act.wait_ge(acc_free[before % 2], c.freed(before))
                    evac(act, c, end, b, lambda m: r[:, m, :], lambda m, o, s: A_(o, s, ACT.Silu))
                else:
                    if c.n["hidden_h"]:
                        act.wait_ge(ready("hidden_h"), c.now("hidden_h"))
                    evac(act, c, end, b, lambda m: r[:, m, :], lambda m, o, s: A_(o, s, ACT.Relu))
                    act.wait_ge(acc_free[b % 2], c.freed(b))
                    for m in range(TT):
                        last = A_(h[:, m, col:col + BLK], r[:, m, :], ACT.Square)
                    last.then_inc(ready("hidden_h"), 1)
                    c.n["hidden_h"] += 1

            def step(ch, last_second=None):
                start = c.n["block"]
                block_split(unit_hi, act, c, KT_D, BLK)
                end0 = c.end

                def mid():
                    if last_second is not None:
                        take_act_hi(act, c, hT_hi, kts)
                    take_block(end0, start, 0, last_second)
                block_split(unit_hi, act, c, KT_D, BLK, mid)
                end1 = c.end
                second = (lambda: take_block(end1, start + 1, BLK, None)) if which == 2 else None
                if last_second is None:
                    if second:
                        second()
                else:
                    for j in range(4):
                        block_split(unit_hi, act, c, kts, BLK, second if j == 0 else None)
            step(0)
            step(1, c.n["block"] - 1)
            with c.loop(act, n - 2, ffn_body(kts)) as i:
                step(i + 2, c.n["block"] - 5)
            take_act_hi(act, c, hT_hi, kts)
            blocks_only(4, kts)

        def root(dst, src, eps_, scale=1.0):
            return A_(dst, src, ACT.Sqrt, bias=eps_, scale=scale)

        take_act_hi(act, c, aT_hi, KT_D)
        project(proj_e, 7, [(7680, 16)])
        for j in range(2):
            turn_take(act, c, 0, gq[:, 2 * j:2 * j + 2, :])
        for j in range(2):
            turn_take(act, c, 0, gk[:, 2 * j:2 * j + 2, :])
        turn_take(act, c, 0, g1T[:])
        act.wait_ge(ready("gla_z"), 1)
        act.wait_ge(ready("even_small"), 16 * 6)
        for h in range(4):
            last = A_(gla_a[:, h * TOK:(h + 1) * TOK], psum[:, h // 2, (h % 2) * TOK:(h % 2 + 1) * TOK], ACT.Identity,
                      bias=gla_bg[:, h:h + 1])
        act_link(c, last)
        act_link(c, A_(ge[:], gla_a[:], ACT.Abs))
        act_link(c, A_(ge[:], ge[:], ACT.Exp, scale=-1.0))
        A_(ge[:], ge[:], ACT.Ln, bias=one).then_inc(ready("gla_soft"), 1)
        act.wait_ge(ready("gla_b"), 1)
        A_(ge[:], gb[:], ACT.Exp, scale=1 / 16).then_inc(ready("gla_e"), 1)
        A_(gla_a[:], gb[:], ACT.Exp, scale=-1 / 16).then_inc(ready("gla_e"), 1)
        A_(gdec[:], gb[:].rearrange("p (n l) -> p n l", l=CHUNK)[:, :, CHUNK - 1], ACT.Exp, scale=1 / 16).then_inc(ready("gla_e"), 1)
        act.wait_ge(ready("gla_end"), 1)
        A_(gke[:], gke[:], ACT.Exp, scale=1 / 16).then_inc(ready("gla_e"), 1)
        for m in range(TT):
            turn_take(act, c, 0, gkt[:, m, :])
        for j in range(8):
            h, m = j // 2, j % 2
            act.wait_ge(ready("gla_o"), j + 1)
            act_link(c, nc.scalar.copy(g_o[:, m, h * 256:(h + 1) * 256], psum[:, 4 + j % 2, :256]))
            A_(gsq[:], g_o[:, m, h * 256:(h + 1) * 256], ACT.Square, accum_out=sumsq[:, j:j + 1]).then_inc(ready("gla_o_out"), 1)
            act.wait_ge(ready("gla_o_out"), j + 1)
        root(rms[:], sumsq[:], eps6, 1 / 256).then_inc(ready("gla_rms"), 1)
        A_(proj_e[:, :, G_R:G_R + 1024], proj_e[:, :, G_R:G_R + 1024], ACT.Silu).then_inc(ready("gla_rms"), 1)
        for s in range(0, 12, 2):
            turn_take(act, c, 0, dqT[:, s:s + 2, :])
        for s in range(0, 12, 2):
            turn_take(act, c, 0, dkT[:, s:s + 2, :])
        att_act(act, c, dil_items())
        take_act_hi(act, c, aT_hi, 12)
        blocks_only(4, 12)
        layer_norm(1)
        if upto >= 2:
            take_act_hi(act, c, aT_hi, KT_D)
            hidden(0)
            layer_norm(2)
        if upto >= 3:
            take_act_hi(act, c, aT_hi, KT_D)
            project(proj_o, 3, [(3584, BLK), (4096, 72)])
            wait_blocks(act, c)
            for m in range(TT):
                for j, col in enumerate((L_Q, L_KV)):
                    k = 2 * m + j
                    A_(rope_t[:, 0:2, :].rearrange("p a b -> p (a b)"), proj_o[:, m, col:col + 512], ACT.Square,
                       accum_out=sumsq[:, k:k + 1]).then_inc(ready("mla_sq"), 1)
                    act.wait_ge(ready("mla_sq"), k + 1)
            root(rms[:, 0:4], sumsq[:, 0:4], eps6, 1 / 512).then_inc(ready("mla_rms"), 1)
            act.wait_ge(ready("rope_ang"), 1)
            A_(rope_cs[:].rearrange("p a m r -> p (a m r)"), ang[:, 0:2, :].rearrange("p a r -> p (a r)"),
               ACT.Sin).then_inc(ready("rope_cs"), 1)
            take_act_hi(act, c, aT_hi, 8)
            project(qb, 0, [(BLK * j, BLK) for j in range(1, 3)], 4)
            project(kvb, 0, [(BLK * j, BLK) for j in range(1, 4)], 4)
            for h in range(0, 8, 2):
                turn_take(act, c, 0, lqT[:, h:h + 2, :])
            for h in range(0, 8, 2):
                turn_take(act, c, 0, lkT[:, h:h + 2, :])
            for h in range(0, 8, 2):
                turn_take(act, c, 0, lqr[:, h:h + 2, :])
            turn_take(act, c, 0, lkr[:])
            att_act(act, c, mla_items())
            for t in range(0, 8, 2):
                turn_take(act, c, 0, craw[:, t:t + 2, 3:259])
            for j in (R_LI, R_LF):
                turn_take(act, c, 0, rows[:, j, :])
            act.wait_ge(ready("ml_gates"), 1)
            act_link(c, A_(rows[:, R_B, :], rows[:, R_LF, :], ACT.Abs))
            act_link(c, A_(rows[:, R_B, :], rows[:, R_B, :], ACT.Exp, scale=-1.0))
            A_(rows[:, R_B, :], rows[:, R_B, :], ACT.Ln, bias=one[0:4, :]).then_inc(ready("ml_soft"), 1)
            act.wait_ge(ready("ml_rows"), 1)
            for n in range(4):
                ch = slice(n * CHUNK, (n + 1) * CHUNK)
                A_(rows[:, R_IS, ch], rows[:, R_M, ch], ACT.Exp, scale=-1.0, bias=m_prev[:, n:n + 1])
                A_(rows[:, R_W, ch], rows[:, R_A, ch], ACT.Exp, bias=nm_last[:, n:n + 1])
            A_(rows[:, R_E, :], rows[:, R_E, :], ACT.Exp, scale=-1.0)
            A_(s_old, s_old, ACT.Exp).then_inc(ready("ml_exps"), 1)
            act.wait_ge(ready("ml_conv"), 1)
            A_(qk[:].rearrange("p t n -> p (t n)"), qk[:].rearrange("p t n -> p (t n)"), ACT.Silu).then_inc(ready("ml_qk"), 1)
            turn_take(act, c, 0, col6[:].rearrange("p a b -> p (a b)"))
            for m in range(TT):
                turn_take(act, c, 0, kw[:, m, :])
            for j in range(8):
                h, m = j // 2, j % 2
                act.wait_ge(ready("ml_s"), j + 1)
                if j >= 2:
                    act.wait_ge(ready("ml_p"), j - 1)
                A_(eT[:, j % 2, :], psum[:, 2 + j % 2, 0:P], ACT.Exp, scale=-1.0,
                   bias=col6[:, m, h:h + 1]).then_inc(ready("ml_e"), 1)
            act.wait_ge(ready("ml_stats"), 1)
            root(ml_rs[:], ml_mv[:, :, 1], eps).then_inc(ready("ml_std"), 1)
            A_(proj_o[:, :, M_O:M_O + 1024], proj_o[:, :, M_O:M_O + 1024], ACT.Sigmoid).then_inc(ready("ml_std"), 1)
            take_act_hi(act, c, aT_hi, KT_D)
            blocks_only(4, KT_D)
            layer_norm(3)
        if upto >= 4:
            take_act_hi(act, c, aT_hi, KT_D)
            hidden(1)
            layer_norm(4)
        if upto >= 5:
            act.wait_ge(ready("mem_in"), 16 * 3)
            for m in range(TT):
                act_link(c, A_(pre[:, m, :], mem_x[:, m, :], ACT.Square, accum_out=sumsq[:, m:m + 1]))
            root(rms[:, 0:2], sumsq[:, 0:2], eps6, 1 / D).then_inc(ready("pre_rms"), 1)
            take_act_hi(act, c, aT_hi, KT_D)
            project(kvm, 0, [(BLK, BLK)])
            act.wait_ge(ready("x_normed"), 4)
            for m in range(TT):
                act_link(c, A_(pre[:, m, :], x[:, m, :], ACT.Square, accum_out=sumsq[:, m:m + 1]))
            root(rms[:, 0:2], sumsq[:, 0:2], eps6, 1 / D).then_inc(ready("pre_rms"), 1)
            take_act_hi(act, c, aT_hi, KT_D)
            project(proj_s, 3, [(3584, BLK)])
            for h in range(0, 8, 2):
                turn_take(act, c, 0, nqT[:, h:h + 2, :])
            for h in range(0, 8, 2):
                turn_take(act, c, 0, nkT[:, h:h + 2, :])
            for h in range(0, 4, 2):
                turn_take(act, c, 0, mqT[:, h:h + 2, :])
            for h in range(0, 4, 2):
                turn_take(act, c, 0, mkT[:, h:h + 2, :])
            att_act(act, c, second_items())
            for q in range(0, 4, 2):
                turn_take(act, c, 0, uT[:, q:q + 2, :])
            act.wait_ge(ready("ssm_in"), 16 * 4)
            A_(par[:, 2, :], par[:, 2, :], ACT.Exp).then_inc(ready("ssm_dt"), 1)
            act.wait_ge(ready("ssm_turns"), 1)
            A_(par[:, 8, :], par[:, 6, :], ACT.Sin)
            A_(par[:, 9, :], par[:, 7, :], ACT.Sin)
            A_(par[:, 10, :], par[:, 3, :], ACT.Exp).then_inc(ready("ssm_lam"), 1)
            for d in range(2):
                for ri in range(2):
                    turn_take(act, c, 0, bT[:, d, ri, :, :].rearrange("p q n -> p (q n)"))
            act.wait_ge(ready("ssm_ph"), 1)
            A_(eb[:, 0, :, :], ph[1][:], ACT.Sin, scale=TWO_PI)
            A_(eb[:, 1, :, :], ph[0][:], ACT.Sin, scale=TWO_PI).then_inc(ready("ssm_tab"), 1)
            act.wait_ge(ready("ssm_ph"), 2)
            A_(fa[:, :, 0, :], ph[1][:], ACT.Sin, scale=TWO_PI)
            A_(fa[:, :, 1, :], ph[0][:], ACT.Sin, scale=TWO_PI)
            A_(fa[:, :, 2, :], ph[0][:], ACT.Sin, scale=-TWO_PI)
            A_(fa[:, :, 3, :], ph[1][:], ACT.Sin, scale=TWO_PI).then_inc(ready("ssm_tab"), 1)
            act.wait_ge(ready("ssm_y"), 1)
            A_(y[:, :, 1024:1536], y[:, :, 1024:1536], ACT.Gelu_apprx_tanh).then_inc(ready("ssm_gelu"), 1)
            take_act_hi(act, c, aT_hi, 4)
            block_split(unit_hi, act, c, 4, BLK)
            act.wait_ge(ready("glu_z"), 1)
            A_(t_glu[:], t_glu[:], ACT.Sigmoid).then_inc(ready("glu_s"), 1)
            act.wait_ge(ready("ssm_out"), 1)
            for m in range(TT):
                for j, (lo, w) in enumerate(((0, 1024), (1024, 512), (1536, 512))):
                    act_link(c, A_(proj_s[:, m, 0:w], y[:, m, lo:lo + w], ACT.Square, accum_out=sumsq[:, 3 * m + j:3 * m + j + 1]))
                    last = root(rms[:, 3 * m + j:3 * m + j + 1], sumsq[:, 3 * m + j:3 * m + j + 1], eps6, 1 / w)
                    act_link(c, last)
            A_(sumsq[:, 6:7], eps, ACT.Copy).then_inc(ready("out_rms"), 1)
            take_act_hi(act, c, aT_hi, KT_D)
            project(acc_y, 0, [(BLK * j, BLK) for j in range(1, 4)])
            wait_blocks(act, c)
            for m in range(TT):
                act_link(c, A_(pre[:, m, :], acc_y[:, m, :], ACT.Square, accum_out=sumsq[:, m:m + 1]))
            root(rms[:, 0:2], sumsq[:, 0:2], eps6, 1 / D).then_inc(ready("post_rms"), 1)
        if upto >= 6:
            act.wait_ge(ready("x_normed"), 5)
            for m in range(TT):
                act_link(c, A_(pre[:, m, :], x[:, m, :], ACT.Square, accum_out=sumsq[:, m:m + 1]))
            root(rms[:, 0:2], sumsq[:, 0:2], eps6, 1 / D).then_inc(ready("pre_rms"), 1)
            take_act_hi(act, c, aT_hi, KT_D)
            hidden(2)
            act.wait_ge(ready("ffn_out"), 1)
            for m in range(TT):
                act_link(c, A_(pre[:, m, :], acc_y[:, m, :], ACT.Square, accum_out=sumsq[:, m:m + 1]))
            root(rms[:, 0:2], sumsq[:, 0:2], eps6, 1 / D).then_inc(ready("post_rms"), 1)

    @block.vector
    def _(dve):
        c = Count()
        V = nc.vector
        TS, STT, TENS = V.tensor_scalar, V.scalar_tensor_tensor, V.tensor_tensor

        def link(ins):
            dve_link(c, ins)

        def project(pairs, rest, kts=KT_D):
            block_split(unit_lo, dve, c, kts, BLK)
            if pairs:
                with c.loop(dve, pairs, {"unit": 16, "block": 2}):
                    for _ in range(2):
                        block_split(unit_lo, dve, c, kts, BLK)
            for _, cols in rest:
                block_split(unit_lo, dve, c, kts, cols)

        def add_out(end, b, dst, j, scale=None):
            def do(m, o, s):
                if scale is None:
                    return TENS(o, o, s, ALU.add)
                return STT(out=o, in0=o, scalar=scale, in1=s, op0=ALU.mult, op1=ALU.add)
            return lambda: evac(dve, c, end, b, lambda m: dst[:, m, j * BLK:(j + 1) * BLK], do)

        def residual(kts):
            out_ = None
            for j in range(4):
                block_split(unit_lo, dve, c, kts, BLK, out_)
                out_ = add_out(c.end, c.n["block"] - 1, x, j, ALPHA)
            out_()

        def layer_norm(n, vec_name):
            wait_blocks(dve, c)
            for m in range(TT):
                for j in range(4):
                    last = V.bn_stats(stats[:, m, :, :].rearrange("p c s -> p (c s)")[:, 6 * j:6 * j + 6],
                                      x[:, m, j * BLK:(j + 1) * BLK])
                link(last)
                last = V.bn_aggr(mean_var[:, m, :], stats[:, m, :, :].rearrange("p c s -> p (c s)"))
            last.then_inc(ready("ln_stats"), 1)
            dve.wait_ge(ready("ln_std"), n)
            link(V.reciprocal(rstd, rstd))
            link(STT(out=shift, in0=mean_var[:, :, 0], scalar=-1.0, in1=rstd, op0=ALU.mult, op1=ALU.mult))
            for m in range(TT):
                last = TS(x[:, m, :], x[:, m, :], rstd[:, m:m + 1], shift[:, m:m + 1], ALU.mult, ALU.add)
            link(last)
            dve.wait_ge(ready(vec_name), 32)
            for m in range(TT):
                last = TENS(x[:, m, :], x[:, m, :], vec[0][:], ALU.mult)
            link(last)
            for m in range(TT):
                last = TENS(x[:, m, :], x[:, m, :], vec[1][:], ALU.add)
            last.then_inc(ready("x_normed"), 1)

        def hidden(which):
            w1, w2, n, cols, kts = ffn(which)
            r, h = ft_r[which // 2], ft_h[which // 2]
            dst = x if which < 2 else acc_y
            tail = slice(3 * BLK, 4 * BLK)
            if which < 2:
                dve.wait_ge(turn_free[0], c.now("turn", 1, 2))
                dve.wait_ge(turn_free[1], c.now("turn", 0, 2))
                last = TS(x[:, :, tail], x[:, :, tail], ALPHA, None, ALU.mult)
            else:
                last = V.memset(acc_y[:, :, tail], 0.0)
            link(last)

            def take_second(end, b):
                dve.wait_ge(acc_free[(b - 1) % 2], c.freed(b - 1))
                evac(dve, c, end, b, lambda m: h[:, m, :], lambda m, o, s: TENS(o, r[:, m, :], s, ALU.mult))

            def first_out(end, b, j):
                if which < 2:
                    return add_out(end, b, x, j, ALPHA)
                return lambda: evac(dve, c, end, b, lambda m: dst[:, m, j * BLK:(j + 1) * BLK],
                                    lambda m, o, s: V.tensor_copy(o, s))

            def step(ch, before, first_outs):
                start = c.n["block"]
                block_split(unit_lo, dve, c, KT_D, BLK, before)
                block_split(unit_lo, dve, c, KT_D, BLK, (lambda: take_act_lo(dve, c, hT_hi, hT_lo, kts)) if ch is not None else None)
                end1 = c.end
                if ch is None:
                    return lambda: take_second(end1, start + 1)
                out_ = (lambda: take_second(end1, start + 1)) if which < 2 else None
                for j in range(4):
                    block_split(unit_lo, dve, c, kts, BLK, out_)
                    e, b = c.end, c.n["block"] - 1
                    out_ = first_out(e, b, j) if first_outs and j < 3 else add_out(e, b, dst, j)
                return out_
            after = step(None, None, False)
            after = step(1, after if which < 2 else None, True)
            end, b = c.end, c.n["block"] - 1
            with c.loop(dve, n - 2, ffn_body(kts) | {"dve_step": 0}):
                step(2, add_out(end, b, dst, 3), False)
            end, b = c.end, c.n["block"] - 1
            add_out(end, b, dst, 3)()
            take_act_lo(dve, c, hT_hi, hT_lo, kts)
            out_ = None
            for j in range(4):
                block_split(unit_lo, dve, c, kts, BLK, out_)
                out_ = add_out(c.end, c.n["block"] - 1, dst, j)
            out_()

        def turns_of(ang_, whole, turn_):
            link(TS(whole, ang_, 1 / TWO_PI, ROUND, ALU.mult, ALU.add))
            link(TS(whole, whole, ROUND, None, ALU.subtract))
            link(STT(out=turn_, in0=whole, scalar=-TWO_PI_1, in1=ang_, op0=ALU.mult, op1=ALU.add))
            link(STT(out=turn_, in0=whole, scalar=-TWO_PI_2, in1=turn_, op0=ALU.mult, op1=ALU.add))
            link(STT(out=turn_, in0=whole, scalar=-TWO_PI_3, in1=turn_, op0=ALU.mult, op1=ALU.add))

        def sin_and_cos_of(turn_, cos_, spare):
            link(TS(spare, turn_, math.pi / 2, TWO_PI, ALU.is_gt, ALU.mult))
            link(STT(out=cos_, in0=turn_, scalar=math.pi / 2, in1=spare, op0=ALU.add, op1=ALU.subtract))
            TS(cos_, cos_, PI_IN, -PI_IN, ALU.min, ALU.max)
            return TS(turn_, turn_, PI_IN, -PI_IN, ALU.min, ALU.max)

        take_act_lo(dve, c, aT_hi, aT_lo, KT_D)
        project(7, [(7680, 16)])
        for j in range(2):
            turn_take(dve, c, 1, gq[:, 2 * j:2 * j + 2, :])
        for j in range(2):
            turn_take(dve, c, 1, gk[:, 2 * j:2 * j + 2, :])
        turn_take(dve, c, 1, g1T[:])
        dve.wait_ge(ready("gla_soft"), 1)
        link(STT(out=gla_a[:], in0=gla_a[:], scalar=0.0, in1=ge[:], op0=ALU.min, op1=ALU.subtract))
        V.tensor_tensor_scan(gb[:], restart[:], gla_a[:], 0.0, ALU.mult, ALU.add).then_inc(ready("gla_b"), 1)
        dve.wait_ge(ready("gla_b"), 1)
        by_chunk = gb[:].rearrange("p (n l) -> p n l", l=CHUNK)
        TENS(gke[:].rearrange("p (n l) -> p n l", l=CHUNK), by_chunk[:, :, CHUNK - 1:].broadcast_to([P, 16, CHUNK]),
             by_chunk, ALU.subtract).then_inc(ready("gla_end"), 1)
        dve.wait_ge(ready("gla_e"), 4)
        wait_turns(dve, c)
        TENS(gke[:], gke[:], gk[:].rearrange("p h t -> p (h t)"), ALU.mult).then_inc(ready("gla_ke"), 1)
        dve.wait_ge(ready("gla_ke"), 1)
        STT(out=gq[:].rearrange("p h t -> p (h t)"), in0=gq[:].rearrange("p h t -> p (h t)"), scalar=P ** -0.5, in1=ge[:],
            op0=ALU.mult, op1=ALU.mult)
        V.memset(gsT[:], 0.0)
        TENS(gk[:].rearrange("p h t -> p (h t)"), gk[:].rearrange("p h t -> p (h t)"), gla_a[:], ALU.mult).then_inc(ready("gla_qk"), 1)
        dve.wait_ge(ready("gla_qk"), 1)
        for m in range(TT):
            turn_take(dve, c, 1, gkt[:, m, :])
        for h in range(4):
            dve.wait_ge(ready("gla_loc"), h + 1)
            b0 = 2 * (h % 2)
            link(V.tensor_copy(gst[:, h, 0, :], psum[:, b0, 0:256]))
            for n in (1, 2):
                ins = STT(out=gst[:, h, n, :], in0=gst[:, h, n - 1, :], scalar=gdec[:, 4 * h + n:4 * h + n + 1],
                          in1=(psum[:, b0, 256:512] if n == 2 else psum[:, b0 + 1, 0:256]), op0=ALU.mult, op1=ALU.add)
                if n == 1:
                    link(ins)
                else:
                    ins.then_inc(ready("gla_state"), 1)
        for j in range(8):
            dve.wait_ge(ready("gla_s"), j + 1)
            if j >= 2:
                dve.wait_ge(ready("gla_o"), j - 1)
            V.copy_predicated(gsT[:, j % 2, :], chunk_pred[:], psum[:, 6 + j % 2, :P]).then_inc(ready("gla_sm"), 1)
        dve.wait_ge(ready("gla_rms"), 2)
        link(V.reciprocal(rms[:], rms[:]))
        for j in range(8):
            h, m = j // 2, j % 2
            o = g_o[:, m, h * 256:(h + 1) * 256]
            last = STT(out=o, in0=o, scalar=rms[:, j:j + 1], in1=gla_g[:], op0=ALU.mult, op1=ALU.mult)
        link(last)
        link(TENS(proj_e[:, :, G_R:G_R + 1024], proj_e[:, :, G_R:G_R + 1024], g_o[:], ALU.mult))
        TENS(sumsq[:, 0:1], sumsq[:, 1:2], sumsq[:, 2:3], ALU.add).then_inc(ready("gla_done"), 1)
        for s in range(0, 12, 2):
            turn_take(dve, c, 1, dqT[:, s:s + 2, :])
        for s in range(0, 12, 2):
            turn_take(dve, c, 1, dkT[:, s:s + 2, :])
        att_dve(dve, c, dil_items())
        take_act_lo(dve, c, aT_hi, aT_lo, 12)
        residual(12)
        layer_norm(1, "vec0")
        if upto >= 2:
            take_act_lo(dve, c, aT_hi, aT_lo, KT_D)
            hidden(0)
            layer_norm(2, "vec1")
        if upto >= 3:
            take_act_lo(dve, c, aT_hi, aT_lo, KT_D)
            project(3, [(3584, BLK), (4096, 72)])
            dve.wait_ge(ready("odd_small"), 16 * 10)
            link(V.tensor_copy(pos_f[:], pos_i[:]))
            for m in range(TT):
                last = TS(ang[:, 0, 32 * m:32 * m + 32], inv_freq[:], pos_f[:, m:m + 1], None, ALU.mult)
            link(last)
            turns_of(ang[:, 0, :], ang[:, 2, :], ang[:, 0, :])
            sin_and_cos_of(ang[:, 0, :], ang[:, 1, :], ang[:, 2, :]).then_inc(ready("rope_ang"), 1)
            dve.wait_ge(ready("mla_rms"), 1)
            link(V.reciprocal(rms[:, 0:4], rms[:, 0:4]))
            for m in range(TT):
                for j, (col, g) in enumerate(((L_Q, qn_g), (L_KV, kvn_g))):
                    o = proj_o[:, m, col:col + 512]
                    last = STT(out=o, in0=o, scalar=rms[:, 2 * m + j:2 * m + j + 1], in1=g[:], op0=ALU.mult, op1=ALU.mult)
            last.then_inc(ready("mla_normed"), 1)
            take_act_lo(dve, c, aT_hi, aT_lo, 8)
            for _ in range(7):
                block_split(unit_lo, dve, c, 4, BLK)
            dve.wait_ge(ready("rope_cs"), 1)
            wait_blocks(dve, c)

            def rope(pair, m, n, t):
                x1, x2 = pair
                sn, cs = (rope_cs[:, k, m:m + 1, :].broadcast_to([P, n, 32]) for k in range(2))
                t = [rope_t[:, k, :32 * n].rearrange("p (h r) -> p h r", r=32) for k in range(4)]
                TENS(t[0], x1, cs, ALU.mult)
                TENS(t[1], x2, sn, ALU.mult)
                TENS(t[2], x1, sn, ALU.mult)
                link(TENS(t[3], x2, cs, ALU.mult))
                TENS(x1, t[0], t[1], ALU.subtract)
                last = TENS(x2, t[2], t[3], ALU.add)
                link(last)
            for m in range(TT):
                q = qb[:, m, :].rearrange("p (h c) -> p h c", c=192)
                rope((q[:, :, 128:160], q[:, :, 160:192]), m, 8, None)
                k = proj_o[:, m, L_KR:L_KR + 64].rearrange("p (h c) -> p h c", c=64)
                rope((k[:, :, 0:32], k[:, :, 32:64]), m, 1, None)
            V.tensor_copy(smalls[:, 96:98], ident[:, 0:2]).then_inc(ready("roped"), 1)
            for h in range(0, 8, 2):
                turn_take(dve, c, 1, lqT[:, h:h + 2, :])
            for h in range(0, 8, 2):
                turn_take(dve, c, 1, lkT[:, h:h + 2, :])
            for h in range(0, 8, 2):
                turn_take(dve, c, 1, lqr[:, h:h + 2, :])
            turn_take(dve, c, 1, lkr[:])
            att_dve(dve, c, mla_items())
            dve.wait_ge(att_done, 8 + 16)
            V.memset(craw[:, :, 0:3], 0.0)
            V.memset(vaug[:, :, :, 256:257], 1.0)
            V.memset(pT[:], 0.0)
            V.memset(zrow[:], 0.0)
            V.memset(m_prev[:, 0:1], 0.0)
            for h in range(4):
                last = V.tensor_copy(head_row[:, h, :], ident[0:4, h:h + 1].broadcast_to([4, P]))
            for m in range(TT):
                last = V.tensor_copy(vaug[:, m, :, 0:256], proj_o[:, m, M_V:M_V + 1024].rearrange("p (h e) -> p h e", h=4))
            link(last)
            for t in range(0, 8, 2):
                turn_take(dve, c, 1, craw[:, t:t + 2, 3:259])
            for j in (R_LI, R_LF):
                turn_take(dve, c, 1, rows[:, j, :])
            wait_turns(dve, c)
            TS(rows[:, R_LI, :], rows[:, R_LI, :], gate_b[:, 0:1], None, ALU.add)
            TS(rows[:, R_LF, :], rows[:, R_LF, :], gate_b[:, 1:2], None, ALU.add).then_inc(ready("ml_gates"), 1)
            for k in range(4):
                for t in range(8):
                    if k == 0:
                        last = TS(qk[:, t, :], craw[:, t, 0:TOK], conv_w[:, t, 0:1], conv_b[:, t:t + 1], ALU.mult, ALU.add)
                    else:
                        last = STT(out=qk[:, t, :], in0=craw[:, t, k:k + TOK], scalar=conv_w[:, t, k:k + 1],
                                   in1=qk[:, t, :], op0=ALU.mult, op1=ALU.add)
                if k < 3:
                    link(last)
                else:
                    last.then_inc(ready("ml_conv"), 1)
            dve.wait_ge(ready("ml_soft"), 1)
            link(STT(out=rows[:, R_LF, :], in0=rows[:, R_LF, :], scalar=0.0, in1=rows[:, R_B, :], op0=ALU.min, op1=ALU.subtract))
            link(V.tensor_tensor_scan(rows[:, R_B, :], restart_o[:], rows[:, R_LF, :], 0.0, ALU.mult, ALU.add))
            link(TENS(rows[:, R_A, :], rows[:, R_LI, :], rows[:, R_B, :], ALU.subtract))
            for n in range(4):
                ch = slice(n * CHUNK, (n + 1) * CHUNK)
                e = (n + 1) * CHUNK - 1
                link(V.tensor_tensor_scan(rows[:, R_M, ch], zrow[:], rows[:, R_A, ch], m_prev[:, n:n + 1], ALU.add, ALU.max))
                V.tensor_copy(m_last[:, n:n + 1], rows[:, R_M, e:e + 1])
                link(TENS(m_prev[:, n + 1:n + 2], rows[:, R_B, e:e + 1], rows[:, R_M, e:e + 1], ALU.add))
            TS(nm_last, m_last, -1.0, None, ALU.mult)
            TENS(s_old, m_prev[:, 0:4], m_last, ALU.subtract)
            TENS(rows[:, R_E, :], rows[:, R_B, :], rows[:, R_M, :], ALU.add).then_inc(ready("ml_rows"), 1)
            turn_take(dve, c, 1, col6[:].rearrange("p a b -> p (a b)"))
            for m in range(TT):
                turn_take(dve, c, 1, kw[:, m, :])
            wait_turns(dve, c)
            for m in range(TT):
                for h in range(4):
                    last = TS(kw[:, m, h * P:(h + 1) * P], kw[:, m, h * P:(h + 1) * P], col6[:, 2 + m, h:h + 1],
                              P ** -0.5, ALU.mult, ALU.mult)
            last.then_inc(ready("ml_kw"), 1)
            dve.wait_ge(ready("ml_sold"), 1)
            link(V.tensor_copy(s_old_c[:].rearrange("p h n -> p (h n)"), psum[:, 6, 0:16]))
            for h in range(4):
                dve.wait_ge(ready("ml_loc"), h + 1)
                b3 = ((0, 1, 4), (2, 3, 5))[h % 2]
                link(V.tensor_copy(cst[:, h, 0, 0:257], psum[:, b3[0], 0:257]))
                for n in (1, 2):
                    ins = STT(out=cst[:, h, n, 0:257], in0=cst[:, h, n - 1, 0:257], scalar=s_old_c[:, h, n:n + 1],
                              in1=psum[:, b3[n], 0:257], op0=ALU.mult, op1=ALU.add)
                    if n == 1:
                        link(ins)
                    else:
                        ins.then_inc(ready("ml_state"), 1)

            def ml_weights(j):
                h, m = j // 2, j % 2
                dve.wait_ge(ready("ml_e"), j + 1)
                if j >= 1:
                    dve.wait_ge(ready("ml_p"), j)
                if j >= 2:
                    dve.wait_ge(ready("ml_n"), j - 1)
                link(STT(out=sE[:], in0=psum[:, 2 + j % 2, 256:384], scalar=P ** -0.5, in1=eT[:, j % 2, :],
                         op0=ALU.mult, op1=ALU.mult))
                V.copy_predicated(pT[:, j % 2, :], chunk_pred[:], sE[:])
                TENS(qs[:, j % 2, :], qk[:, h, m * P:(m + 1) * P], psum[:, 2 + j % 2, 128:256],
                     ALU.mult).then_inc(ready("ml_p"), 1)

            ml_weights(0)
            for j in range(8):
                h, m = j // 2, j % 2
                if j < 7:
                    ml_weights(j + 1)
                dve.wait_ge(ready("ml_n"), j + 1)
                V.tensor_copy(o257[:, 0:257], psum[:, 6 + j % 2, 0:257]).then_inc(ready("ml_out"), 1)
                dve.wait_ge(ready("ml_out"), j + 1)
                link(STT(out=den[:, 0:1], in0=o257[:, 256:257], scalar=-1.0, in1=o257[:, 256:257], op0=ALU.mult, op1=ALU.max))
                link(TENS(den[:, 1:2], den[:, 0:1], col6[:, 4 + m, h:h + 1], ALU.max))
                link(V.reciprocal(den[:, 0:1], den[:, 1:2]))
                o = m_o[:, m, h * 256:(h + 1) * 256]
                link(TS(o, o257[:, 0:256], den[:, 0:1], None, ALU.mult))
                link(V.bn_stats(ml_st[:], o))
                link(V.bn_aggr(ml_mv[:, j, :], ml_st[:]))
            V.tensor_copy(smalls[:, 98:100], ident[:, 0:2]).then_inc(ready("ml_stats"), 1)
            dve.wait_ge(ready("ml_std"), 2)
            link(V.reciprocal(ml_rs[:], ml_rs[:]))
            link(STT(out=ml_sh[:], in0=ml_mv[:, :, 0], scalar=-1.0, in1=ml_rs[:], op0=ALU.mult, op1=ALU.mult))
            for j in range(8):
                h, m = j // 2, j % 2
                o = m_o[:, m, h * 256:(h + 1) * 256]
                last = TS(o, o, ml_rs[:, j:j + 1], ml_sh[:, j:j + 1], ALU.mult, ALU.add)
            link(last)
            for j in range(8):
                h, m = j // 2, j % 2
                o = m_o[:, m, h * 256:(h + 1) * 256]
                last = TENS(o, o, mln_g[:], ALU.mult)
            link(last)
            co = proj_o[:, :, M_O:M_O + 1024]
            TENS(co, co, m_o[:], ALU.mult).then_inc(ready("ml_done"), 1)
            take_act_lo(dve, c, aT_hi, aT_lo, KT_D)
            residual(KT_D)
            layer_norm(3, "vec2")
        if upto >= 4:
            take_act_lo(dve, c, aT_hi, aT_lo, KT_D)
            hidden(1)
            layer_norm(4, "vec3")
        def gained(dst, src, g, n_rms, which_, scale_ready, signal):
            dve.wait_ge(ready(which_), n_rms)
            link(V.reciprocal(rms[:, 0:2], rms[:, 0:2]))
            dve.wait_ge(ready(scale_ready[0]), scale_ready[1])
            for m in range(TT):
                last = STT(out=dst[:, m, :], in0=src[:, m, :], scalar=rms[:, m:m + 1], in1=g[:], op0=ALU.mult, op1=ALU.mult)
            if signal:
                last.then_inc(ready(signal), 1)
            else:
                link(last)

        if upto >= 5:
            gained(pre, mem_x, gain_a, 1, "pre_rms", ("mem_in", 48), "pre_done")
            take_act_lo(dve, c, aT_hi, aT_lo, KT_D)
            project(0, [(0, BLK)])
            gained(pre, x, gain_b, 2, "pre_rms", ("mix_pre_g", 16), "pre_done")
            take_act_lo(dve, c, aT_hi, aT_lo, KT_D)
            project(3, [(3584, BLK)])
            for h in range(0, 8, 2):
                turn_take(dve, c, 1, nqT[:, h:h + 2, :])
            for h in range(0, 8, 2):
                turn_take(dve, c, 1, nkT[:, h:h + 2, :])
            for h in range(0, 4, 2):
                turn_take(dve, c, 1, mqT[:, h:h + 2, :])
            for h in range(0, 4, 2):
                turn_take(dve, c, 1, mkT[:, h:h + 2, :])
            dve.wait_ge(ready("bias_in"), 16)
            att_dve(dve, c, second_items())
            for q in range(0, 4, 2):
                turn_take(dve, c, 1, uT[:, q:q + 2, :])
            pr = lambda k: par[:, k, :]
            dve.wait_ge(ready("ssm_dt"), 1)
            link(TS(pr(4), pr(0), -1e-4, None, ALU.min))
            TENS(pr(3), pr(4), pr(2), ALU.mult)
            link(TENS(pr(5), pr(1), pr(2), ALU.mult))
            turns_of(pr(5), pr(21), pr(6))
            link(TS(pr(11), pr(6), 1 / TWO_PI, None, ALU.mult))
            sin_and_cos_of(pr(6), pr(7), pr(20)).then_inc(ready("ssm_turns"), 1)
            link(TS(pr(18), pr(11), 65536.0, ROUND, ALU.mult, ALU.add))
            link(TS(pr(18), pr(18), ROUND, 1 / 65536.0, ALU.subtract, ALU.mult))
            link(TENS(pr(19), pr(11), pr(18), ALU.subtract))
            dve.wait_ge(ready("ssm_lam"), 1)
            TENS(pr(12), pr(10), pr(9), ALU.mult)
            TENS(pr(13), pr(10), pr(8), ALU.mult)
            TENS(pr(14), pr(4), pr(4), ALU.mult)
            link(TENS(pr(15), pr(1), pr(1), ALU.mult))
            TS(pr(12), pr(12), 1.0, None, ALU.subtract)
            link(TENS(pr(14), pr(14), pr(15), ALU.add))
            link(V.reciprocal(pr(14), pr(14)))
            TENS(pr(16), pr(12), pr(4), ALU.mult)
            TENS(pr(17), pr(13), pr(4), ALU.mult)
            TENS(pr(15), pr(13), pr(1), ALU.mult)
            link(TENS(pr(20), pr(12), pr(1), ALU.mult))
            TENS(pr(16), pr(16), pr(15), ALU.add)
            link(TENS(pr(17), pr(17), pr(20), ALU.subtract))
            TENS(pr(16), pr(16), pr(14), ALU.mult)
            link(TENS(pr(17), pr(17), pr(14), ALU.mult))
            wr, wi = (par[:, k, :].unsqueeze(2).broadcast_to([P, NDJ, 32]) for k in (16, 17))
            for ri in range(2):
                TENS(bbar[:, ri, :, :], braw[:, ri, :, :], wr, ALU.mult)
                link(TENS(bmul[:], braw[:, 1 - ri, :, :], wi, ALU.mult))
                link(TENS(bbar[:, ri, :, :], bbar[:, ri, :, :], bmul[:], ALU.add if ri else ALU.subtract))
            TS(cmat[:, 1, :, :], cmat[:, 1, :, :], -1.0, None, ALU.mult).then_inc(ready("ssm_bbar"), 1)
            for d in range(2):
                for ri in range(2):
                    turn_take(dve, c, 1, bT[:, d, ri, :, :].rearrange("p q n -> p (q n)"))
            wait_turns(dve, c)
            hi_, lo_ = (par[:, k, :].unsqueeze(2).broadcast_to([P, NDJ, 16]) for k in (18, 19))
            for kind in range(2):
                if kind:
                    dve.wait_ge(ready("ssm_tab"), 1)
                s_, a, b_ = steps16[:, kind, :, :], ph[0][:], ph[1][:]
                w = ph[2][:]
                link(TENS(a, s_, hi_, ALU.mult))
                link(TS(w, a, ROUND, ROUND, ALU.add, ALU.subtract))
                TENS(a, a, w, ALU.subtract)
                link(TENS(b_, s_, lo_, ALU.mult))
                link(TENS(a, a, b_, ALU.add))
                link(TS(w, a, ROUND, ROUND, ALU.add, ALU.subtract))
                link(TENS(a, a, w, ALU.subtract))
                link(TS(w, a, 0.25, None, ALU.is_gt))
                link(STT(out=b_, in0=a, scalar=0.25, in1=w, op0=ALU.add, op1=ALU.subtract))
                link(TS(b_, b_, HALF_IN, -HALF_IN, ALU.min, ALU.max))
                TS(a, a, HALF_IN, -HALF_IN, ALU.min, ALU.max).then_inc(ready("ssm_ph"), 1)
            for i in range(NDJ):
                dj = 16 * (i % 2) + i // 2
                back = i % 2 == 1
                w, ws = wave[:, i % 2, :, :], wave[:, i % 2, ::-1, :]
                dve.wait_ge(ready("ssm_wave"), i + 1)
                dve.wait_ge(ready("ssm_bu"), i + 1)
                if i >= 1:
                    dve.wait_ge(ready("ssm_h"), i)
                bu = psum[:, i % 2, :].rearrange("p (r t) -> p r t", r=2)
                TENS(q1[:], w, bu, ALU.mult)
                TENS(q2[:], ws, bu, ALU.mult).then_inc(ready("ssm_x"), 1)
                dve.wait_ge(ready("ssm_x"), i + 1)
                TENS(xp[:, 0, :], q1[:, 0, :], q1[:, 1, :], ALU.add)
                link(TENS(xp[:, 1, :], q2[:, 1, :], q2[:, 0, :], ALU.subtract))
                rho = par[:, 10, dj:dj + 1].broadcast_to([P, TOK])
                V.tensor_tensor_scan(gs[:, 0, :], rho, xp[:, 0, :], 0.0, ALU.mult, ALU.add)
                link(V.tensor_tensor_scan(gs[:, 1, :], rho, xp[:, 1, :], 0.0, ALU.mult, ALU.add))
                TENS(q1[:], w, gs[:], ALU.mult)
                link(TENS(q2[:], ws, gs[:], ALU.mult))
                if i >= 2:
                    dve.wait_ge(ready("ssm_yp"), i - 1)
                o = [hs[:, i % 2, ri, ::-1] if back else hs[:, i % 2, ri, :] for ri in range(2)]
                TENS(o[0], q1[:, 0, :], q1[:, 1, :], ALU.subtract)
                TENS(o[1], q2[:, 0, :], q2[:, 1, :], ALU.add).then_inc(ready("ssm_h"), 1)
            dve.wait_ge(ready("ssm_small"), 32)
            for m in range(TT):
                last = TENS(y[:, m, 1024:1536], proj_s[:, m, S_U:S_U + 512], ssm_d[:], ALU.mult)
            link(last)
            dve.wait_ge(ready("ssm_yp"), NDJ)
            for m in range(TT):
                last = TENS(y[:, m, 1024:1536], y[:, m, 1024:1536], psum[:, 6 + m, :], ALU.add)
            last.then_inc(ready("ssm_y"), 1)
            take_act_lo(dve, c, aT_hi, aT_lo, 4)
            block_split(unit_lo, dve, c, 4, BLK)
            evac(dve, c, c.end, c.n["block"] - 1, lambda m: t_glu[:, m, :], lambda m, o, s: TENS(o, s, b_glu[:], ALU.add))
            wait_blocks(dve, c)
            V.tensor_copy(smalls[:, 100:102], ident[:, 0:2]).then_inc(ready("glu_z"), 1)
            dve.wait_ge(ready("glu_s"), 1)
            TENS(y[:, :, 1024:1536], y[:, :, 1024:1536], t_glu[:], ALU.mult).then_inc(ready("ssm_out"), 1)
            dve.wait_ge(ready("out_rms"), 1)
            link(V.reciprocal(rms[:, 0:6], rms[:, 0:6]))
            dve.wait_ge(ready("out_norms"), 48)
            for m in range(TT):
                for j, (lo, w) in enumerate(((0, 1024), (1024, 512), (1536, 512))):
                    o = y[:, m, lo:lo + w]
                    last = STT(out=o, in0=o, scalar=rms[:, 3 * m + j:3 * m + j + 1], in1=gain_a[:, lo:lo + w],
                               op0=ALU.mult, op1=ALU.mult)
            last.then_inc(ready("mix_done"), 1)
            take_act_lo(dve, c, aT_hi, aT_lo, KT_D)
            V.tensor_copy(smalls[:, 102:104], ident[:, 0:2]).then_inc(ready("mix_turned"), 1)
            project(0, [(0, BLK)] * 3)
            gained(acc_y, acc_y, gain_b, 1, "post_rms", ("mix_post_g", 16), None)
            TENS(x[:], x[:], acc_y[:], ALU.add).then_inc(ready("x_normed"), 1)
            dve.wait_ge(ready("x_normed"), 5)
        if upto >= 6:
            gained(pre, x, mlp_g[0], 3, "pre_rms", ("mlp_pre_g", 16), "pre_done")
            take_act_lo(dve, c, aT_hi, aT_lo, KT_D)
            hidden(2)
            wait_blocks(dve, c)
            V.tensor_copy(smalls[:, 104:106], ident[:, 0:2]).then_inc(ready("ffn_out"), 1)
            gained(acc_y, acc_y, mlp_g[1], 2, "post_rms", ("mlp_post_g", 16), None)
            TENS(x[:], x[:], acc_y[:], ALU.add).then_inc(ready("x_normed"), 1)
        dve.wait_ge(ready("x_normed"), min(upto, 6))
        TENS(sumsq[:, 0:1], sumsq[:, 1:2], sumsq[:, 2:3], ALU.add).then_inc(ready("x_out"), 1)

    @block.tensor
    def _(pe):
        c = Count()
        MM = nc.tensor.matmul

        def project(pairs, rest, kts=KT_D, k0=0):
            wait_turns(pe, c)
            block_mm(pe, c, kts, BLK, aT_hi, aT_lo, k0)
            if pairs:
                with c.loop(pe, pairs, {"unit": 16, "block": 2}):
                    for _ in range(2):
                        block_mm(pe, c, kts, BLK, aT_hi, aT_lo, k0)
            for _, cols in rest:
                block_mm(pe, c, kts, cols, aT_hi, aT_lo, k0)

        def hidden(which):
            w1, w2, n, cols, kts = ffn(which)
            h = ft_h[which // 2]

            def turn_hidden(second, times):
                if which < 2:
                    pe.wait_ge(acc_free[second % 2], c.freed(second))
                else:
                    pe.wait_ge(ready("hidden_h"), times)
                turn_act(pe, c, lambda m, k: h[:, m, k * P:(k + 1) * P], kts)

            def step(second, times):
                block_mm(pe, c, KT_D, BLK, aT_hi, aT_lo)
                if second is not None:
                    turn_hidden(second, times)
                block_mm(pe, c, KT_D, BLK, aT_hi, aT_lo)
                if second is not None:
                    pe.wait_ge(turn_free[0], c.now("turn", 1, 2))
                    pe.wait_ge(turn_free[1], c.now("turn", 0, 2))
                    for _ in range(4):
                        block_mm(pe, c, kts, BLK, hT_hi, hT_lo)
            wait_turns(pe, c)
            step(None, 0)
            step(c.n["block"] - 1, 2)
            with c.loop(pe, n - 2, ffn_body(kts)) as i:
                step(c.n["block"] - 5, 4 + 2 * i)
            turn_hidden(c.n["block"] - 5, 2 * n)
            wait_turns(pe, c)
            for _ in range(4):
                block_mm(pe, c, kts, BLK, hT_hi, hT_lo)

        def heads(src, col, n, w=P, step=P):
            for h in range(0, n, 2):
                turn(pe, c, [src[:, m, col + (h + j) * step:col + (h + j) * step + w] for j in range(2) for m in range(TT)])

        pe.wait_ge(ready("ident"), 16)
        pe.wait_ge(ready("x_in"), 16 * TT)
        turn_act(pe, c, lambda m, k: x[:, m, k * P:(k + 1) * P], KT_D)
        project(7, [(7680, 16)])
        wait_blocks(pe, c)
        heads(proj_e, G_Q, 4)
        heads(proj_e, G_K, 4)
        turn(pe, c, [proj_e[:, m, G_G:G_G + 16] for m in range(TT)])
        wait_turns(pe, c)
        pe.wait_ge(ready("even_small"), 16 * 6)
        for h in range(4):
            last = MM(psum[:, h // 2, (h % 2) * TOK:(h % 2 + 1) * TOK], wg2[:, h * P:(h + 1) * P], g1T[:], start=True, stop=True)
        last.then_inc(ready("gla_z"), 1)
        pe.wait_ge(ready("gla_ke"), 1)
        for m in range(TT):
            turn(pe, c, [gke[:, h * TOK + m * P:h * TOK + (m + 1) * P] for h in range(4)])
        wait_turns(pe, c)

        def half(n):
            return slice(64 * (n % 2), 64 * (n % 2) + 64)

        for h in range(4):
            if h >= 2:
                pe.wait_ge(ready("gla_state"), h - 1)
            for n in range(3):
                o = psum[:, 2 * (h % 2) + n % 2, (n // 2) * 256:(n // 2) * 256 + 256]
                last = MM(o, gkt[half(n), n // 2, h * P:(h + 1) * P],
                          proj_e[half(n), n // 2, G_V + h * 256:G_V + (h + 1) * 256], start=True, stop=True)
            last.then_inc(ready("gla_loc"), 1)
        pe.wait_ge(ready("gla_qk"), 1)

        def gla_scores(j):
            h, m = j // 2, j % 2
            if j >= 2:
                pe.wait_ge(ready("gla_sm"), j - 1)
            MM(psum[:, 6 + j % 2, :P], gk[:, h, m * P:(m + 1) * P], gq[:, h, m * P:(m + 1) * P],
               start=True, stop=True).then_inc(ready("gla_s"), 1)

        gla_scores(0)
        pe.wait_ge(ready("gla_state"), 4)
        for j in range(8):
            h, m = j // 2, j % 2
            if j < 7:
                gla_scores(j + 1)
            pe.wait_ge(ready("gla_sm"), j + 1)
            if j >= 2:
                pe.wait_ge(ready("gla_o_out"), j - 1)
            v = proj_e[:, m, G_V + h * 256:G_V + (h + 1) * 256]
            last = MM(psum[:, 4 + j % 2, :256], gsT[:, j % 2, :], v, start=True, stop=True, skip_group_check=True)
            for n in (2 * m, 2 * m + 1):
                if n:
                    last = MM(psum[half(n), 4 + j % 2, :256], gq[:, h, n * CHUNK:(n + 1) * CHUNK], gst[:, h, n - 1, :],
                              start=False, stop=True, skip_group_check=True)
            last.then_inc(ready("gla_o"), 1)
        pe.wait_ge(ready("gla_done"), 1)
        heads(proj_e, D_Q, 12)
        heads(proj_e, D_K, 12)
        wait_turns(pe, c)
        att_pe(pe, c, dil_items())
        pe.wait_ge(att_done, 8)

        def mixed_e(m, k):
            if k < 8:
                return proj_e[:, m, G_R + k * P:G_R + (k + 1) * P]
            return dil_o[:, m, (k - 8) * P:(k - 7) * P]
        turn_act(pe, c, mixed_e, 12)
        project(0, [(0, BLK)] * 3, 12)
        if upto >= 2:
            pe.wait_ge(ready("x_normed"), 1)
            turn_act(pe, c, lambda m, k: x[:, m, k * P:(k + 1) * P], KT_D)
            hidden(0)
        if upto >= 3:
            pe.wait_ge(ready("x_normed"), 2)
            turn_act(pe, c, lambda m, k: x[:, m, k * P:(k + 1) * P], KT_D)
            project(3, [(3584, BLK), (4096, 72)])
            pe.wait_ge(ready("mla_normed"), 1)
            turn_act(pe, c, lambda m, k: proj_o[:, m, L_Q + k * P:L_Q + (k + 1) * P], 8)
            project(0, [(0, BLK)] * 2, 4)
            project(0, [(0, BLK)] * 3, 4, 4)
            pe.wait_ge(ready("roped"), 1)
            heads(qb, 0, 8, P, 192)
            heads(kvb, 0, 8, P, 256)
            heads(qb, P, 8, 64, 192)
            turn(pe, c, [proj_o[:, m, L_KR:L_KR + 64] for m in range(TT)])
            wait_turns(pe, c)
            att_pe(pe, c, mla_items())
            heads(proj_o, M_Q, 8)
            turn(pe, c, [proj_o[:, m, M_I:M_I + 4] for m in range(TT)])
            turn(pe, c, [proj_o[:, m, M_F:M_F + 4] for m in range(TT)])
            pe.wait_ge(ready("ml_exps"), 1)
            for h in range(4):
                last = MM(psum[:, 6, 4 * h:4 * h + 4], head_row[:, h, :], s_old, start=True, stop=True)
            last.then_inc(ready("ml_sold"), 1)
            turn(pe, c, [rows[:, j, m * P:(m + 1) * P] for j in (R_A, R_W, R_E) for m in range(TT)])
            pe.wait_ge(ready("ml_qk"), 1)
            for m in range(TT):
                turn(pe, c, [qk[:, 4 + h, m * P:(m + 1) * P] for h in range(4)])
            pe.wait_ge(ready("ml_kw"), 1)
            for h in range(4):
                if h >= 2:
                    pe.wait_ge(ready("ml_state"), h - 1)
                b3 = ((0, 1, 4), (2, 3, 5))[h % 2]
                for n in range(3):
                    last = MM(psum[:, b3[n], 0:257], kw[half(n), n // 2, h * P:(h + 1) * P],
                              vaug[half(n), n // 2, h, 0:257], start=True, stop=True)
                last.then_inc(ready("ml_loc"), 1)

            def ml_scores(j):
                h, m = j // 2, j % 2
                t = slice(m * P, (m + 1) * P)
                if j >= 2:
                    pe.wait_ge(ready("ml_p"), j - 1)
                o = psum[:, 2 + j % 2, :]
                MM(o[:, 0:128], head_row[:, h, :], rows[:, R_M, t], start=True, stop=True)
                MM(o[:, 128:256], head_row[:, h, :], rows[:, R_IS, t], start=True, stop=True)
                MM(o[:, 256:384], qk[:, 4 + h, t], qk[:, h, t], start=True, stop=True).then_inc(ready("ml_s"), 1)

            pe.wait_ge(ready("ml_state"), 4)
            ml_scores(0)
            for j in range(8):
                h, m = j // 2, j % 2
                if j < 7:
                    ml_scores(j + 1)
                pe.wait_ge(ready("ml_p"), j + 1)
                if j >= 2:
                    pe.wait_ge(ready("ml_out"), j - 1)
                last = MM(psum[:, 6 + j % 2, 0:257], pT[:, j % 2, :], vaug[:, m, h, 0:257], start=True, stop=True,
                          skip_group_check=True)
                for n in (2 * m, 2 * m + 1):
                    if n:
                        last = MM(psum[half(n), 6 + j % 2, 0:257], qs[:, j % 2, half(n)], cst[:, h, n - 1, 0:257],
                                  start=False, stop=True, skip_group_check=True)
                last.then_inc(ready("ml_n"), 1)
            pe.wait_ge(ready("ml_done"), 1)

            def mixed_o(m, k):
                if k < 8:
                    return proj_o[:, m, M_O + k * P:M_O + (k + 1) * P]
                return mla_o[:, m, (k - 8) * P:(k - 7) * P]
            turn_act(pe, c, mixed_o, KT_D)
            project(0, [(0, BLK)] * 3)
        if upto >= 4:
            pe.wait_ge(ready("x_normed"), 3)
            turn_act(pe, c, lambda m, k: x[:, m, k * P:(k + 1) * P], KT_D)
            hidden(1)
        if upto >= 5:
            for n, rest in ((1, (0, [(0, BLK)])), (2, (3, [(3584, BLK)]))):
                pe.wait_ge(ready("pre_done"), n)
                turn_act(pe, c, lambda m, k: pre[:, m, k * P:(k + 1) * P], KT_D)
                project(*rest)
            wait_blocks(pe, c)
            heads(proj_s, S_Q, 8)
            heads(proj_s, S_K, 8)
            heads(proj_s, S_MQ, 4)
            heads(kvm, 0, 4)
            wait_turns(pe, c)
            att_pe(pe, c, second_items())
            pe.wait_ge(att_done, c.n["att"])
            heads(proj_s, S_U, 4)
            pe.wait_ge(ready("ssm_bbar"), 1)
            for d in range(2):
                for ri in range(2):
                    turn(pe, c, [bbar[:, ri, 16 * d + 4 * q:16 * d + 4 * q + 4, :].rearrange("p j n -> p (j n)") for q in range(4)])
            wait_turns(pe, c)

            def drive(i):
                d, j = i % 2, i // 2
                q, r = j // 4, slice(32 * (j % 4), 32 * (j % 4) + 32)
                if i >= 2:
                    pe.wait_ge(ready("ssm_x"), i - 1)
                for ri in range(2):
                    u = uT[r, q, ::-1] if d else uT[r, q, :]
                    last = MM(psum[:, i % 2, ri * TOK:(ri + 1) * TOK], bT[r, d, ri, q, :], u, start=True, stop=True)
                last.then_inc(ready("ssm_bu"), 1)

            drive(0)
            for i in range(NDJ):
                d, j = i % 2, i // 2
                if i + 1 < NDJ:
                    drive(i + 1)
                pe.wait_ge(ready("ssm_h"), i + 1)
                for m in range(TT):
                    for ri in range(2):
                        last = MM(psum[:, 6 + m, 32 * j:32 * j + 32], hs[:, i % 2, ri, m * P:(m + 1) * P],
                                  cmat[:, ri, 16 * d + j, :], start=(d == 0 and ri == 0), stop=(d == 1 and ri == 1))
                last.then_inc(ready("ssm_yp"), 1)
            pe.wait_ge(ready("ssm_gelu"), 1)
            turn_act(pe, c, lambda m, k: y[:, m, 1024 + k * P:1024 + (k + 1) * P], 4)
            project(0, [], 4)
            pe.wait_ge(ready("mix_done"), 1)
            turn_act(pe, c, lambda m, k: y[:, m, k * P:(k + 1) * P], KT_D)
            project(0, [(0, BLK)] * 3)
        if upto >= 6:
            pe.wait_ge(ready("pre_done"), 3)
            turn_act(pe, c, lambda m, k: pre[:, m, k * P:(k + 1) * P], KT_D)
            hidden(2)

    ctx.close()


def program(nc, shapes, dtypes, upto=99):
    aps = {n[3:]: nc.dram_tensor(n, shapes[n], dtypes[n], kind="ExternalInput").ap() for n in shapes}
    out = nc.dram_tensor("out_x", (1, TOK, D), F32, kind="ExternalOutput").ap()
    build(nc, aps, out, upto)


def tables():
    i = np.arange(P)[:, None]
    f = np.float32
    ident = np.eye(P, dtype=f)
    j = np.arange(P)[None, :]
    chunk_pred = ((i <= j) & (i // CHUNK == j // CHUNK)).astype(np.int32)
    restart = np.tile((np.arange(1024) % CHUNK != 0).astype(f), (P, 1))
    parts = []
    for m in range(TT):
        q = np.arange(P)[:, None] + m * P
        k = np.arange(P * (m + 1))[None, :]
        for window, dilation in ((128, 1), (512, 4), (2048, 16)):
            ok = (k <= q) & ((q - k) % dilation == 0) & (q - k <= window)
            parts.append(np.where(ok, 0.0, NEG).astype(f))
    q = np.arange(P)[:, None] + P
    mla = np.where(np.arange(TOK)[None, :] <= q, 0.0, NEG).astype(f)
    inv = (10000.0 ** (-np.arange(0, 64, 2) / 64)).astype(f)
    steps = np.tile(np.stack([np.arange(16), 16 * np.arange(16)])[:, None, :], (1, 32, 1)).astype(f)
    return {
        "c_ident": ident, "c_chunk_pred": chunk_pred, "c_restart": restart,
        "c_dil_mask": np.concatenate(parts, 1), "c_mla_mask": mla,
        "c_inv_freq": np.tile(inv, (P, 1)), "c_steps": np.tile(steps[None], (P, 1, 1, 1)),
    }


def laid_out(a):
    f = np.float32
    out = {
        "l_gla_bg": a["even_gla_bg"][0].reshape(4, P).T,
        "l_conv_w": a["odd_conv_w"][0].reshape(4, 8, P).transpose(2, 1, 0),
        "l_conv_b": a["odd_conv_b"][0].reshape(8, P).T,
        "l_gate_b": np.stack([a["odd_mlstm_bi"][0], a["odd_mlstm_bf"][0]], 1),
        "l_pos": a["positions"][0].reshape(TT, P).T,
        "l_ssm_d": a["ssm_d_2"].reshape(1, 512),
    }
    t = np.arange(TOK)
    r, col = t // 64, t % 64
    start = np.clip(col - 8, 0, 48)
    inside = (col[None, :] >= start[:, None]) & (col[None, :] < start[:, None] + 16)
    dr = r[None, :] - r[:, None] + 7
    dc = np.clip(col[None, :] - col[:, None] + 15, 0, 30)
    bias = np.where(inside[None], a["na_rpb_2"][0][:, dr, dc], f(NEG))
    out["l_bias"] = bias.reshape(8, TT, P, TOK).transpose(2, 0, 1, 3).reshape(P, 16, TOK)
    def states(v):
        return v.reshape(2, 16, P).transpose(2, 0, 1).reshape(P, 32)
    dt = np.broadcast_to(a["ssm_log_dt_2"][0][:, :, None], (2, 32, 64))
    out["l_lam"] = np.stack([states(a["ssm_lam_re_2"][0]), states(a["ssm_lam_im_2"][0]), states(dt)], 1)
    b = np.zeros((2, P, 32, 32), f)
    cm = np.zeros((2, P, 32, 32), f)
    for ri, part in enumerate(("re", "im")):
        vb = a[f"ssm_b_{part}_2"][0].reshape(2, 16, 2, 64, 16)
        vc = a[f"ssm_c_{part}_2"][0].reshape(2, 16, 2, 16, 64)
        for g in range(2):
            b[ri, 64 * g:64 * g + 64, :, 16 * g:16 * g + 16] = vb[:, :, g].transpose(2, 0, 1, 3).reshape(64, 32, 16)
            cm[ri, 64 * g:64 * g + 64, :, 16 * g:16 * g + 16] = vc[:, :, g].transpose(3, 0, 1, 2).reshape(64, 32, 16)
    out["l_b"] = b.transpose(1, 0, 2, 3)
    out["l_c"] = cm.transpose(1, 0, 2, 3)
    return out


_DIRECT = ["x", "even_w_in", "even_gla_wg2", "even_gla_norm_g", "even_w_o", "odd_w_in", "odd_mlstm_norm_g",
           "odd_mla_qnorm_g", "odd_mla_kvnorm_g", "odd_mla_wuq", "odd_mla_wukv", "odd_w_o", "ln1_g", "ln1_b",
           "ffn_wgu", "ffn_wd", "ln2_g", "ln2_b", "mem_2", "norm_mix_pre_2", "w_in_2", "w_glu_2", "b_glu_2",
           "mem_norm_2", "w_mem_kv_2", "out_norm_na_2", "out_norm_ssm_2", "out_norm_mem_2", "w_out_2",
           "norm_mix_post_2", "norm_mlp_pre_2", "w_ff1_2", "w_ff2_2", "norm_mlp_post_2"]


def operands(inputs):
    given = {n: inputs[n] for n in _DIRECT} | laid_out(inputs) | tables()
    return {f"in_{n}": np.ascontiguousarray(a) for n, a in given.items()}


def kernel(**inputs):
    import concourse.bacc as _bacc
    from concourse.bass_utils import run_bass_kernel_spmd as _run

    arrays = operands({n: np.asarray(a) for n, a in inputs.items()})
    nc = _bacc.Bacc("TRN2", target_bir_lowering=False, num_devices=1)
    program(nc, {n: a.shape for n, a in arrays.items()}, {n: mybir.dt.from_np(a.dtype) for n, a in arrays.items()})
    r = _run(nc, [arrays], core_ids=[0])
    return r.results[0]["out_x"]
```

```python
from collections import Counter
from contextlib import ExitStack, contextmanager
import math

import numpy as np
import concourse.bass as bass
from concourse import mybir

F32 = mybir.dt.float32
F32R = mybir.dt.float32r
I32 = mybir.dt.int32
ACT = mybir.ActivationFunctionType
ALU = mybir.AluOpType
AX_X = mybir.AxisListType.X

P = 128
TOK = 256
TT = TOK // P
D = 2048
KT_D = D // P
BLK = 512
UNIT = 1024
RAW_SLOTS = 8
SPLIT_SLOTS = 4
CHUNK = 64
NEG = -1e30
TWO_PI = 2 * math.pi
ROUND = 12582912.0
TWO_PI_1 = 6.28125
TWO_PI_2 = round((TWO_PI - TWO_PI_1) * 2**20) / 2**20
TWO_PI_3 = TWO_PI - TWO_PI_1 - TWO_PI_2
PI_IN = 3.1415925
HALF_IN = 0.49999994
ALPHA = 4.0 ** 0.25

EVEN_N = 7696
ODD_N = 4168
SEC_N = 4096
HID = 5632
FF = 8192


class Count:

    def __init__(self):
        self.n = Counter()
        self.i = None
        self.per = {}
        self.end = 0

    def until(self, unit):
        return self.now("unit", unit - self.n["unit"])

    def freed(self, block):
        v = block // 2 + 1
        return v if self.i is None else v + self.i * (self.per["block"] // 2)

    def now(self, name, add=0, each=1, times=1):
        v = times * ((self.n[name] + add) // each)
        if self.i is None or not self.per.get(name):
            return v
        return v + self.i * (times * self.per[name] // each)

    @contextmanager
    def loop(self, eng, trips, per):
        start = Counter(self.n)
        with eng.Fori(0, trips) as i:
            self.i, self.per = i, per
            yield i
            self.i, self.per = None, {}
        for name in list(self.n):
            done = self.n[name] - start[name]
            assert done == per.get(name, 0), (name, done, per)
            self.n[name] += done * (trips - 1)
        self.end += per["unit"] * (trips - 1)


def units_of(kts, cols):
    most = max(1, UNIT // cols)
    n = -(-kts // most)
    size = -(-kts // n)
    return [(k, min(size, kts - k)) for k in range(0, kts, size)]


def build(nc, A, out, upto=99):
    ctx = ExitStack()
    base = -(-nc.sbuf_base // 64) * 64
    ctx.enter_context(nc.sbuf_tensor("all_sbuf", [P, (nc.sbuf_usable_end - base) // 4 - 16], F32))

    def at(name, word, shape, dt=F32):
        assert base + 4 * (word + int(np.prod(shape[1:]))) <= nc.sbuf_usable_end, name
        return nc.alloc_sbuf_tensor_at(name, shape, dt, offset=base + 4 * word)

    def sem(name):
        return ctx.enter_context(nc.semaphore(name))

    raw = at("weights_raw", 0, [P, RAW_SLOTS, UNIT])
    w_hi = at("weights_hi", 8192, [P, SPLIT_SLOTS, UNIT], F32R)
    w_lo = at("weights_lo", 12288, [P, SPLIT_SLOTS, UNIT], F32R)
    x = at("x", 16384, [P, TT, D])
    SCR = 20480
    aT_hi = at("act_hi", SCR, [P, KT_D, TOK], F32R)
    aT_lo = at("act_lo", SCR + 4096, [P, KT_D, TOK], F32R)
    hT_hi = at("hid_hi", SCR + 8192, [P, 8, TOK], F32R)
    hT_lo = at("hid_lo", SCR + 10240, [P, 8, TOK], F32R)
    CON = SCR + 12288
    ident = at("ident", CON, [P, P])
    smalls = at("smalls", CON + 128, [P, 128])
    BIG = CON + 256
    BIG_END = 53200
    n_view = [0]

    def scr(off, shape, dt=F32):
        n_view[0] += 1
        assert off + int(np.prod(shape[1:])) <= 12288
        return at(f"scratch_{n_view[0]}", SCR + off, shape, dt)

    def big(off, shape, dt=F32):
        n_view[0] += 1
        assert BIG + off + int(np.prod(shape[1:])) <= BIG_END
        return at(f"big_{n_view[0]}", BIG + off, shape, dt)

    psum = ctx.enter_context(nc.psum_tensor("psum", [P, 8, BLK], F32))

    def bank(i):
        return psum[:, i, :]

    landed = [sem(f"unit_landed{i}") for i in range(RAW_SLOTS)]
    hi_ready = sem("hi_ready")
    lo_ready = sem("lo_ready")
    w_used = sem("w_used")
    acc_free = [sem("acc_free0"), sem("acc_free1")]
    turned = sem("turned")
    turn_hi = sem("turn_hi")
    turn_free = [sem("turn_free0"), sem("turn_free1")]
    dve_step = sem("dve_step")
    act_step = sem("act_step")
    pool_step = sem("pool_step")
    att_scored = sem("att_scored")
    att_scaled = sem("att_scaled")
    att_maxed = sem("att_maxed")
    att_exped = sem("att_exped")
    att_turned = sem("att_turned")
    att_pt = sem("att_pt")
    att_pved = sem("att_pved")
    att_done = sem("att_done")
    named = {}

    def ready(name):
        if name not in named:
            named[name] = sem(name)
        return named[name]

    def unit_load(sp, c, src, cols):
        u = c.n["unit"]
        slot = u % RAW_SLOTS
        nk = src.shape[1]
        if u >= RAW_SLOTS:
            sp.wait_ge(lo_ready, c.now("unit", 1 - RAW_SLOTS))
        sp.dma_start(raw[:, slot, :nk * cols].rearrange("p (k n) -> p k n", n=cols), src).then_inc(landed[slot], 16)
        c.n["unit"] += 1

    def block_load(sp, c, w, row0, kts, col0, cols):
        for k, nk in units_of(kts, cols):
            src = w[bass.ds(row0 + k * P, nk * P), bass.ds(col0, cols)]
            unit_load(sp, c, src.rearrange("(k p) n -> p k n", p=P), cols)

    def unit_hi(act, c, size):
        u = c.n["unit"]
        act.wait_ge(landed[u % RAW_SLOTS], c.now("unit", RAW_SLOTS, RAW_SLOTS, 16))
        if u >= SPLIT_SLOTS:
            act.wait_ge(w_used, c.now("unit", 1 - SPLIT_SLOTS))
        nc.scalar.copy(w_hi[:, u % SPLIT_SLOTS, :size], raw[:, u % RAW_SLOTS, :size]).then_inc(hi_ready, 1)
        c.n["unit"] += 1

    def unit_lo(dve, c, size):
        u = c.n["unit"]
        dve.wait_ge(hi_ready, c.now("unit", 1))
        nc.vector.tensor_tensor(w_lo[:, u % SPLIT_SLOTS, :size], raw[:, u % RAW_SLOTS, :size],
                                w_hi[:, u % SPLIT_SLOTS, :size].bitcast(F32), ALU.subtract).then_inc(lo_ready, 1)
        c.n["unit"] += 1

    def block_split(one, eng, c, kts, cols, between=None):
        us = units_of(kts, cols)
        for j, (_, nk) in enumerate(us):
            if between is not None and j == (len(us) + 1) // 2:
                between()
                between = None
            one(eng, c, nk * cols)
        c.end = c.n["unit"]
        c.n["block"] += 1
        if between is not None:
            between()

    def block_mm(pe, c, kts, cols, hi, lo, k0=0):
        b = c.n["block"]
        pair = b % 2
        if b >= 2:
            pe.wait_ge(acc_free[pair], c.freed(b - 2))
        for k, nk in units_of(kts, cols):
            s = c.n["unit"] % SPLIT_SLOTS
            pe.wait_ge(lo_ready, c.now("unit", 1))
            for j in range(nk):
                wh = w_hi[:, s, j * cols:(j + 1) * cols]
                wl = w_lo[:, s, j * cols:(j + 1) * cols]
                for m in range(TT):
                    ah = hi[:, k0 + k + j, m * P:(m + 1) * P]
                    al = lo[:, k0 + k + j, m * P:(m + 1) * P]
                    o = psum[:, 2 * pair + m, :cols]
                    nc.tensor.matmul(o, ah, wh, start=(k + j == 0), stop=False)
                    nc.tensor.matmul(o, ah, wl, start=False, stop=False)
                    last = nc.tensor.matmul(o, al, wh, start=False, stop=(k + j == kts - 1))
            last.then_inc(w_used, 1)
            c.n["unit"] += 1
        c.n["block"] += 1

    def narrow_mm(pe, c, cols):
        pair = c.n["block"] % 2
        pe.wait_ge(acc_free[pair], c.freed(c.n["block"] - 2))
        o = psum[:cols, 2 * pair, :TOK]
        for k, nk in units_of(KT_D, cols):
            s = c.n["unit"] % SPLIT_SLOTS
            pe.wait_ge(lo_ready, c.now("unit", 1))
            for j in range(nk):
                wh, wl = (w[:, s, j * cols:(j + 1) * cols] for w in (w_hi, w_lo))
                ah, al = aT_hi[:, k + j, :], aT_lo[:, k + j, :]
                nc.tensor.matmul(o, wh, ah, start=(k + j == 0), stop=False)
                nc.tensor.matmul(o, wl, ah, start=False, stop=False)
                last = nc.tensor.matmul(o, wh, al, start=False, stop=(k + j == KT_D - 1))
            last.then_inc(w_used, 1)
            c.n["unit"] += 1
        c.n["block"] += 1

    def narrow_out(act, c, dst):
        end, pair, cols = c.end, (c.n["block"] - 1) % 2, dst.shape[0]

        def go():
            act.wait_ge(w_used, end)
            nc.scalar.copy(dst, psum[:cols, 2 * pair, :TOK]).then_inc(acc_free[pair], 1)
        return go

    def evac(eng, c, end, block, dst, do):
        eng.wait_ge(w_used, c.until(end))
        pair = block % 2
        for m in range(TT):
            last = do(m, dst(m), psum[:, 2 * pair + m, :])
        last.then_inc(acc_free[pair], 1)

    def wait_blocks(eng, c):
        b = c.n["block"]
        eng.wait_ge(acc_free[0], (b + 1) // 2)
        eng.wait_ge(acc_free[1], b // 2)

    def turn(pe, c, srcs):
        t = c.n["turn"]
        if t >= 2:
            pe.wait_ge(turn_free[t % 2], c.now("turn", 0, 2))
        at_col = 0
        for src in srcs:
            p, w = src.shape
            last = nc.tensor.transpose(psum[:w, 4 + t % 2, at_col:at_col + p], src, ident[:p, :p])
            at_col += p
        last.then_inc(turned, 1)
        c.n["turn"] += 1

    def turn_take_hi(act, c, dst):
        act.wait_ge(turned, c.now("turn", 1))
        t = c.n["turn"]
        nc.scalar.copy(dst, psum[:, 4 + t % 2, :]).then_inc(turn_hi, 1)
        c.n["turn"] += 1
        c.n["split_turn"] += 1

    def turn_take_lo(dve, c, dst, hi):
        dve.wait_ge(turn_hi, c.now("split_turn", 1))
        t = c.n["turn"]
        nc.vector.tensor_tensor(dst, psum[:, 4 + t % 2, :], hi.bitcast(F32), ALU.subtract).then_inc(turn_free[t % 2], 1)
        c.n["turn"] += 1
        c.n["split_turn"] += 1

    def turn_take(eng, c, mine, dst, scale=None):
        t = c.n["turn"]
        if t % 2 == mine:
            w, n = dst.shape[0], int(np.prod(dst.shape[1:]))
            eng.wait_ge(turned, t + 1)
            src = psum[:w, 4 + t % 2, :n]
            if mine == 0:
                ins = nc.scalar.activation(dst, src, ACT.Copy, scale=scale or 1.0)
            elif scale is None:
                ins = nc.vector.tensor_copy(dst, src)
            else:
                ins = nc.vector.tensor_scalar(dst, src, scale, None, ALU.mult)
            ins.then_inc(turn_free[t % 2], 1)
        c.n["turn"] += 1

    def wait_turns(eng, c):
        t = c.n["turn"]
        eng.wait_ge(turn_free[0], c.now("turn", 1, 2))
        if t >= 2 or t == 2:
            eng.wait_ge(turn_free[1], c.now("turn", 0, 2))

    def turn_act(pe, c, src, kts):
        for k in range(0, kts, 2):
            turn(pe, c, [src(m, k + j) for j in range(2) for m in range(TT)])

    def take_act_hi(act, c, hi, kts, k0=0):
        for k in range(0, kts, 2):
            turn_take_hi(act, c, hi[:, k0 + k:k0 + k + 2, :].rearrange("p k t -> p (k t)"))

    def take_act_lo(dve, c, hi, lo, kts, k0=0):
        for k in range(0, kts, 2):
            turn_take_lo(dve, c, lo[:, k0 + k:k0 + k + 2, :].rearrange("p k t -> p (k t)"),
                         hi[:, k0 + k:k0 + k + 2, :].rearrange("p k t -> p (k t)"))

    LEAD = KT_D // 2
    LEAD_EARLY = 2

    def lead_early(one, eng, c):
        for _ in range(LEAD_EARLY):
            one(eng, c, UNIT)

    def lead_split(one, eng, c, take, prepare=None):
        if prepare is not None:
            prepare(0)
            prepare(1)
        for u in range(LEAD):
            if prepare is not None and u in (2, 4):
                prepare(u // 2 + 1)
            k = slice(2 * u, 2 * u + 2)
            take(k)
            if u >= LEAD_EARLY:
                one(eng, c, UNIT)
        c.end = c.n["unit"]
        c.n["block"] += 1

    def lead_hi(act, c):
        lead_split(unit_hi, act, c, lambda k: turn_take_hi(act, c, aT_hi[:, k, :].rearrange("p k t -> p (k t)")))

    def lead_lo(dve, c, prepare):
        lead_split(unit_lo, dve, c, lambda k: turn_take_lo(dve, c, aT_lo[:, k, :].rearrange("p k t -> p (k t)"),
                                                           aT_hi[:, k, :].rearrange("p k t -> p (k t)")), prepare)

    def lead_mm(pe, c, src, stands):
        b, t0 = c.n["block"], c.n["turn"]

        def batch(u):
            if u % 2 == 0:
                stands(u // 2)
            turn(pe, c, [src(m, 2 * u + j) for j in range(2) for m in range(TT)])

        batch(0)
        batch(1)
        pair = b % 2
        if b >= 2:
            pe.wait_ge(acc_free[pair], c.freed(b - 2))
        for u in range(LEAD):
            if u + 2 < LEAD:
                batch(u + 2)
            pe.wait_ge(turn_free[(t0 + u) % 2], (t0 + u) // 2 + 1)
            pe.wait_ge(lo_ready, c.now("unit", 1))
            s = c.n["unit"] % SPLIT_SLOTS
            for j in range(2):
                wh, wl = (w[:, s, j * BLK:(j + 1) * BLK] for w in (w_hi, w_lo))
                for m in range(TT):
                    ah, al = (a[:, 2 * u + j, m * P:(m + 1) * P] for a in (aT_hi, aT_lo))
                    o = psum[:, 2 * pair + m, :]
                    nc.tensor.matmul(o, ah, wh, start=(u + j == 0), stop=False)
                    nc.tensor.matmul(o, ah, wl, start=False, stop=False)
                    last = nc.tensor.matmul(o, al, wh, start=False, stop=(2 * u + j == KT_D - 1))
            last.then_inc(w_used, 1)
            c.n["unit"] += 1
        c.n["block"] += 1

    def wait_normed(eng, n):
        eng.wait_ge(ready("x_quarter"), 4 * n)

    def dve_link(c, ins):
        c.n["dve_step"] += 1
        ins.then_inc(dve_step, 1)
        nc.vector.wait_ge(dve_step, c.now("dve_step"))

    def act_link(c, ins):
        c.n["act_step"] += 1
        ins.then_inc(act_step, 1)
        nc.scalar.wait_ge(act_step, c.now("act_step"))

    def pool_link(c, ins):
        c.n["pool_step"] += 1
        ins.then_inc(pool_step, 1)
        nc.gpsimd.wait_ge(pool_step, c.now("pool_step"))

    def att_buf(c0, slots=4, width=256):
        sc = scr(c0, [P, slots, width])
        pb = scr(c0 + slots * width, [P, slots, width])
        pt = scr(c0 + 2 * slots * width, [P, 2, width])
        stat = scr(c0 + (2 * slots + 2) * width, [P, 3, 8])
        return sc, pb, pt, stat

    def scores_of(it, n):
        if it["wide"]:
            return psum[:, 2 * (n % 2):2 * (n % 2) + 2, :].rearrange("p b n -> p (b n)")
        return psum[:, n % it["slots"], :]

    def turned_of(it, n):
        if it["wide"]:
            return psum[:, 4:6, :].rearrange("p b n -> p (b n)")
        return psum[:, 4 if it["lean"] else 4 + n % 2, :]

    def product_of(it, n):
        return psum[:, 5 if it["lean"] else 6 + n % 2, :P]

    def att_order(items, ahead, first, then, last, also=None, also_last=True):
        k = len(items)
        for j in range(min(ahead, k)):
            first(j)
        for j in range(k + 1):
            if j + ahead < k:
                first(j + ahead)
            if then is not None and j < k:
                then(j)
            if also is not None and not also_last:
                also(j)
            if j >= 1:
                last(j - 1)
            if also is not None and also_last:
                also(j)

    def att_pe(pe, c, items, also=None):
        n0, slots = c.n["att"], items[0]["slots"]

        def scores(j):
            it, n = items[j], n0 + j
            if j >= slots:
                pe.wait_ge(att_scaled, n - slots + 1)
            flat = scores_of(it, j)
            for col, pairs in it["parts"]:
                for i, (q, k) in enumerate(pairs):
                    last = nc.tensor.matmul(flat[:, col:col + k.shape[1]], q, k, start=(i == 0), stop=(i == len(pairs) - 1))
            last.then_inc(att_scored, 1)

        def turn_probs(j):
            it, n = items[j], n0 + j
            pe.wait_ge(att_exped, n + 1)
            free = n if it["wide"] or it["lean"] else n - 1
            if free >= 1:
                pe.wait_ge(att_pt, free)
            flat = turned_of(it, n)
            for col in range(0, it["cols"], P):
                last = nc.tensor.transpose(flat[:, col:col + P], it["pb"][:, j % slots, col:col + P], ident[:])
            last.then_inc(att_turned, 1)

        def product(j):
            it, n = items[j], n0 + j
            pe.wait_ge(att_pt, n + 1)
            if it["lean"]:
                pe.wait_ge(att_done, n)
            elif n >= 2:
                pe.wait_ge(att_done, n - 1)
            nt = it["cols"] // P
            for i in range(nt):
                last = nc.tensor.matmul(product_of(it, n), it["pt"][:, n % 2, i * P:(i + 1) * P], it["v"][i],
                                        start=(i == 0), stop=(i == nt - 1))
            last.then_inc(att_pved, 1)

        att_order(items, slots - 1, scores, turn_probs, product, also)
        c.n["att"] += len(items)

    def att_act(act, c, items):
        n0, slots = c.n["att"], items[0]["slots"]

        def exp(j):
            it, n = items[j], n0 + j
            act.wait_ge(att_maxed, n + 1)
            if j >= slots:
                act.wait_ge(att_turned, n - slots + 1)
            s = slice(n % 8, n % 8 + 1)
            nc.scalar.activation(it["pb"][:, j % slots, :it["cols"]], it["sc"][:, j % slots, :it["cols"]], ACT.Exp,
                                 bias=it["stat"][:, 0, s], accum_out=it["stat"][:, 1, s]).then_inc(att_exped, 1)

        def take(j):
            it, n = items[j], n0 + j
            act.wait_ge(att_turned, n + 1)
            if n >= 2:
                act.wait_ge(att_pved, n - 1)
            nc.scalar.copy(it["pt"][:, n % 2, :it["cols"]], turned_of(it, n)[:, :it["cols"]]).then_inc(att_pt, 1)

        att_order(items, slots - 1, exp, None, take)
        c.n["att"] += len(items)

    def att_dve(dve, c, items, also=None):
        n0, slots = c.n["att"], items[0]["slots"]

        def scale(j):
            it, n = items[j], n0 + j
            dve.wait_ge(att_scored, n + 1)
            if j >= slots:
                dve.wait_ge(att_exped, n - slots + 1)
            flat = scores_of(it, j)[:, :it["cols"]]
            sc = it["sc"][:, j % slots, :it["cols"]]
            top = it["stat"][:, 2, n % 8:n % 8 + 1]
            if it["mask"] is None:
                nc.vector.tensor_scalar(sc, flat, it["scale"], None, ALU.mult).then_inc(att_scaled, 1)
                dve.wait_ge(att_scaled, n + 1)
                dve_link(c, nc.vector.reduce_max(top, sc, AX_X))
            else:
                nc.vector.tensor_tensor_reduce(sc, flat, it["mask"], it["scale"], -3e38, ALU.add, ALU.max,
                                               top).then_inc(att_scaled, 1)
                dve.wait_ge(att_scaled, n + 1)
            nc.vector.tensor_scalar(it["stat"][:, 0, n % 8:n % 8 + 1], top, -1.0, None, ALU.mult).then_inc(att_maxed, 1)

        def finish(j):
            it, n = items[j], n0 + j
            dve.wait_ge(att_pved, n + 1)
            inv = it["stat"][:, 2, n % 8:n % 8 + 1]
            dve_link(c, nc.vector.reciprocal(inv, it["stat"][:, 1, n % 8:n % 8 + 1]))
            nc.vector.tensor_scalar(it["out"], product_of(it, n), inv, None, ALU.mult).then_inc(att_done, 1)

        att_order(items, slots - 1, scale, None, finish, also, False)
        c.n["att"] += len(items)

    proj_e = big(0, [P, TT, EVEN_N])
    dil_o = big(15392, [P, TT, 512])
    wg2 = big(16416, [16, 512])
    dil_mask = big(16928, [P, 1152])
    gla_bg = big(18080, [P, 4])
    gla_g = big(18088, [P, 256])
    chunk_pred = big(20048, [P, P], I32)
    restart = big(19024, [P, 1024])
    G_Q, G_K, G_V, G_G, G_R, D_Q, D_K, D_V = 0, 512, 1024, 2048, 2064, 3088, 4624, 6160

    ln_vec = [[big(10784, [P, D]), big(12832, [P, D])]] * 3 + [[big(10240, [P, D]), big(12288, [P, D])]]
    eps = smalls[:, 0:1]
    one = smalls[:, 1:2]
    eps6 = smalls[:, 3:4]
    mean_var = smalls[:, 4:8].rearrange("p (m two) -> p m two", two=2)
    rstd = smalls[:, 8:10]
    sumsq = smalls[:, 16:24]
    mem_sq = smalls[:, 116:118]
    mem_rs = smalls[:, 118:120]
    rms = smalls[:, 24:32]
    stats = smalls[:, 32:80].rearrange("p (m c s) -> p m c s", m=2, s=6)

    gq = scr(0, [P, 4, TOK])
    gk = scr(1024, [P, 4, TOK])
    gkt = scr(2048, [P, TT, 512])
    gst = scr(3072, [P, 4, 3, 256])
    gsT = scr(6144, [P, 2, P])
    gsq = scr(6400, [P, 256])
    gb = scr(8192, [P, 1024])
    gke = scr(9216, [P, 1024])
    ge = scr(10240, [P, 1024])
    gla_a = scr(11264, [P, 1024])
    g1T = big(15392, [16, TOK])
    gdec = big(15648, [P, 16])
    g_o = scr(8192, [P, TT, 1024])
    GATE_AT = G_G // BLK
    LAST5 = [G_R + BLK * j for j in range(6, 11)]
    dqT = scr(0, [P, 12, TOK])
    dkT = scr(3072, [P, 12, TOK])
    d_sc, d_pb, d_pt, d_stat = att_buf(6144, 2, 768)

    def att(sc, pb, pt, stat, parts, v, mask, scale, out, cols, lean=False):
        return {"sc": sc, "pb": pb, "pt": pt, "stat": stat, "parts": parts, "v": v, "mask": mask, "scale": scale,
                "out": out, "cols": cols, "slots": sc.shape[1], "wide": sc.shape[2] > 256, "lean": lean}

    def dil_items():
        items = []
        for h in range(4):
            for m in range(TT):
                nk = P * (m + 1)
                parts, vs = [], []
                for g in range(3):
                    s = 4 * g + h
                    parts.append((g * nk, [(dqT[:, s, m * P:(m + 1) * P], dkT[:, s, :nk])]))
                    vs += [proj_e[:, j, D_V + s * P:D_V + (s + 1) * P] for j in range(m + 1)]
                mask = dil_mask[:, 0:384] if m == 0 else dil_mask[:, 384:1152]
                items.append(att(d_sc, d_pb, d_pt, d_stat, parts, vs, mask, P ** -0.5,
                                 dil_o[:, m, h * P:(h + 1) * P], 3 * nk))
        return items

    proj_o = big(0, [P, TT, ODD_N])
    M_Q, M_K, M_V, M_I, M_F, M_O, L_Q, L_KV, L_KR = 0, 512, 1024, 2048, 2052, 2056, 3080, 3592, 4104
    qb = big(8336, [P, TT, 1536])
    kvb = big(11408, [P, TT, 2048])
    mla_o = big(15504, [P, TT, 1024])
    conv_w = big(17552, [P, 8, 4])
    conv_b = big(17584, [P, 8])
    gate_b = big(17592, [4, 2])
    mln_g = big(17600, [P, 256])
    qn_g = big(17856, [P, 512])
    kvn_g = big(18368, [P, 512])
    inv_freq = big(18880, [P, 32])
    mla_mask = big(18912, [P, 256])
    pos_i = big(19168, [P, TT], I32)
    pos_f = big(19176, [P, TT])
    rope_cs = big(19184, [P, 2, TT, 32])
    restart_o = big(19312, [4, 256])
    ang = big(19568, [P, 4, 64])
    lqT = scr(0, [P, 8, TOK])
    lkT = scr(2048, [P, 8, TOK])
    lqr = scr(4096, [64, 8, TOK])
    lkr = scr(6144, [64, TOK])
    l_sc, l_pb, l_pt, l_stat = att_buf(6400)
    rope_t = scr(11024, [P, 4, 256])
    tail_T = scr(10752, [72, TOK])

    def mla_items():
        items = []
        for h in range(8):
            for m in range(TT):
                nk = P * (m + 1)
                q = slice(m * P, (m + 1) * P)
                parts = [(0, [(lqT[:, h, q], lkT[:, h, :nk]), (lqr[:, h, q], lkr[:, :nk])])]
                vs = [kvb[:, j, 256 * h + 128:256 * h + 256] for j in range(m + 1)]
                mask = mla_mask[:, 128:256] if m == 0 else mla_mask[:, :]
                items.append(att(l_sc, l_pb, l_pt, l_stat, parts, vs, mask, 192 ** -0.5,
                                 mla_o[:, m, h * P:(h + 1) * P], nk))
        return items

    craw = scr(0, [P, 8, 260])
    qk = scr(2080, [P, 8, TOK])
    kw = scr(4128, [P, TT, 512])
    vaug = scr(5152, [P, TT, 4, 258])
    cst = scr(7216, [P, 4, 3, 258])
    eT = scr(10312, [P, 2, P])
    pT = scr(10568, [P, 2, P])
    qs = scr(10824, [P, 2, P])
    sE = scr(11080, [P, P])
    o257 = scr(11208, [P, 258])
    rows = big(8336, [4, 8, TOK])
    R_LI, R_LF, R_B, R_A, R_M, R_IS, R_W, R_E = range(8)
    zrow = big(10384, [4, 64])
    small4 = big(10448, [4, 32])
    m_prev, m_last, s_old, nm_last = small4[:, 0:5], small4[:, 8:12], small4[:, 16:20], small4[:, 24:28]
    head_row = big(10480, [4, 4, P])
    col6 = big(10992, [P, 6, 4])
    s_old_c = big(11016, [P, 4, 4])
    ml_mv = big(11032, [P, 8, 2])
    ml_rs = big(11048, [P, 8])
    ml_sh = big(11056, [P, 8])
    ml_st = big(11064, [P, 6])
    den = big(11072, [P, 2])
    m_o = big(11080, [P, TT, 1024])

    proj_s = big(0, [P, TT, SEC_N])
    kvm = big(8192, [P, TT, 1024])
    y = big(10240, [P, TT, D])
    pre = y
    mem_x = big(14336, [P, TT, D])
    bias = big(14336, [P, 16, 256])
    gain_a = big(14336, [P, D])
    gain_b = big(16384, [P, D])
    mix_g = big(2048, [P, D])
    mem_g = big(8192, [P, D])
    dump = scr(0, [P, TT, D])
    ssm_d = big(18432, [P, 512])
    b_glu = big(18944, [P, 512])
    S_Q, S_K, S_V, S_U, S_MQ = 0, 1024, 2048, 3072, 3584
    nqT = scr(0, [P, 8, TOK])
    nkT = scr(2048, [P, 8, TOK])
    n_sc, n_pb, n_pt, n_stat = att_buf(4096, 2)
    mqT = scr(5656, [P, 4, TOK])
    mkT = scr(6680, [P, 4, TOK])

    def second_items():
        items = []
        for h in range(8):
            for m in range(TT):
                parts = [(0, [(nqT[:, h, m * P:(m + 1) * P], nkT[:, h, :])])]
                vs = [proj_s[:, j, S_V + h * P:S_V + (h + 1) * P] for j in range(TT)]
                items.append(att(n_sc, n_pb, n_pt, n_stat, parts, vs, bias[:, 2 * h + m, :], 1.0,
                                 y[:, m, h * P:(h + 1) * P], 256, True))
        for h in range(4):
            for m in range(TT):
                parts = [(0, [(mqT[:, h, m * P:(m + 1) * P], mkT[:, h, :])])]
                vs = [kvm[:, j, 512 + h * P:512 + (h + 1) * P] for j in range(TT)]
                items.append(att(n_sc, n_pb, n_pt, n_stat, parts, vs, None, P ** -0.5,
                                 y[:, m, 1536 + h * P:1536 + (h + 1) * P], 256, True))
        return items

    NDJ = 32
    par = big(19456, [P, 22, NDJ])
    eb = scr(8192, [P, 2, NDJ, 16])
    fa = scr(9216, [P, NDJ, 4, 16])
    bmul = scr(11264, [P, NDJ, 32])
    braw = big(10240, [P, 2, NDJ, 32])
    ph = [big(10240 + 512 * j, [P, NDJ, 16]) for j in range(3)]
    steps16 = smalls[:, 80:96]
    bbar = big(12288, [P, 2, NDJ, 32])
    cmat = big(0, [P, 2, NDJ, 32])

    states = big(4096, [P, 2, 2, TOK])

    def spare(off, shape, dt=F32):
        n_view[0] += 1
        assert off + int(np.prod(shape[1:])) <= 8192
        return at(f"spare_{n_view[0]}", 8192 + off, shape, dt)

    uT_hi = spare(0, [P, 4, TOK], F32R)
    uT_lo = spare(1024, [P, 4, TOK], F32R)
    bT_hi = spare(2048, [P, 2, 2, 4, P], F32R)
    bT_lo = spare(4096, [P, 2, 2, 4, P], F32R)
    wave = spare(6144, [P, 3, 2, TOK])
    back1 = spare(7680, [P, 2, TOK])
    back2 = big(3584, [P, 2, TOK])
    t1 = big(5120, [P, 2, TOK])
    t2 = big(5632, [P, 2, TOK])
    q1 = scr(11264, [P, 2, TOK])
    q2 = scr(11776, [P, 2, TOK])
    xp = big(11264, [P, 2, TOK])
    gs = big(13312, [P, 2, TOK])
    t_glu = big(0, [P, TT, BLK])

    def ssm_items(j):
        return range(4 * j // 3, min(NDJ, 4 * (j + 1) // 3))

    ft_r = [big(0, [P, TT, BLK]), big(8192, [P, TT, BLK])]
    ft_h = [big(1024, [P, TT, 512]), big(9216, [P, TT, 1024])]
    acc_y = big(4096, [P, TT, D])
    mlp_g = [big(0, [P, D]), big(2048, [P, D])]

    def ffn(which):
        if which < 2:
            return A["ffn_wgu"][which], A["ffn_wd"][which], HID // 512, lambda ch: (ch * 512, ch * 512 + HID), 4
        return A["w_ff1_2"][0], A["w_ff2_2"][0], FF // 1024, lambda ch: (ch * 1024, ch * 1024 + 512), 8

    def ffn_body(kts):
        n = 16 + 4 * len(units_of(kts, 512))
        return {"unit": n, "block": 6, "turn": kts // 2, "split_turn": kts // 2, "hidden_h": 2 if kts == 8 else 0}

    def fused(E, link, out, in0, scalar, in1, op0, op1, tmp):
        if tmp is None:
            return E.scalar_tensor_tensor(out=out, in0=in0, scalar=scalar, in1=in1, op0=op0, op1=op1)
        link(E.tensor_scalar(tmp, in0, scalar, None, op0))
        return E.tensor_tensor(out, tmp, in1, op1)

    def turns_of(E, link, ang_, whole, turn_, tmp=None):
        TS = E.tensor_scalar
        link(TS(whole, ang_, 1 / TWO_PI, ROUND, ALU.mult, ALU.add))
        link(TS(whole, whole, ROUND, None, ALU.subtract))
        for part, base_ in ((TWO_PI_1, ang_), (TWO_PI_2, turn_), (TWO_PI_3, turn_)):
            link(fused(E, link, turn_, whole, -part, base_, ALU.mult, ALU.add, tmp))

    def sin_and_cos_of(E, link, turn_, cos_, spare_, tmp=None):
        TS = E.tensor_scalar
        link(TS(spare_, turn_, math.pi / 2, TWO_PI, ALU.is_gt, ALU.mult))
        link(fused(E, link, cos_, turn_, math.pi / 2, spare_, ALU.add, ALU.subtract, tmp))
        TS(cos_, cos_, PI_IN, -PI_IN, ALU.min, ALU.max)
        return TS(turn_, turn_, PI_IN, -PI_IN, ALU.min, ALU.max)

    def ssm_tables(pool, pc):
        G = nc.gpsimd
        TS, TENS = G.tensor_scalar, G.tensor_tensor
        pr = lambda k: par[:, k, :]

        def link(ins):
            pool_link(pc, ins)

        pool.wait_ge(ready("ssm_dt"), 1)
        link(TS(pr(4), pr(0), -1e-4, None, ALU.min))
        TENS(pr(3), pr(4), pr(2), ALU.mult)
        link(TENS(pr(5), pr(1), pr(2), ALU.mult))
        turns_of(G, link, pr(5), pr(21), pr(6), pr(20))
        link(TS(pr(11), pr(6), 1 / TWO_PI, None, ALU.mult))
        sin_and_cos_of(G, link, pr(6), pr(7), pr(20), pr(7)).then_inc(ready("ssm_turns"), 1)
        link(TS(pr(18), pr(11), 65536.0, ROUND, ALU.mult, ALU.add))
        link(TS(pr(18), pr(18), ROUND, 1 / 65536.0, ALU.subtract, ALU.mult))
        link(TENS(pr(19), pr(11), pr(18), ALU.subtract))
        pool.wait_ge(ready("ssm_ratio"), 1)
        pool.wait_ge(ready("ssm_b"), 16)
        wr, wi = (par[:, k, :].unsqueeze(2).broadcast_to([P, NDJ, 32]) for k in (16, 17))
        for ri in range(2):
            TENS(bbar[:, ri, :, :], braw[:, ri, :, :], wr, ALU.mult)
            link(TENS(bmul[:], braw[:, 1 - ri, :, :], wi, ALU.mult))
            last = TENS(bbar[:, ri, :, :], bbar[:, ri, :, :], bmul[:], ALU.add if ri else ALU.subtract)
            link(last)
        G.tensor_copy(smalls[:, 106:108], ident[:, 0:2]).then_inc(ready("ssm_bbar"), 1)
        hi_, lo_ = (par[:, k, :].unsqueeze(2).broadcast_to([P, NDJ, 16]) for k in (18, 19))
        pool.wait_ge(ready("ssm_steps"), 16)
        for kind in range(2):
            if kind:
                pool.wait_ge(ready("ssm_tab"), 1)
            s_ = steps16.unsqueeze(1).broadcast_to([P, NDJ, 16])
            a, b_, w = ph[0][:], ph[1][:], ph[2][:]
            link(TENS(a, s_, hi_, ALU.mult))
            if kind:
                link(TS(a, a, 16.0, None, ALU.mult))
            link(TS(w, a, ROUND, ROUND, ALU.add, ALU.subtract))
            TENS(a, a, w, ALU.subtract)
            link(TENS(b_, s_, lo_, ALU.mult))
            if kind:
                link(TS(b_, b_, 16.0, None, ALU.mult))
            link(TENS(a, a, b_, ALU.add))
            link(TS(w, a, ROUND, ROUND, ALU.add, ALU.subtract))
            link(TENS(a, a, w, ALU.subtract))
            link(TS(w, a, 0.25, None, ALU.is_gt))
            link(fused(G, link, b_, a, 0.25, w, ALU.add, ALU.subtract, b_))
            link(TS(b_, b_, HALF_IN, -HALF_IN, ALU.min, ALU.max))
            TS(a, a, HALF_IN, -HALF_IN, ALU.min, ALU.max).then_inc(ready("ssm_ph"), 1)

    block = ctx.enter_context(nc.Block())

    @block.sync
    def _(sp):
        c = Count()
        def project(w, pairs, rest, kts=KT_D):
            block_load(sp, c, w, 0, kts, 0, BLK)
            if pairs:
                with c.loop(sp, pairs, {"unit": 16}) as i:
                    for j in range(2):
                        block_load(sp, c, w, 0, kts, (2 * i + 1 + j) * BLK, BLK)
            for col, cols in rest:
                block_load(sp, c, w, 0, kts, col, cols)

        def hidden(which):
            w1, w2, n, cols, kts = ffn(which)

            def step(ch, first=False):
                for col in cols(ch):
                    block_load(sp, c, w1, 0, KT_D, col, BLK)
                if not first:
                    for j in range(4):
                        block_load(sp, c, w2, (ch - 1) * kts * P, kts, j * BLK, BLK)
            step(0, True)
            step(1)
            with c.loop(sp, n - 2, {"unit": ffn_body(kts)["unit"]}) as i:
                step(i + 2)
            for j in range(4):
                block_load(sp, c, w2, (n - 1) * kts * P, kts, j * BLK, BLK)

        w = A["even_w_in"][0]
        for k, nk in units_of(KT_D, BLK):
            if k % 4 == 0:
                for m in range(TT):
                    col = slice(k * P, (k + 4) * P)
                    sp.dma_start(x[:, m, col], A["x"][0, m * P:(m + 1) * P, col]).then_inc(ready(f"x_in{k // 4}"), 16)
            unit_load(sp, c, w[k * P:(k + nk) * P, 0:BLK].rearrange("(k p) n -> p k n", p=P), BLK)
        for col, cols in [(BLK * j, BLK) for j in range(1, GATE_AT)] + [(G_G, 16)]:
            block_load(sp, c, w, 0, KT_D, col, cols)
        with c.loop(sp, 3, {"unit": 16}) as i:
            for j in range(2):
                block_load(sp, c, w, 0, KT_D, (2 * i + j) * BLK + G_R, BLK)
        for col in LAST5:
            block_load(sp, c, w, 0, KT_D, col, BLK)
        project(A["even_w_o"][0], 0, [(BLK * j, BLK) for j in range(1, 4)], 12)
        if upto >= 2:
            hidden(0)
        if upto >= 3:
            project(A["odd_w_in"][0], 3, [(4096, 72), (3584, BLK)])
            project(A["odd_mla_wuq"][0], 0, [(BLK * j, BLK) for j in range(1, 3)], 4)
            project(A["odd_mla_wukv"][0], 0, [(BLK * j, BLK) for j in range(1, 4)], 4)
            project(A["odd_w_o"][0], 0, [(BLK * j, BLK) for j in range(1, 4)])
        if upto >= 4:
            hidden(1)
        if upto >= 5:
            project(A["w_in_2"][0], 3, [(3584, BLK)])
            project(A["w_mem_kv_2"][0], 0, [(BLK, BLK)])
            project(A["w_glu_2"][0], 0, [], 4)
            project(A["w_out_2"][0], 0, [(BLK * j, BLK) for j in range(1, 4)])
        if upto >= 6:
            hidden(2)
        for q in range(4):
            sp.wait_ge(ready("x_quarter"), 4 * (min(upto, 6) - 1) + q + 1)
            col = slice(q * BLK, (q + 1) * BLK)
            for m in range(TT):
                sp.dma_start(out[0, m * P:(m + 1) * P, col], x[:, m, col]).then_inc(ready("stored"), 16)
        sp.wait_ge(ready("stored"), 16 * TT * 4)

    @block.gpsimd
    def _(pool):
        pc = Count()

        def spread(dst, row):
            return pool.dma_start(dst, row.broadcast_to([P, row.shape[-1]]))

        for n, v in ((0, 1e-5), (1, 1.0), (3, 1e-6)):
            nc.gpsimd.memset(smalls[:, n:n + 1], v).then_inc(ready("consts"), 1)
        pool.dma_start(ident[:], A["c_ident"]).then_inc(ready("ident"), 16)
        for dst, src in ((chunk_pred[:], A["c_chunk_pred"]), (restart[:], A["c_restart"]), (dil_mask[:], A["c_dil_mask"]),
                         (wg2[:], A["even_gla_wg2"][0]), (gla_bg[:], A["l_gla_bg"])):
            pool.dma_start(dst, src).then_inc(ready("even_small"), 16)
        spread(gla_g[:], A["even_gla_norm_g"]).then_inc(ready("even_small"), 16)

        def vectors(n, which, layer):
            name = f"vec{n}"
            spread(ln_vec[n][0][:], A[f"{which}_g"][layer:layer + 1, :]).then_inc(ready(name), 16)
            spread(ln_vec[n][1][:], A[f"{which}_b"][layer:layer + 1, :]).then_inc(ready(name), 16)

        pool.wait_ge(att_done, 8)
        vectors(0, "ln1", 0)
        if upto >= 2:
            wait_normed(pool, 1)
            vectors(1, "ln2", 0)
        if upto >= 3:
            for dst, src in ((conv_w[:], A["l_conv_w"]), (conv_b[:], A["l_conv_b"]), (gate_b[:], A["l_gate_b"]),
                             (inv_freq[:], A["c_inv_freq"]), (mla_mask[:], A["c_mla_mask"]),
                             (pos_i[:], A["l_pos"]), (restart_o[:], A["c_restart"][0:4, 0:256])):
                pool.dma_start(dst, src).then_inc(ready("odd_small"), 16)
            spread(mln_g[:], A["odd_mlstm_norm_g"]).then_inc(ready("odd_small"), 16)
            spread(qn_g[:], A["odd_mla_qnorm_g"]).then_inc(ready("odd_small"), 16)
            spread(kvn_g[:], A["odd_mla_kvnorm_g"]).then_inc(ready("odd_small"), 16)
            pool.wait_ge(ready("ml_done"), 1)
            vectors(2, "ln1", 1)
        if upto >= 4:
            wait_normed(pool, 3)
            vectors(3, "ln2", 1)
        if upto >= 5:
            for m in range(TT):
                pool.dma_start(mem_x[:, m, :], A["mem_2"][0, m * P:(m + 1) * P, :]).then_inc(ready("mem_in"), 16)
            pool.dma_start(par[:, 0:3, :], A["l_lam"]).then_inc(ready("ssm_par"), 16)
            spread(mix_g[:], A["norm_mix_pre_2"]).then_inc(ready("mix_pre_g"), 16)
            spread(mem_g[:], A["mem_norm_2"]).then_inc(ready("mem_g"), 16)
            pool.wait_ge(ready("pre_turned"), 1)
            pool.dma_start(braw[:], A["l_b"]).then_inc(ready("ssm_b"), 16)
            pool.dma_start(steps16, A["c_steps"]).then_inc(ready("ssm_steps"), 16)
            ssm_tables(pool, pc)
            pool.wait_ge(ready("mem_turned"), 1)
            pool.dma_start(bias[:], A["l_bias"]).then_inc(ready("bias_in"), 16)
            spread(b_glu[:], A["b_glu_2"]).then_inc(ready("ssm_small"), 16)
            spread(ssm_d[:], A["l_ssm_d"]).then_inc(ready("ssm_small"), 16)
            pool.wait_ge(ready("heads_turned"), 1)
            pool.dma_start(cmat[:], A["l_c"]).then_inc(ready("ssm_c_in"), 16)

            def wave_of(i):
                dj = 16 * (i % 2) + i // 2
                if i >= 1:
                    pool.wait_ge(ready("ssm_wave"), i)
                if i >= 3:
                    pool.wait_ge(ready("ssm_back"), i - 2)
                for o, k, e in ((t1, 0, 0), (t2, 2, 1)):
                    last = nc.gpsimd.tensor_tensor(
                        o[:].rearrange("p r (a b) -> p r a b", b=16),
                        fa[:, dj, k:k + 2, :].unsqueeze(3).broadcast_to([P, 2, 16, 16]),
                        eb[:, e, dj, :].unsqueeze(1).unsqueeze(1).broadcast_to([P, 2, 16, 16]), ALU.mult)
                pool_link(pc, last)
                nc.gpsimd.tensor_tensor(wave[:, i % 3, :, :], t1[:], t2[:], ALU.add).then_inc(ready("ssm_wave"), 1)

            pool.wait_ge(ready("ssm_tab"), 2)
            wave_of(0)
            pool.wait_ge(ready("ssm_c_in"), 16)
            nc.gpsimd.tensor_scalar(cmat[:, 1, :, :], cmat[:, 1, :, :], -1.0, None, ALU.mult).then_inc(ready("ssm_c"), 1)
            for i in range(1, NDJ):
                wave_of(i)
            pool.wait_ge(att_done, 8 + 16 + 24)
            for j, name in enumerate(("out_norm_na_2", "out_norm_ssm_2", "out_norm_mem_2")):
                lo = (0, 1024, 1536)[j]
                spread(gain_a[:, lo:lo + (1024, 512, 512)[j]], A[name]).then_inc(ready("out_norms"), 16)
            spread(gain_b[:], A["norm_mix_post_2"]).then_inc(ready("mix_post_g"), 16)
            pool.wait_ge(ready("mix_turned"), 1)
            spread(mlp_g[0][:], A["norm_mlp_pre_2"]).then_inc(ready("mlp_pre_g"), 16)
            spread(mlp_g[1][:], A["norm_mlp_post_2"]).then_inc(ready("mlp_post_g"), 16)

    @block.scalar
    def _(act):
        c = Count()
        A_ = nc.scalar.activation
        act.wait_ge(ready("consts"), 3)

        def copy_out(col, dst, cols=BLK):
            end, b = c.end, c.n["block"] - 1

            def go():
                evac(act, c, end, b, lambda m: dst[:, m, bass.ds(col, cols)],
                     lambda m, o, s: nc.scalar.copy(o, s[:, :cols]))
            return go

        def project(dst, pairs, rest, kts=KT_D, led=False):
            if not led:
                block_split(unit_hi, act, c, kts, BLK)
            last, width = 0, BLK
            if pairs:
                with c.loop(act, pairs, {"unit": 16, "block": 2}) as i:
                    for j in range(2):
                        block_split(unit_hi, act, c, kts, BLK, copy_out((2 * i + j) * BLK, dst))
                last = 2 * pairs * BLK
            for col, cols in rest:
                block_split(unit_hi, act, c, kts, cols, copy_out(last, dst, width))
                last, width = col, cols
            return copy_out(last, dst, width)

        def blocks_only(n, kts):
            for _ in range(n):
                block_split(unit_hi, act, c, kts, BLK)

        def layer_norm(n):
            if upto > n:
                lead_early(unit_hi, act, c)
            act.wait_ge(ready("ln_stats"), n)
            A_(rstd, mean_var[:, :, 1], ACT.Sqrt, bias=eps).then_inc(ready("ln_std"), 1)
            if upto > n and n < 4:
                lead_hi(act, c)

        def square_quarter(src, q, away=dump):
            for m in range(TT):
                col = slice(q * BLK, (q + 1) * BLK)
                last = A_(away[:, m, col], src[:, m, col], ACT.Square, accum_out=sumsq[:, 4 * m + q:4 * m + q + 1])
            last.then_inc(ready("squared"), 1)

        def row_rms(k):
            act.wait_ge(ready("square_sum"), k)
            root(rms[:, 0:2], rms[:, 2:4], eps6, 1 / D).then_inc(ready("row_rms"), 1)

        def rms_of_x(n, k):
            for q in range(4):
                act.wait_ge(ready("x_quarter"), 4 * (n - 1) + q + 1)
                square_quarter(x, q)
            row_rms(k)
            lead_hi(act, c)

        def hidden(which):
            w1, w2, n, cols, kts = ffn(which)
            r, h = ft_r[which // 2], ft_h[which // 2]

            def take_block(end, b, col, before):
                if which < 2:
                    if before is not None:
                        act.wait_ge(acc_free[before % 2], c.freed(before))
                    evac(act, c, end, b, lambda m: r[:, m, :], lambda m, o, s: A_(o, s, ACT.Silu))
                else:
                    if c.n["hidden_h"]:
                        act.wait_ge(ready("hidden_h"), c.now("hidden_h"))
                    evac(act, c, end, b, lambda m: r[:, m, :], lambda m, o, s: A_(o, s, ACT.Relu))
                    act.wait_ge(acc_free[b % 2], c.freed(b))
                    for m in range(TT):
                        last = A_(h[:, m, col:col + BLK], r[:, m, :], ACT.Square)
                    last.then_inc(ready("hidden_h"), 1)
                    c.n["hidden_h"] += 1

            def step(ch, last_second=None):
                start = c.n["block"]
                if last_second is None:
                    start -= 1
                else:
                    block_split(unit_hi, act, c, KT_D, BLK)
                end0 = c.end

                def mid():
                    if last_second is not None:
                        take_act_hi(act, c, hT_hi, kts)
                    take_block(end0, start, 0, last_second)
                block_split(unit_hi, act, c, KT_D, BLK, mid)
                end1 = c.end
                second = (lambda: take_block(end1, start + 1, BLK, None)) if which == 2 else None
                if last_second is None:
                    if second:
                        second()
                else:
                    for j in range(4):
                        block_split(unit_hi, act, c, kts, BLK, second if j == 0 else None)
            step(0)
            step(1, c.n["block"] - 1)
            with c.loop(act, n - 2, ffn_body(kts)) as i:
                step(i + 2, c.n["block"] - 5)
            take_act_hi(act, c, hT_hi, kts)
            if which < 2:
                blocks_only(4, kts)
                return
            between = None
            for j in range(4):
                block_split(unit_hi, act, c, kts, BLK, between)
                between = squares_of_out(c.n["block"] - 1, j)
            between()

        def squares_of_out(b, j):
            def go():
                act.wait_ge(acc_free[b % 2], c.freed(b))
                square_quarter(acc_y, j)
            return go

        def root(dst, src, eps_, scale=1.0):
            return A_(dst, src, ACT.Sqrt, bias=eps_, scale=scale)

        lead_early(unit_hi, act, c)
        lead_hi(act, c)
        out_ = project(proj_e, 0, [(BLK * j, BLK) for j in range(1, GATE_AT)], led=True)
        block_split(unit_hi, act, c, KT_D, 16, out_)
        out_ = narrow_out(act, c, g1T[:])
        block_split(unit_hi, act, c, KT_D, BLK, out_)
        out_ = copy_out(G_R, proj_e)
        block_split(unit_hi, act, c, KT_D, BLK, out_)
        with c.loop(act, 2, {"unit": 16, "block": 2}) as i:
            for j in range(2):
                block_split(unit_hi, act, c, KT_D, BLK, copy_out((2 * i + j + 1) * BLK + G_R, proj_e))
        out_ = copy_out(G_R + 5 * BLK, proj_e)

        def gate_soft():
            act.wait_ge(ready("gla_z"), 1)
            for h in range(4):
                last = A_(gla_a[:, h * TOK:(h + 1) * TOK], psum[:, 6 + h // 2, (h % 2) * TOK:(h % 2 + 1) * TOK],
                          ACT.Identity, bias=gla_bg[:, h:h + 1])
            act_link(c, last)
            act_link(c, A_(ge[:], gla_a[:], ACT.Abs))
            act_link(c, A_(ge[:], ge[:], ACT.Exp, scale=-1.0))
            A_(ge[:], ge[:], ACT.Ln, bias=one).then_inc(ready("gla_soft"), 1)

        def gate_exps():
            act.wait_ge(ready("gla_b"), 1)
            A_(ge[:], gb[:], ACT.Exp, scale=1 / 16).then_inc(ready("gla_e"), 1)
            A_(gla_a[:], gb[:], ACT.Exp, scale=-1 / 16).then_inc(ready("gla_e"), 1)
            A_(gdec[:], gb[:].rearrange("p (n l) -> p n l", l=CHUNK)[:, :, CHUNK - 1], ACT.Exp, scale=1 / 16).then_inc(ready("gla_e"), 1)

        def gate_to_end():
            act.wait_ge(ready("gla_end"), 1)
            A_(gke[:], gke[:], ACT.Exp, scale=1 / 16).then_inc(ready("gla_e"), 1)

        def gate_out():
            A_(proj_e[:, :, G_R:G_R + 1024], proj_e[:, :, G_R:G_R + 1024], ACT.Silu).then_inc(ready("gla_silu"), 1)

        for col, gate in zip(LAST5, (gate_soft, gate_exps, gate_to_end, gate_out, None)):
            def between(out_=out_, gate=gate):
                out_()
                if gate is not None:
                    gate()
            block_split(unit_hi, act, c, KT_D, BLK, between)
            out_ = copy_out(col, proj_e)
        out_()
        for j in range(2):
            turn_take(act, c, 0, gq[:, 2 * j:2 * j + 2, :])
        for j in range(2):
            turn_take(act, c, 0, gk[:, 2 * j:2 * j + 2, :])
        for m in range(TT):
            turn_take(act, c, 0, gkt[:, m, :])
        for j in range(8):
            h, m = j // 2, j % 2
            act.wait_ge(ready("gla_o"), j + 1)
            act_link(c, nc.scalar.copy(g_o[:, m, h * 256:(h + 1) * 256], psum[:, 4 + j % 2, :256]))
            A_(gsq[:], g_o[:, m, h * 256:(h + 1) * 256], ACT.Square, accum_out=sumsq[:, j:j + 1]).then_inc(ready("gla_o_out"), 1)
            act.wait_ge(ready("gla_o_out"), j + 1)
        root(rms[:], sumsq[:], eps6, 1 / 256).then_inc(ready("gla_rms"), 1)
        for s in range(0, 12, 2):
            turn_take(act, c, 0, dqT[:, s:s + 2, :])
        for s in range(0, 12, 2):
            turn_take(act, c, 0, dkT[:, s:s + 2, :])
        att_act(act, c, dil_items())
        take_act_hi(act, c, aT_hi, 12)
        blocks_only(4, 12)
        layer_norm(1)
        if upto >= 2:
            hidden(0)
            layer_norm(2)
        if upto >= 3:
            out_ = project(proj_o, 3, [], led=True)
            block_split(unit_hi, act, c, KT_D, 72, out_)
            block_split(unit_hi, act, c, KT_D, BLK, narrow_out(act, c, tail_T[:]))
            copy_out(3584, proj_o)()
            turn_take(act, c, 0, proj_o[:, :, 4096:4168])
            wait_blocks(act, c)
            for m in range(TT):
                for j, col in enumerate((L_Q, L_KV)):
                    k = 2 * m + j
                    A_(rope_t[:, 0:2, :].rearrange("p a b -> p (a b)"), proj_o[:, m, col:col + 512], ACT.Square,
                       accum_out=sumsq[:, k:k + 1]).then_inc(ready("mla_sq"), 1)
                    act.wait_ge(ready("mla_sq"), k + 1)
            root(rms[:, 0:4], sumsq[:, 0:4], eps6, 1 / 512).then_inc(ready("mla_rms"), 1)
            A_(proj_o[:, :, M_O:M_O + 1024], proj_o[:, :, M_O:M_O + 1024], ACT.Sigmoid).then_inc(ready("ml_sigmoid"), 1)
            act.wait_ge(ready("rope_ang"), 1)
            A_(rope_cs[:].rearrange("p a m r -> p (a m r)"), ang[:, 0:2, :].rearrange("p a r -> p (a r)"),
               ACT.Sin).then_inc(ready("rope_cs"), 1)
            take_act_hi(act, c, aT_hi, 8)
            project(qb, 0, [(BLK * j, BLK) for j in range(1, 3)], 4)()
            project(kvb, 0, [(BLK * j, BLK) for j in range(1, 4)], 4)()
            for h in range(0, 8, 2):
                turn_take(act, c, 0, lqT[:, h:h + 2, :])
            for h in range(0, 8, 2):
                turn_take(act, c, 0, lkT[:, h:h + 2, :])
            for h in range(0, 8, 2):
                turn_take(act, c, 0, lqr[:, h:h + 2, :])
            turn_take(act, c, 0, lkr[:])
            att_act(act, c, mla_items())
            for t in range(0, 8, 2):
                turn_take(act, c, 0, craw[:, t:t + 2, 3:259])
            for j in (R_LI, R_LF):
                turn_take(act, c, 0, rows[:, j, :])
            act.wait_ge(ready("ml_gates"), 1)
            act_link(c, A_(rows[:, R_B, :], rows[:, R_LF, :], ACT.Abs))
            act_link(c, A_(rows[:, R_B, :], rows[:, R_B, :], ACT.Exp, scale=-1.0))
            A_(rows[:, R_B, :], rows[:, R_B, :], ACT.Ln, bias=one[0:4, :]).then_inc(ready("ml_soft"), 1)
            act.wait_ge(ready("ml_rows"), 1)
            for n in range(4):
                ch = slice(n * CHUNK, (n + 1) * CHUNK)
                A_(rows[:, R_IS, ch], rows[:, R_M, ch], ACT.Exp, scale=-1.0, bias=m_prev[:, n:n + 1])
                A_(rows[:, R_W, ch], rows[:, R_A, ch], ACT.Exp, bias=nm_last[:, n:n + 1])
            A_(rows[:, R_E, :], rows[:, R_E, :], ACT.Exp, scale=-1.0)
            A_(s_old, s_old, ACT.Exp).then_inc(ready("ml_exps"), 1)
            act.wait_ge(ready("ml_conv"), 1)
            A_(qk[:].rearrange("p t n -> p (t n)"), qk[:].rearrange("p t n -> p (t n)"), ACT.Silu).then_inc(ready("ml_qk"), 1)
            turn_take(act, c, 0, col6[:].rearrange("p a b -> p (a b)"))
            for m in range(TT):
                turn_take(act, c, 0, kw[:, m, :])
            for j in range(8):
                h, m = j // 2, j % 2
                act.wait_ge(ready("ml_s"), j + 1)
                if j >= 2:
                    act.wait_ge(ready("ml_p"), j - 1)
                A_(eT[:, j % 2, :], psum[:, 2 + j % 2, 0:P], ACT.Exp, scale=-1.0,
                   bias=col6[:, m, h:h + 1]).then_inc(ready("ml_e"), 1)
            act.wait_ge(ready("ml_stats"), 1)
            root(ml_rs[:], ml_mv[:, :, 1], eps).then_inc(ready("ml_std"), 1)
            take_act_hi(act, c, aT_hi, KT_D)
            blocks_only(4, KT_D)
            layer_norm(3)
        if upto >= 4:
            hidden(1)
            if upto >= 5:
                act.wait_ge(ready("mem_in"), 32)
                for m in range(TT):
                    act_link(c, A_(dump[:, m, :], mem_x[:, m, :], ACT.Square, accum_out=mem_sq[:, m:m + 1]))
                root(mem_rs, mem_sq, eps6, 1 / D).then_inc(ready("mem_rms"), 1)
                act.wait_ge(ready("ssm_par"), 16)
                A_(par[:, 2, :], par[:, 2, :], ACT.Exp).then_inc(ready("ssm_dt"), 1)
            layer_norm(4)
        if upto >= 5:
            rms_of_x(4, 1)
            def lam_bar():
                act.wait_ge(ready("ssm_turns"), 1)
                A_(par[:, 8, :], par[:, 6, :], ACT.Sin)
                A_(par[:, 9, :], par[:, 7, :], ACT.Sin)
                A_(par[:, 10, :], par[:, 3, :], ACT.Exp).then_inc(ready("ssm_lam"), 1)

            def fine_turns():
                act.wait_ge(ready("ssm_ph"), 1)
                A_(eb[:, 0, :, :], ph[1][:], ACT.Sin, scale=TWO_PI)
                A_(eb[:, 1, :, :], ph[0][:], ACT.Sin, scale=TWO_PI).then_inc(ready("ssm_tab"), 1)

            def coarse_turns():
                act.wait_ge(ready("ssm_ph"), 2)
                A_(fa[:, :, 0, :], ph[1][:], ACT.Sin, scale=TWO_PI)
                A_(fa[:, :, 1, :], ph[0][:], ACT.Sin, scale=TWO_PI)
                A_(fa[:, :, 2, :], ph[0][:], ACT.Sin, scale=-TWO_PI)
                A_(fa[:, :, 3, :], ph[1][:], ACT.Sin, scale=TWO_PI).then_inc(ready("ssm_tab"), 1)

            def step(out_, tables):
                def go():
                    if out_ is not None:
                        out_()
                    if tables is not None:
                        tables()
                return go
            out_ = copy_out(0, proj_s)
            for j, tables in enumerate((lam_bar, None, None, fine_turns, None, coarse_turns, None), 1):
                block_split(unit_hi, act, c, KT_D, BLK, step(out_, tables))
                out_ = copy_out(j * BLK, proj_s)
            out_()
            take_act_hi(act, c, aT_hi, KT_D)
            project(kvm, 0, [(BLK, BLK)])()
            for h in range(0, 8, 2):
                turn_take(act, c, 0, nqT[:, h:h + 2, :], P ** -0.5)
            for h in range(0, 8, 2):
                turn_take(act, c, 0, nkT[:, h:h + 2, :])
            for h in range(0, 4, 2):
                turn_take(act, c, 0, mqT[:, h:h + 2, :])
            for h in range(0, 4, 2):
                turn_take(act, c, 0, mkT[:, h:h + 2, :])
            for q in range(0, 4, 2):
                turn_take_hi(act, c, uT_hi[:, q:q + 2, :].rearrange("p q t -> p (q t)"))
            for d in range(2):
                for ri in range(2):
                    turn_take_hi(act, c, bT_hi[:, d, ri, :, :].rearrange("p q n -> p (q n)"))
            att_act(act, c, second_items())
            act.wait_ge(ready("ssm_y"), 1)
            A_(y[:, :, 1024:1536], y[:, :, 1024:1536], ACT.Gelu_apprx_tanh).then_inc(ready("ssm_gelu"), 1)
            take_act_hi(act, c, aT_hi, 4)
            block_split(unit_hi, act, c, 4, BLK)
            act.wait_ge(ready("glu_z"), 1)
            A_(t_glu[:], t_glu[:], ACT.Sigmoid).then_inc(ready("glu_s"), 1)
            act.wait_ge(ready("ssm_out"), 1)
            for m in range(TT):
                for j, (lo, w) in enumerate(((0, 1024), (1024, 512), (1536, 512))):
                    act_link(c, A_(proj_s[:, m, 0:w], y[:, m, lo:lo + w], ACT.Square, accum_out=sumsq[:, 3 * m + j:3 * m + j + 1]))
                    last = root(rms[:, 3 * m + j:3 * m + j + 1], sumsq[:, 3 * m + j:3 * m + j + 1], eps6, 1 / w)
                    act_link(c, last)
            A_(sumsq[:, 6:7], eps, ACT.Copy).then_inc(ready("out_rms"), 1)
            take_act_hi(act, c, aT_hi, KT_D)
            def out_and_squares(j):
                out_, b = copy_out(j * BLK, acc_y), c.n["block"] - 1

                def go():
                    out_()
                    act.wait_ge(acc_free[b % 2], c.freed(b))
                    square_quarter(acc_y, j, pre)
                return go
            between = None
            for j in range(4):
                block_split(unit_hi, act, c, KT_D, BLK, between)
                between = out_and_squares(j)
            if upto >= 6:
                lead_early(unit_hi, act, c)
            between()
            row_rms(2)
        if upto >= 6:
            rms_of_x(5, 3)
            hidden(2)
            row_rms(4)

    @block.vector
    def _(dve):
        c = Count()
        V = nc.vector
        TS, STT, TENS = V.tensor_scalar, V.scalar_tensor_tensor, V.tensor_tensor

        def link(ins):
            dve_link(c, ins)

        def project(pairs, rest, kts=KT_D, led=False):
            if not led:
                block_split(unit_lo, dve, c, kts, BLK)
            if pairs:
                with c.loop(dve, pairs, {"unit": 16, "block": 2}):
                    for _ in range(2):
                        block_split(unit_lo, dve, c, kts, BLK)
            for _, cols in rest:
                block_split(unit_lo, dve, c, kts, cols)

        def add_out(end, b, dst, j, scale=None):
            def do(m, o, s):
                if scale is None:
                    return TENS(o, o, s, ALU.add)
                return STT(out=o, in0=o, scalar=scale, in1=s, op0=ALU.mult, op1=ALU.add)
            return lambda: evac(dve, c, end, b, lambda m: dst[:, m, j * BLK:(j + 1) * BLK], do)

        def with_stats(add, b, j):
            def go():
                add()
                dve.wait_ge(acc_free[b % 2], c.freed(b))
                for m in range(TT):
                    last = V.bn_stats(stats[:, m, :, :].rearrange("p c s -> p (c s)")[:, 6 * j:6 * j + 6],
                                      x[:, m, j * BLK:(j + 1) * BLK])
                last.then_inc(ready("ln_cols"), 1)
            return go

        def residual(kts, n):
            out_ = None
            for j in range(4):
                block_split(unit_lo, dve, c, kts, BLK, out_)
                b = c.n["block"] - 1
                out_ = with_stats(add_out(c.end, b, x, j, ALPHA), b, j)
            if upto > n:
                lead_early(unit_lo, dve, c)
            out_()

        def layer_norm(n):
            dve.wait_ge(ready("ln_cols"), 4 * n)
            for m in range(TT):
                last = V.bn_aggr(mean_var[:, m, :], stats[:, m, :, :].rearrange("p c s -> p (c s)"))
            last.then_inc(ready("ln_stats"), 1)
            dve.wait_ge(ready("ln_stats"), n)
            dve.wait_ge(ready(f"vec{n - 1}"), 32)
            g, b = ln_vec[n - 1]

            def prepare(q):
                col = slice(q * BLK, (q + 1) * BLK)
                for m in range(TT):
                    last = STT(out=x[:, m, col], in0=x[:, m, col], scalar=mean_var[:, m, 0:1], in1=g[:, col],
                               op0=ALU.subtract, op1=ALU.mult)
                link(last)
                if q == 0:
                    dve.wait_ge(ready("ln_std"), n)
                    link(V.reciprocal(rstd, rstd))
                for m in range(TT):
                    last = STT(out=x[:, m, col], in0=x[:, m, col], scalar=rstd[:, m:m + 1], in1=b[:, col],
                               op0=ALU.mult, op1=ALU.add)
                last.then_inc(ready("x_quarter"), 1)

            if upto > n and n < 4:
                lead_lo(dve, c, prepare)
            else:
                for q in range(4):
                    prepare(q)

        def row_rms(k):
            dve.wait_ge(ready("squared"), 4 * k)
            V.reduce_sum(rms[:, 2:4], sumsq.rearrange("p (m q) -> p m q", q=4), AX_X).then_inc(ready("square_sum"), 1)
            dve.wait_ge(ready("row_rms"), k)
            link(V.reciprocal(rms[:, 0:2], rms[:, 0:2]))

        def normed_lead(k, g, g_ready):
            row_rms(k)
            dve.wait_ge(ready(g_ready), 16)

            def prepare(q):
                col = slice(q * BLK, (q + 1) * BLK)
                for m in range(TT):
                    last = STT(out=pre[:, m, col], in0=x[:, m, col], scalar=rms[:, m:m + 1], in1=g[:, col],
                               op0=ALU.mult, op1=ALU.mult)
                last.then_inc(ready("pre_quarter"), 1)
            lead_lo(dve, c, prepare)

        def add_normed(k, g, g_ready):
            row_rms(k)
            dve.wait_ge(ready(g_ready), 16)
            for q in range(4):
                col = slice(q * BLK, (q + 1) * BLK)
                for m in range(TT):
                    last = STT(out=acc_y[:, m, col], in0=acc_y[:, m, col], scalar=rms[:, m:m + 1], in1=g[:, col],
                               op0=ALU.mult, op1=ALU.mult)
                link(last)
                TENS(x[:, :, col], x[:, :, col], acc_y[:, :, col], ALU.add).then_inc(ready("x_quarter"), 1)

        def hidden(which):
            w1, w2, n, cols, kts = ffn(which)
            r, h = ft_r[which // 2], ft_h[which // 2]
            dst = x if which < 2 else acc_y
            tail = slice(3 * BLK, 4 * BLK)
            if which < 2:
                dve.wait_ge(turn_free[0], c.now("turn", 1, 2))
                dve.wait_ge(turn_free[1], c.now("turn", 0, 2))
                last = TS(x[:, :, tail], x[:, :, tail], ALPHA, None, ALU.mult)
            else:
                last = V.memset(acc_y[:, :, tail], 0.0)
            link(last)

            def take_second(end, b):
                dve.wait_ge(acc_free[(b - 1) % 2], c.freed(b - 1))
                evac(dve, c, end, b, lambda m: h[:, m, :], lambda m, o, s: TENS(o, r[:, m, :], s, ALU.mult))

            def first_out(end, b, j):
                if which < 2:
                    return add_out(end, b, x, j, ALPHA)
                return lambda: evac(dve, c, end, b, lambda m: dst[:, m, j * BLK:(j + 1) * BLK],
                                    lambda m, o, s: V.tensor_copy(o, s))

            def step(ch, before, first_outs):
                start = c.n["block"]
                if ch is None:
                    start -= 1
                else:
                    block_split(unit_lo, dve, c, KT_D, BLK, before)
                block_split(unit_lo, dve, c, KT_D, BLK, (lambda: take_act_lo(dve, c, hT_hi, hT_lo, kts)) if ch is not None else None)
                end1 = c.end
                if ch is None:
                    return lambda: take_second(end1, start + 1)
                out_ = (lambda: take_second(end1, start + 1)) if which < 2 else None
                for j in range(4):
                    block_split(unit_lo, dve, c, kts, BLK, out_)
                    e, b = c.end, c.n["block"] - 1
                    out_ = first_out(e, b, j) if first_outs and j < 3 else add_out(e, b, dst, j)
                return out_
            after = step(None, None, False)
            after = step(1, after if which < 2 else None, True)
            end, b = c.end, c.n["block"] - 1
            with c.loop(dve, n - 2, ffn_body(kts) | {"dve_step": 0}):
                step(2, add_out(end, b, dst, 3), False)
            end, b = c.end, c.n["block"] - 1
            add_out(end, b, dst, 3)()
            take_act_lo(dve, c, hT_hi, hT_lo, kts)
            out_ = None
            for j in range(4):
                block_split(unit_lo, dve, c, kts, BLK, out_)
                b = c.n["block"] - 1
                out_ = add_out(c.end, b, dst, j)
                if which < 2:
                    out_ = with_stats(out_, b, j)
            if which < 2 and upto > 2 * which + 2:
                lead_early(unit_lo, dve, c)
            out_()

        lead_early(unit_lo, dve, c)
        lead_lo(dve, c, None)
        project(0, [(BLK * j, BLK) for j in range(1, GATE_AT)] + [(G_G, 16)], led=True)
        block_split(unit_lo, dve, c, KT_D, BLK)
        block_split(unit_lo, dve, c, KT_D, BLK)
        with c.loop(dve, 2, {"unit": 16, "block": 2}):
            for _ in range(2):
                block_split(unit_lo, dve, c, KT_D, BLK)

        def gate_sums():
            dve.wait_ge(ready("gla_soft"), 1)
            link(STT(out=gla_a[:], in0=gla_a[:], scalar=0.0, in1=ge[:], op0=ALU.min, op1=ALU.subtract))
            V.tensor_tensor_scan(gb[:], restart[:], gla_a[:], 0.0, ALU.mult, ALU.add).then_inc(ready("gla_b"), 1)

        def gate_to_end():
            dve.wait_ge(ready("gla_b"), 1)
            by_chunk = gb[:].rearrange("p (n l) -> p n l", l=CHUNK)
            TENS(gke[:].rearrange("p (n l) -> p n l", l=CHUNK), by_chunk[:, :, CHUNK - 1:].broadcast_to([P, 16, CHUNK]),
                 by_chunk, ALU.subtract).then_inc(ready("gla_end"), 1)

        for gate in (None, gate_sums, gate_to_end, None, None):
            block_split(unit_lo, dve, c, KT_D, BLK, gate)
        for j in range(2):
            turn_take(dve, c, 1, gq[:, 2 * j:2 * j + 2, :])
        for j in range(2):
            turn_take(dve, c, 1, gk[:, 2 * j:2 * j + 2, :])
        dve.wait_ge(ready("gla_e"), 4)
        wait_turns(dve, c)
        TENS(gke[:], gke[:], gk[:].rearrange("p h t -> p (h t)"), ALU.mult).then_inc(ready("gla_ke"), 1)
        dve.wait_ge(ready("gla_ke"), 1)
        STT(out=gq[:].rearrange("p h t -> p (h t)"), in0=gq[:].rearrange("p h t -> p (h t)"), scalar=P ** -0.5, in1=ge[:],
            op0=ALU.mult, op1=ALU.mult)
        V.memset(gsT[:], 0.0)
        TENS(gk[:].rearrange("p h t -> p (h t)"), gk[:].rearrange("p h t -> p (h t)"), gla_a[:], ALU.mult).then_inc(ready("gla_qk"), 1)
        dve.wait_ge(ready("gla_qk"), 1)
        for m in range(TT):
            turn_take(dve, c, 1, gkt[:, m, :])
        for h in range(4):
            dve.wait_ge(ready("gla_loc"), h + 1)
            b0 = 2 * (h % 2)
            link(V.tensor_copy(gst[:, h, 0, :], psum[:, b0, 0:256]))
            for n in (1, 2):
                ins = STT(out=gst[:, h, n, :], in0=gst[:, h, n - 1, :], scalar=gdec[:, 4 * h + n:4 * h + n + 1],
                          in1=(psum[:, b0, 256:512] if n == 2 else psum[:, b0 + 1, 0:256]), op0=ALU.mult, op1=ALU.add)
                if n == 1:
                    link(ins)
                else:
                    ins.then_inc(ready("gla_state"), 1)
        for j in range(8):
            dve.wait_ge(ready("gla_s"), j + 1)
            if j >= 2:
                dve.wait_ge(ready("gla_o"), j - 1)
            V.copy_predicated(gsT[:, j % 2, :], chunk_pred[:], psum[:, 6 + j % 2, :P]).then_inc(ready("gla_sm"), 1)
        dve.wait_ge(ready("gla_rms"), 1)
        link(V.reciprocal(rms[:], rms[:]))
        for j in range(8):
            h, m = j // 2, j % 2
            o = g_o[:, m, h * 256:(h + 1) * 256]
            last = STT(out=o, in0=o, scalar=rms[:, j:j + 1], in1=gla_g[:], op0=ALU.mult, op1=ALU.mult)
        link(last)
        dve.wait_ge(ready("gla_silu"), 1)
        link(TENS(proj_e[:, :, G_R:G_R + 1024], proj_e[:, :, G_R:G_R + 1024], g_o[:], ALU.mult))
        TENS(sumsq[:, 0:1], sumsq[:, 1:2], sumsq[:, 2:3], ALU.add).then_inc(ready("gla_done"), 1)
        for s in range(0, 12, 2):
            turn_take(dve, c, 1, dqT[:, s:s + 2, :])
        for s in range(0, 12, 2):
            turn_take(dve, c, 1, dkT[:, s:s + 2, :])
        att_dve(dve, c, dil_items())
        take_act_lo(dve, c, aT_hi, aT_lo, 12)
        residual(12, 1)
        layer_norm(1)
        if upto >= 2:
            hidden(0)
            layer_norm(2)
        if upto >= 3:
            project(3, [(4096, 72), (3584, BLK)], led=True)
            turn_take(dve, c, 1, proj_o[:, :, 4096:4168])
            dve.wait_ge(ready("odd_small"), 16 * 10)
            link(V.tensor_copy(pos_f[:], pos_i[:]))
            for m in range(TT):
                last = TS(ang[:, 0, 32 * m:32 * m + 32], inv_freq[:], pos_f[:, m:m + 1], None, ALU.mult)
            link(last)
            turns_of(V, link, ang[:, 0, :], ang[:, 2, :], ang[:, 0, :])
            sin_and_cos_of(V, link, ang[:, 0, :], ang[:, 1, :], ang[:, 2, :]).then_inc(ready("rope_ang"), 1)
            dve.wait_ge(ready("mla_rms"), 1)
            link(V.reciprocal(rms[:, 0:4], rms[:, 0:4]))
            for m in range(TT):
                for j, (col, g) in enumerate(((L_Q, qn_g), (L_KV, kvn_g))):
                    o = proj_o[:, m, col:col + 512]
                    last = STT(out=o, in0=o, scalar=rms[:, 2 * m + j:2 * m + j + 1], in1=g[:], op0=ALU.mult, op1=ALU.mult)
            last.then_inc(ready("mla_normed"), 1)
            take_act_lo(dve, c, aT_hi, aT_lo, 8)
            for _ in range(7):
                block_split(unit_lo, dve, c, 4, BLK)
            dve.wait_ge(ready("rope_cs"), 1)
            wait_blocks(dve, c)

            def rope(pair, m, n, t):
                x1, x2 = pair
                sn, cs = (rope_cs[:, k, m:m + 1, :].broadcast_to([P, n, 32]) for k in range(2))
                t = [rope_t[:, k, :32 * n].rearrange("p (h r) -> p h r", r=32) for k in range(4)]
                TENS(t[0], x1, cs, ALU.mult)
                TENS(t[1], x2, sn, ALU.mult)
                TENS(t[2], x1, sn, ALU.mult)
                link(TENS(t[3], x2, cs, ALU.mult))
                TENS(x1, t[0], t[1], ALU.subtract)
                last = TENS(x2, t[2], t[3], ALU.add)
                link(last)
            for m in range(TT):
                q = qb[:, m, :].rearrange("p (h c) -> p h c", c=192)
                rope((q[:, :, 128:160], q[:, :, 160:192]), m, 8, None)
                k = proj_o[:, m, L_KR:L_KR + 64].rearrange("p (h c) -> p h c", c=64)
                rope((k[:, :, 0:32], k[:, :, 32:64]), m, 1, None)
            V.tensor_copy(smalls[:, 96:98], ident[:, 0:2]).then_inc(ready("roped"), 1)
            for h in range(0, 8, 2):
                turn_take(dve, c, 1, lqT[:, h:h + 2, :])
            for h in range(0, 8, 2):
                turn_take(dve, c, 1, lkT[:, h:h + 2, :])
            for h in range(0, 8, 2):
                turn_take(dve, c, 1, lqr[:, h:h + 2, :])
            turn_take(dve, c, 1, lkr[:])
            att_dve(dve, c, mla_items())
            dve.wait_ge(att_done, 8 + 16)
            V.memset(craw[:, :, 0:3], 0.0)
            V.memset(vaug[:, :, :, 256:257], 1.0)
            V.memset(pT[:], 0.0)
            V.memset(zrow[:], 0.0)
            V.memset(m_prev[:, 0:1], 0.0)
            for h in range(4):
                last = V.tensor_copy(head_row[:, h, :], ident[0:4, h:h + 1].broadcast_to([4, P]))
            for m in range(TT):
                last = V.tensor_copy(vaug[:, m, :, 0:256], proj_o[:, m, M_V:M_V + 1024].rearrange("p (h e) -> p h e", h=4))
            link(last)
            for t in range(0, 8, 2):
                turn_take(dve, c, 1, craw[:, t:t + 2, 3:259])
            for j in (R_LI, R_LF):
                turn_take(dve, c, 1, rows[:, j, :])
            wait_turns(dve, c)
            TS(rows[:, R_LI, :], rows[:, R_LI, :], gate_b[:, 0:1], None, ALU.add)
            TS(rows[:, R_LF, :], rows[:, R_LF, :], gate_b[:, 1:2], None, ALU.add).then_inc(ready("ml_gates"), 1)
            for k in range(4):
                for t in range(8):
                    if k == 0:
                        last = TS(qk[:, t, :], craw[:, t, 0:TOK], conv_w[:, t, 0:1], conv_b[:, t:t + 1], ALU.mult, ALU.add)
                    else:
                        last = STT(out=qk[:, t, :], in0=craw[:, t, k:k + TOK], scalar=conv_w[:, t, k:k + 1],
                                   in1=qk[:, t, :], op0=ALU.mult, op1=ALU.add)
                if k < 3:
                    link(last)
                else:
                    last.then_inc(ready("ml_conv"), 1)
            dve.wait_ge(ready("ml_soft"), 1)
            link(STT(out=rows[:, R_LF, :], in0=rows[:, R_LF, :], scalar=0.0, in1=rows[:, R_B, :], op0=ALU.min, op1=ALU.subtract))
            link(V.tensor_tensor_scan(rows[:, R_B, :], restart_o[:], rows[:, R_LF, :], 0.0, ALU.mult, ALU.add))
            link(TENS(rows[:, R_A, :], rows[:, R_LI, :], rows[:, R_B, :], ALU.subtract))
            for n in range(4):
                ch = slice(n * CHUNK, (n + 1) * CHUNK)
                e = (n + 1) * CHUNK - 1
                link(V.tensor_tensor_scan(rows[:, R_M, ch], zrow[:], rows[:, R_A, ch], m_prev[:, n:n + 1], ALU.add, ALU.max))
                V.tensor_copy(m_last[:, n:n + 1], rows[:, R_M, e:e + 1])
                link(TENS(m_prev[:, n + 1:n + 2], rows[:, R_B, e:e + 1], rows[:, R_M, e:e + 1], ALU.add))
            TS(nm_last, m_last, -1.0, None, ALU.mult)
            TENS(s_old, m_prev[:, 0:4], m_last, ALU.subtract)
            TENS(rows[:, R_E, :], rows[:, R_B, :], rows[:, R_M, :], ALU.add).then_inc(ready("ml_rows"), 1)
            turn_take(dve, c, 1, col6[:].rearrange("p a b -> p (a b)"))
            for m in range(TT):
                turn_take(dve, c, 1, kw[:, m, :])
            wait_turns(dve, c)
            for m in range(TT):
                for h in range(4):
                    last = TS(kw[:, m, h * P:(h + 1) * P], kw[:, m, h * P:(h + 1) * P], col6[:, 2 + m, h:h + 1],
                              P ** -0.5, ALU.mult, ALU.mult)
            last.then_inc(ready("ml_kw"), 1)
            dve.wait_ge(ready("ml_sold"), 1)
            link(V.tensor_copy(s_old_c[:].rearrange("p h n -> p (h n)"), psum[:, 6, 0:16]))
            for h in range(4):
                dve.wait_ge(ready("ml_loc"), h + 1)
                b3 = ((0, 1, 4), (2, 3, 5))[h % 2]
                link(V.tensor_copy(cst[:, h, 0, 0:257], psum[:, b3[0], 0:257]))
                for n in (1, 2):
                    ins = STT(out=cst[:, h, n, 0:257], in0=cst[:, h, n - 1, 0:257], scalar=s_old_c[:, h, n:n + 1],
                              in1=psum[:, b3[n], 0:257], op0=ALU.mult, op1=ALU.add)
                    if n == 1:
                        link(ins)
                    else:
                        ins.then_inc(ready("ml_state"), 1)

            def ml_weights(j):
                h, m = j // 2, j % 2
                dve.wait_ge(ready("ml_e"), j + 1)
                if j >= 1:
                    dve.wait_ge(ready("ml_p"), j)
                if j >= 2:
                    dve.wait_ge(ready("ml_n"), j - 1)
                link(STT(out=sE[:], in0=psum[:, 2 + j % 2, 256:384], scalar=P ** -0.5, in1=eT[:, j % 2, :],
                         op0=ALU.mult, op1=ALU.mult))
                V.copy_predicated(pT[:, j % 2, :], chunk_pred[:], sE[:])
                TENS(qs[:, j % 2, :], qk[:, h, m * P:(m + 1) * P], psum[:, 2 + j % 2, 128:256],
                     ALU.mult).then_inc(ready("ml_p"), 1)

            ml_weights(0)
            for j in range(8):
                h, m = j // 2, j % 2
                if j < 7:
                    ml_weights(j + 1)
                dve.wait_ge(ready("ml_n"), j + 1)
                V.tensor_copy(o257[:, 0:257], psum[:, 6 + j % 2, 0:257]).then_inc(ready("ml_out"), 1)
                dve.wait_ge(ready("ml_out"), j + 1)
                link(STT(out=den[:, 0:1], in0=o257[:, 256:257], scalar=-1.0, in1=o257[:, 256:257], op0=ALU.mult, op1=ALU.max))
                link(TENS(den[:, 1:2], den[:, 0:1], col6[:, 4 + m, h:h + 1], ALU.max))
                link(V.reciprocal(den[:, 0:1], den[:, 1:2]))
                o = m_o[:, m, h * 256:(h + 1) * 256]
                link(TS(o, o257[:, 0:256], den[:, 0:1], None, ALU.mult))
                link(V.bn_stats(ml_st[:], o))
                link(V.bn_aggr(ml_mv[:, j, :], ml_st[:]))
            V.tensor_copy(smalls[:, 98:100], ident[:, 0:2]).then_inc(ready("ml_stats"), 1)
            dve.wait_ge(ready("ml_std"), 1)
            link(V.reciprocal(ml_rs[:], ml_rs[:]))
            link(STT(out=ml_sh[:], in0=ml_mv[:, :, 0], scalar=-1.0, in1=ml_rs[:], op0=ALU.mult, op1=ALU.mult))
            for j in range(8):
                h, m = j // 2, j % 2
                o = m_o[:, m, h * 256:(h + 1) * 256]
                last = TS(o, o, ml_rs[:, j:j + 1], ml_sh[:, j:j + 1], ALU.mult, ALU.add)
            link(last)
            for j in range(8):
                h, m = j // 2, j % 2
                o = m_o[:, m, h * 256:(h + 1) * 256]
                last = TENS(o, o, mln_g[:], ALU.mult)
            link(last)
            dve.wait_ge(ready("ml_sigmoid"), 1)
            co = proj_o[:, :, M_O:M_O + 1024]
            TENS(co, co, m_o[:], ALU.mult).then_inc(ready("ml_done"), 1)
            take_act_lo(dve, c, aT_hi, aT_lo, KT_D)
            residual(KT_D, 3)
            layer_norm(3)
        if upto >= 4:
            hidden(1)
            layer_norm(4)
        if upto >= 5:
            normed_lead(1, mix_g, "mix_pre_g")
            V.tensor_copy(smalls[:, 108:110], ident[:, 0:2]).then_inc(ready("pre_turned"), 1)

            def norm_memory():
                dve.wait_ge(ready("mem_rms"), 1)
                link(V.reciprocal(mem_rs, mem_rs))
                dve.wait_ge(ready("mem_g"), 16)
                for m in range(TT):
                    last = STT(out=mem_x[:, m, :], in0=mem_x[:, m, :], scalar=mem_rs[:, m:m + 1], in1=mem_g[:],
                               op0=ALU.mult, op1=ALU.mult)
                last.then_inc(ready("mem_normed"), 1)

            pr = lambda k: par[:, k, :]

            def ratio():
                dve.wait_ge(ready("ssm_lam"), 1)
                TENS(pr(12), pr(10), pr(9), ALU.mult)
                TENS(pr(13), pr(10), pr(8), ALU.mult)
                TENS(pr(14), pr(4), pr(4), ALU.mult)
                link(TENS(pr(15), pr(1), pr(1), ALU.mult))
                TS(pr(12), pr(12), 1.0, None, ALU.subtract)
                link(TENS(pr(14), pr(14), pr(15), ALU.add))
                link(V.reciprocal(pr(14), pr(14)))
                TENS(pr(16), pr(12), pr(4), ALU.mult)
                TENS(pr(17), pr(13), pr(4), ALU.mult)
                TENS(pr(15), pr(13), pr(1), ALU.mult)
                link(TENS(pr(20), pr(12), pr(1), ALU.mult))
                TENS(pr(16), pr(16), pr(15), ALU.add)
                link(TENS(pr(17), pr(17), pr(20), ALU.subtract))
                TENS(pr(16), pr(16), pr(14), ALU.mult)
                TENS(pr(17), pr(17), pr(14), ALU.mult).then_inc(ready("ssm_ratio"), 1)

            for between in (norm_memory, ratio) + (None,) * 5:
                block_split(unit_lo, dve, c, KT_D, BLK, between)
            take_act_lo(dve, c, aT_hi, aT_lo, KT_D)
            V.tensor_copy(smalls[:, 110:112], ident[:, 0:2]).then_inc(ready("mem_turned"), 1)
            project(0, [(0, BLK)])
            for h in range(0, 8, 2):
                turn_take(dve, c, 1, nqT[:, h:h + 2, :], P ** -0.5)
            for h in range(0, 8, 2):
                turn_take(dve, c, 1, nkT[:, h:h + 2, :])
            for h in range(0, 4, 2):
                turn_take(dve, c, 1, mqT[:, h:h + 2, :])
            for h in range(0, 4, 2):
                turn_take(dve, c, 1, mkT[:, h:h + 2, :])
            for q in range(0, 4, 2):
                turn_take_lo(dve, c, uT_lo[:, q:q + 2, :].rearrange("p q t -> p (q t)"),
                             uT_hi[:, q:q + 2, :].rearrange("p q t -> p (q t)"))
            for d in range(2):
                for ri in range(2):
                    turn_take_lo(dve, c, bT_lo[:, d, ri, :, :].rearrange("p q n -> p (q n)"),
                                 bT_hi[:, d, ri, :, :].rearrange("p q n -> p (q n)"))
            wait_turns(dve, c)
            V.tensor_copy(smalls[:, 112:114], ident[:, 0:2]).then_inc(ready("heads_turned"), 1)
            dve.wait_ge(ready("bias_in"), 16)

            def ssm_in(i):
                w, ws = wave[:, i % 3, :, :], wave[:, i % 3, ::-1, :]
                dve.wait_ge(ready("ssm_wave"), i + 1)
                dve.wait_ge(ready("ssm_bu"), i + 1)
                if i >= 1:
                    dve.wait_ge(ready("ssm_xp"), 2 * i)
                bu = psum[:, 2 + i % 2, :].rearrange("p (r t) -> p r t", r=2)
                TENS(q1[:], w, bu, ALU.mult)
                TENS(q2[:], ws, bu, ALU.mult).then_inc(ready("ssm_x"), 1)

            def ssm_turn_back(i):
                w, ws = wave[:, i % 3, :, :], wave[:, i % 3, ::-1, :]
                dve.wait_ge(ready("ssm_g"), 2 * i + 2)
                if i >= 1:
                    dve.wait_ge(ready("ssm_h"), i)
                TENS(back1[:], w, gs[:], ALU.mult)
                TENS(back2[:], ws, gs[:], ALU.mult).then_inc(ready("ssm_back"), 1)

            def ssm_states(i):
                dve.wait_ge(ready("ssm_back"), i + 1)
                if i >= 2:
                    dve.wait_ge(ready("ssm_yp"), i - 1)
                o = [states[:, i % 2, ri, ::-1] if i % 2 else states[:, i % 2, ri, :] for ri in range(2)]
                TENS(o[0], back1[:, 0, :], back1[:, 1, :], ALU.subtract)
                TENS(o[1], back2[:, 0, :], back2[:, 1, :], ALU.add).then_inc(ready("ssm_h"), 1)

            def ssm_sums(i):
                dve.wait_ge(ready("ssm_x"), i + 1)
                if i >= 1:
                    dve.wait_ge(ready("ssm_g"), 2 * i)
                TENS(xp[:, 0, :], q1[:, 0, :], q1[:, 1, :], ALU.add).then_inc(ready("ssm_xp"), 1)
                TENS(xp[:, 1, :], q2[:, 1, :], q2[:, 0, :], ALU.subtract).then_inc(ready("ssm_xp"), 1)

            def ssm_scan(i):
                dj = 16 * (i % 2) + i // 2
                if i >= 1:
                    dve.wait_ge(ready("ssm_back"), i)
                rho = par[:, 10, dj:dj + 1].broadcast_to([P, TOK])
                for ri in range(2):
                    dve.wait_ge(ready("ssm_xp"), 2 * i + 1 + ri)
                    V.tensor_tensor_scan(gs[:, ri, :], rho, xp[:, ri, :], 0.0, ALU.mult, ALU.add).then_inc(ready("ssm_g"), 1)

            def ssm_between(j):
                for i in ssm_items(j):
                    ssm_in(i)
                    if i >= 1:
                        ssm_turn_back(i - 1)
                    ssm_sums(i)
                    if i >= 1:
                        ssm_states(i - 1)
                    ssm_scan(i)
                    if i == NDJ - 1:
                        ssm_turn_back(i)
                        ssm_states(i)

            att_dve(dve, c, second_items(), ssm_between)
            dve.wait_ge(ready("ssm_small"), 32)
            for m in range(TT):
                last = TENS(y[:, m, 1024:1536], proj_s[:, m, S_U:S_U + 512], ssm_d[:], ALU.mult)
            link(last)
            dve.wait_ge(ready("ssm_yp"), NDJ)
            for m in range(TT):
                last = TENS(y[:, m, 1024:1536], y[:, m, 1024:1536], psum[:, 6 + m, :], ALU.add)
            last.then_inc(ready("ssm_y"), 1)
            take_act_lo(dve, c, aT_hi, aT_lo, 4)
            block_split(unit_lo, dve, c, 4, BLK)
            evac(dve, c, c.end, c.n["block"] - 1, lambda m: t_glu[:, m, :], lambda m, o, s: TENS(o, s, b_glu[:], ALU.add))
            wait_blocks(dve, c)
            V.tensor_copy(smalls[:, 100:102], ident[:, 0:2]).then_inc(ready("glu_z"), 1)
            dve.wait_ge(ready("glu_s"), 1)
            TENS(y[:, :, 1024:1536], y[:, :, 1024:1536], t_glu[:], ALU.mult).then_inc(ready("ssm_out"), 1)
            dve.wait_ge(ready("out_rms"), 1)
            link(V.reciprocal(rms[:, 0:6], rms[:, 0:6]))
            dve.wait_ge(ready("out_norms"), 48)
            for m in range(TT):
                for j, (lo, w) in enumerate(((0, 1024), (1024, 512), (1536, 512))):
                    o = y[:, m, lo:lo + w]
                    last = STT(out=o, in0=o, scalar=rms[:, 3 * m + j:3 * m + j + 1], in1=gain_a[:, lo:lo + w],
                               op0=ALU.mult, op1=ALU.mult)
            last.then_inc(ready("mix_done"), 1)
            take_act_lo(dve, c, aT_hi, aT_lo, KT_D)
            V.tensor_copy(smalls[:, 102:104], ident[:, 0:2]).then_inc(ready("mix_turned"), 1)
            project(0, [(0, BLK)] * 3)
            if upto >= 6:
                lead_early(unit_lo, dve, c)
            add_normed(2, gain_b, "mix_post_g")
        if upto >= 6:
            normed_lead(3, mlp_g[0], "mlp_pre_g")
            hidden(2)
            add_normed(4, mlp_g[1], "mlp_post_g")

    @block.tensor
    def _(pe):
        c = Count()
        MM = nc.tensor.matmul

        def project(pairs, rest, kts=KT_D, k0=0, led=False):
            if not led:
                wait_turns(pe, c)
                block_mm(pe, c, kts, BLK, aT_hi, aT_lo, k0)
            if pairs:
                with c.loop(pe, pairs, {"unit": 16, "block": 2}):
                    for _ in range(2):
                        block_mm(pe, c, kts, BLK, aT_hi, aT_lo, k0)
            for _, cols in rest:
                block_mm(pe, c, kts, cols, aT_hi, aT_lo, k0)

        def hidden(which):
            w1, w2, n, cols, kts = ffn(which)
            h = ft_h[which // 2]

            def turn_hidden(second, times):
                if which < 2:
                    pe.wait_ge(acc_free[second % 2], c.freed(second))
                else:
                    pe.wait_ge(ready("hidden_h"), times)
                turn_act(pe, c, lambda m, k: h[:, m, k * P:(k + 1) * P], kts)

            def step(second, times):
                if second is not None:
                    block_mm(pe, c, KT_D, BLK, aT_hi, aT_lo)
                    turn_hidden(second, times)
                block_mm(pe, c, KT_D, BLK, aT_hi, aT_lo)
                if second is not None:
                    pe.wait_ge(turn_free[0], c.now("turn", 1, 2))
                    pe.wait_ge(turn_free[1], c.now("turn", 0, 2))
                    for _ in range(4):
                        block_mm(pe, c, kts, BLK, hT_hi, hT_lo)
            step(None, 0)
            step(c.n["block"] - 1, 2)
            with c.loop(pe, n - 2, ffn_body(kts)) as i:
                step(c.n["block"] - 5, 4 + 2 * i)
            turn_hidden(c.n["block"] - 5, 2 * n)
            wait_turns(pe, c)
            for _ in range(4):
                block_mm(pe, c, kts, BLK, hT_hi, hT_lo)

        def heads(src, col, n, w=P, step=P):
            for h in range(0, n, 2):
                turn(pe, c, [src[:, m, col + (h + j) * step:col + (h + j) * step + w] for j in range(2) for m in range(TT)])

        def of_x(m, k):
            return x[:, m, k * P:(k + 1) * P]

        def of_pre(m, k):
            return pre[:, m, k * P:(k + 1) * P]

        pe.wait_ge(ready("ident"), 16)
        lead_mm(pe, c, of_x, lambda q: pe.wait_ge(ready(f"x_in{q}"), 16 * TT))
        project(0, [(0, BLK)] * (GATE_AT - 1), led=True)
        narrow_mm(pe, c, 16)
        block_mm(pe, c, KT_D, BLK, aT_hi, aT_lo)
        block_mm(pe, c, KT_D, BLK, aT_hi, aT_lo)
        with c.loop(pe, 2, {"unit": 16, "block": 2}):
            for _ in range(2):
                block_mm(pe, c, KT_D, BLK, aT_hi, aT_lo)
        pe.wait_ge(ready("even_small"), 16 * 6)
        pe.wait_ge(acc_free[GATE_AT % 2], GATE_AT // 2 + 1)
        for h in range(4):
            last = MM(psum[:, 6 + h // 2, (h % 2) * TOK:(h % 2 + 1) * TOK], wg2[:, h * P:(h + 1) * P], g1T[:],
                      start=True, stop=True)
        last.then_inc(ready("gla_z"), 1)
        for _ in LAST5:
            block_mm(pe, c, KT_D, BLK, aT_hi, aT_lo)
        wait_blocks(pe, c)
        heads(proj_e, G_Q, 4)
        heads(proj_e, G_K, 4)
        pe.wait_ge(ready("gla_ke"), 1)
        for m in range(TT):
            turn(pe, c, [gke[:, h * TOK + m * P:h * TOK + (m + 1) * P] for h in range(4)])
        wait_turns(pe, c)

        def half(n):
            return slice(64 * (n % 2), 64 * (n % 2) + 64)

        for h in range(4):
            if h >= 2:
                pe.wait_ge(ready("gla_state"), h - 1)
            for n in range(3):
                o = psum[:, 2 * (h % 2) + n % 2, (n // 2) * 256:(n // 2) * 256 + 256]
                last = MM(o, gkt[half(n), n // 2, h * P:(h + 1) * P],
                          proj_e[half(n), n // 2, G_V + h * 256:G_V + (h + 1) * 256], start=True, stop=True)
            last.then_inc(ready("gla_loc"), 1)
        pe.wait_ge(ready("gla_qk"), 1)

        def gla_scores(j):
            h, m = j // 2, j % 2
            if j >= 2:
                pe.wait_ge(ready("gla_sm"), j - 1)
            MM(psum[:, 6 + j % 2, :P], gk[:, h, m * P:(m + 1) * P], gq[:, h, m * P:(m + 1) * P],
               start=True, stop=True).then_inc(ready("gla_s"), 1)

        gla_scores(0)
        pe.wait_ge(ready("gla_state"), 4)
        for j in range(8):
            h, m = j // 2, j % 2
            if j < 7:
                gla_scores(j + 1)
            pe.wait_ge(ready("gla_sm"), j + 1)
            if j >= 2:
                pe.wait_ge(ready("gla_o_out"), j - 1)
            v = proj_e[:, m, G_V + h * 256:G_V + (h + 1) * 256]
            last = MM(psum[:, 4 + j % 2, :256], gsT[:, j % 2, :], v, start=True, stop=True, skip_group_check=True)
            for n in (2 * m, 2 * m + 1):
                if n:
                    last = MM(psum[half(n), 4 + j % 2, :256], gq[:, h, n * CHUNK:(n + 1) * CHUNK], gst[:, h, n - 1, :],
                              start=False, stop=True, skip_group_check=True)
            last.then_inc(ready("gla_o"), 1)
        pe.wait_ge(ready("gla_done"), 1)
        heads(proj_e, D_Q, 12)
        heads(proj_e, D_K, 12)
        wait_turns(pe, c)
        att_pe(pe, c, dil_items())
        pe.wait_ge(att_done, 8)

        def mixed_e(m, k):
            if k < 8:
                return proj_e[:, m, G_R + k * P:G_R + (k + 1) * P]
            return dil_o[:, m, (k - 8) * P:(k - 7) * P]
        turn_act(pe, c, mixed_e, 12)
        project(0, [(0, BLK)] * 3, 12)
        if upto >= 2:
            lead_mm(pe, c, of_x, lambda q: pe.wait_ge(ready("x_quarter"), q + 1))
            hidden(0)
        if upto >= 3:
            lead_mm(pe, c, of_x, lambda q: pe.wait_ge(ready("x_quarter"), 4 + q + 1))
            project(3, [], led=True)
            narrow_mm(pe, c, 72)
            block_mm(pe, c, KT_D, BLK, aT_hi, aT_lo)
            pe.wait_ge(acc_free[c.n["block"] % 2], c.freed(c.n["block"] - 2))
            turn(pe, c, [tail_T[:, m * P:(m + 1) * P] for m in range(TT)])
            pe.wait_ge(ready("mla_normed"), 1)
            turn_act(pe, c, lambda m, k: proj_o[:, m, L_Q + k * P:L_Q + (k + 1) * P], 8)
            project(0, [(0, BLK)] * 2, 4)
            project(0, [(0, BLK)] * 3, 4, 4)
            pe.wait_ge(ready("roped"), 1)
            heads(qb, 0, 8, P, 192)
            heads(kvb, 0, 8, P, 256)
            heads(qb, P, 8, 64, 192)
            turn(pe, c, [proj_o[:, m, L_KR:L_KR + 64] for m in range(TT)])
            wait_turns(pe, c)
            att_pe(pe, c, mla_items())
            heads(proj_o, M_Q, 8)
            turn(pe, c, [proj_o[:, m, M_I:M_I + 4] for m in range(TT)])
            turn(pe, c, [proj_o[:, m, M_F:M_F + 4] for m in range(TT)])
            pe.wait_ge(ready("ml_exps"), 1)
            for h in range(4):
                last = MM(psum[:, 6, 4 * h:4 * h + 4], head_row[:, h, :], s_old, start=True, stop=True)
            last.then_inc(ready("ml_sold"), 1)
            turn(pe, c, [rows[:, j, m * P:(m + 1) * P] for j in (R_A, R_W, R_E) for m in range(TT)])
            pe.wait_ge(ready("ml_qk"), 1)
            for m in range(TT):
                turn(pe, c, [qk[:, 4 + h, m * P:(m + 1) * P] for h in range(4)])
            pe.wait_ge(ready("ml_kw"), 1)
            for h in range(4):
                if h >= 2:
                    pe.wait_ge(ready("ml_state"), h - 1)
                b3 = ((0, 1, 4), (2, 3, 5))[h % 2]
                for n in range(3):
                    last = MM(psum[:, b3[n], 0:257], kw[half(n), n // 2, h * P:(h + 1) * P],
                              vaug[half(n), n // 2, h, 0:257], start=True, stop=True)
                last.then_inc(ready("ml_loc"), 1)

            def ml_scores(j):
                h, m = j // 2, j % 2
                t = slice(m * P, (m + 1) * P)
                if j >= 2:
                    pe.wait_ge(ready("ml_p"), j - 1)
                o = psum[:, 2 + j % 2, :]
                MM(o[:, 0:128], head_row[:, h, :], rows[:, R_M, t], start=True, stop=True)
                MM(o[:, 128:256], head_row[:, h, :], rows[:, R_IS, t], start=True, stop=True)
                MM(o[:, 256:384], qk[:, 4 + h, t], qk[:, h, t], start=True, stop=True).then_inc(ready("ml_s"), 1)

            pe.wait_ge(ready("ml_state"), 4)
            ml_scores(0)
            for j in range(8):
                h, m = j // 2, j % 2
                if j < 7:
                    ml_scores(j + 1)
                pe.wait_ge(ready("ml_p"), j + 1)
                if j >= 2:
                    pe.wait_ge(ready("ml_out"), j - 1)
                last = MM(psum[:, 6 + j % 2, 0:257], pT[:, j % 2, :], vaug[:, m, h, 0:257], start=True, stop=True,
                          skip_group_check=True)
                for n in (2 * m, 2 * m + 1):
                    if n:
                        last = MM(psum[half(n), 6 + j % 2, 0:257], qs[:, j % 2, half(n)], cst[:, h, n - 1, 0:257],
                                  start=False, stop=True, skip_group_check=True)
                last.then_inc(ready("ml_n"), 1)
            pe.wait_ge(ready("ml_done"), 1)

            def mixed_o(m, k):
                if k < 8:
                    return proj_o[:, m, M_O + k * P:M_O + (k + 1) * P]
                return mla_o[:, m, (k - 8) * P:(k - 7) * P]
            turn_act(pe, c, mixed_o, KT_D)
            project(0, [(0, BLK)] * 3)
        if upto >= 4:
            lead_mm(pe, c, of_x, lambda q: pe.wait_ge(ready("x_quarter"), 8 + q + 1))
            hidden(1)
        if upto >= 5:
            lead_mm(pe, c, of_pre, lambda q: pe.wait_ge(ready("pre_quarter"), q + 1))
            project(3, [(3584, BLK)], led=True)
            pe.wait_ge(ready("mem_normed"), 1)
            turn_act(pe, c, lambda m, k: mem_x[:, m, k * P:(k + 1) * P], KT_D)
            project(0, [(0, BLK)])
            wait_blocks(pe, c)
            heads(proj_s, S_Q, 8)
            heads(proj_s, S_K, 8)
            heads(proj_s, S_MQ, 4)
            heads(kvm, 0, 4)
            heads(proj_s, S_U, 4)
            pe.wait_ge(ready("ssm_bbar"), 1)
            for d in range(2):
                for ri in range(2):
                    turn(pe, c, [bbar[:, ri, 16 * d + 4 * q:16 * d + 4 * q + 4, :].rearrange("p j n -> p (j n)") for q in range(4)])
            wait_turns(pe, c)

            def drive(i):
                d, j = i % 2, i // 2
                q, r = j // 4, slice(32 * (j % 4), 32 * (j % 4) + 32)
                if i >= 2:
                    pe.wait_ge(ready("ssm_x"), i - 1)
                turned_u = slice(None, None, -1) if d else slice(None)
                for ri in range(2):
                    o = psum[:, 2 + i % 2, ri * TOK:(ri + 1) * TOK]
                    MM(o, bT_hi[r, d, ri, q, :], uT_hi[r, q, turned_u], start=True, stop=False)
                    MM(o, bT_hi[r, d, ri, q, :], uT_lo[r, q, turned_u], start=False, stop=False)
                    last = MM(o, bT_lo[r, d, ri, q, :], uT_hi[r, q, turned_u], start=False, stop=True)
                last.then_inc(ready("ssm_bu"), 1)

            def give(i):
                d, j = i % 2, i // 2
                pe.wait_ge(ready("ssm_h"), i + 1)
                if i == 0:
                    pe.wait_ge(ready("ssm_c"), 1)
                for m in range(TT):
                    for ri in range(2):
                        last = MM(psum[:, 6 + m, 32 * j:32 * j + 32], states[:, i % 2, ri, m * P:(m + 1) * P],
                                  cmat[:, ri, 16 * d + j, :], start=(d == 0 and ri == 0), stop=(d == 1 and ri == 1))
                last.then_inc(ready("ssm_yp"), 1)

            def ssm_between(j):
                for i in ssm_items(j):
                    if i + 1 < NDJ:
                        drive(i + 1)
                    if i >= 2:
                        give(i - 2)

            drive(0)
            att_pe(pe, c, second_items(), ssm_between)
            give(NDJ - 2)
            give(NDJ - 1)
            pe.wait_ge(att_done, c.n["att"])
            pe.wait_ge(ready("ssm_gelu"), 1)
            turn_act(pe, c, lambda m, k: y[:, m, 1024 + k * P:1024 + (k + 1) * P], 4)
            project(0, [], 4)
            pe.wait_ge(ready("mix_done"), 1)
            turn_act(pe, c, lambda m, k: y[:, m, k * P:(k + 1) * P], KT_D)
            project(0, [(0, BLK)] * 3)
        if upto >= 6:
            lead_mm(pe, c, of_pre, lambda q: pe.wait_ge(ready("pre_quarter"), 4 + q + 1))
            hidden(2)

    ctx.close()


def program(nc, shapes, dtypes, upto=99):
    aps = {n[3:]: nc.dram_tensor(n, shapes[n], dtypes[n], kind="ExternalInput").ap() for n in shapes}
    out = nc.dram_tensor("out_x", (1, TOK, D), F32, kind="ExternalOutput").ap()
    build(nc, aps, out, upto)


def tables():
    i = np.arange(P)[:, None]
    f = np.float32
    ident = np.eye(P, dtype=f)
    j = np.arange(P)[None, :]
    chunk_pred = ((i <= j) & (i // CHUNK == j // CHUNK)).astype(np.int32)
    restart = np.tile((np.arange(1024) % CHUNK != 0).astype(f), (P, 1))
    parts = []
    for m in range(TT):
        q = np.arange(P)[:, None] + m * P
        k = np.arange(P * (m + 1))[None, :]
        for window, dilation in ((128, 1), (512, 4), (2048, 16)):
            ok = (k <= q) & ((q - k) % dilation == 0) & (q - k <= window)
            parts.append(np.where(ok, 0.0, NEG).astype(f))
    q = np.arange(P)[:, None] + P
    mla = np.where(np.arange(TOK)[None, :] <= q, 0.0, NEG).astype(f)
    inv = (10000.0 ** (-np.arange(0, 64, 2) / 64)).astype(f)
    return {
        "c_ident": ident, "c_chunk_pred": chunk_pred, "c_restart": restart,
        "c_dil_mask": np.concatenate(parts, 1), "c_mla_mask": mla,
        "c_inv_freq": np.tile(inv, (P, 1)), "c_steps": np.tile(np.arange(16).astype(f), (P, 1)),
    }


def laid_out(a):
    f = np.float32
    out = {
        "l_gla_bg": a["even_gla_bg"][0].reshape(4, P).T,
        "l_conv_w": a["odd_conv_w"][0].reshape(4, 8, P).transpose(2, 1, 0),
        "l_conv_b": a["odd_conv_b"][0].reshape(8, P).T,
        "l_gate_b": np.stack([a["odd_mlstm_bi"][0], a["odd_mlstm_bf"][0]], 1),
        "l_pos": a["positions"][0].reshape(TT, P).T,
        "l_ssm_d": a["ssm_d_2"].reshape(1, 512),
    }
    t = np.arange(TOK)
    r, col = t // 64, t % 64
    start = np.clip(col - 8, 0, 48)
    inside = (col[None, :] >= start[:, None]) & (col[None, :] < start[:, None] + 16)
    dr = r[None, :] - r[:, None] + 7
    dc = np.clip(col[None, :] - col[:, None] + 15, 0, 30)
    bias = np.where(inside[None], a["na_rpb_2"][0][:, dr, dc], f(NEG))
    out["l_bias"] = bias.reshape(8, TT, P, TOK).transpose(2, 0, 1, 3).reshape(P, 16, TOK)
    def states(v):
        return v.reshape(2, 16, P).transpose(2, 0, 1).reshape(P, 32)
    dt = np.broadcast_to(a["ssm_log_dt_2"][0][:, :, None], (2, 32, 64))
    out["l_lam"] = np.stack([states(a["ssm_lam_re_2"][0]), states(a["ssm_lam_im_2"][0]), states(dt)], 1)
    b = np.zeros((2, P, 32, 32), f)
    cm = np.zeros((2, P, 32, 32), f)
    for ri, part in enumerate(("re", "im")):
        vb = a[f"ssm_b_{part}_2"][0].reshape(2, 16, 2, 64, 16)
        vc = a[f"ssm_c_{part}_2"][0].reshape(2, 16, 2, 16, 64)
        for g in range(2):
            b[ri, 64 * g:64 * g + 64, :, 16 * g:16 * g + 16] = vb[:, :, g].transpose(2, 0, 1, 3).reshape(64, 32, 16)
            cm[ri, 64 * g:64 * g + 64, :, 16 * g:16 * g + 16] = vc[:, :, g].transpose(3, 0, 1, 2).reshape(64, 32, 16)
    out["l_b"] = b.transpose(1, 0, 2, 3)
    out["l_c"] = cm.transpose(1, 0, 2, 3)
    return out


_DIRECT = ["x", "even_w_in", "even_gla_wg2", "even_gla_norm_g", "even_w_o", "odd_w_in", "odd_mlstm_norm_g",
           "odd_mla_qnorm_g", "odd_mla_kvnorm_g", "odd_mla_wuq", "odd_mla_wukv", "odd_w_o", "ln1_g", "ln1_b",
           "ffn_wgu", "ffn_wd", "ln2_g", "ln2_b", "mem_2", "norm_mix_pre_2", "w_in_2", "w_glu_2", "b_glu_2",
           "mem_norm_2", "w_mem_kv_2", "out_norm_na_2", "out_norm_ssm_2", "out_norm_mem_2", "w_out_2",
           "norm_mix_post_2", "norm_mlp_pre_2", "w_ff1_2", "w_ff2_2", "norm_mlp_post_2"]


def operands(inputs):
    given = {n: inputs[n] for n in _DIRECT} | laid_out(inputs) | tables()
    return {f"in_{n}": np.ascontiguousarray(a) for n, a in given.items()}


def kernel(**inputs):
    import concourse.bacc as _bacc
    from concourse.bass_utils import run_bass_kernel_spmd as _run

    arrays = operands({n: np.asarray(a) for n, a in inputs.items()})
    nc = _bacc.Bacc("TRN2", target_bir_lowering=False, num_devices=1)
    program(nc, {n: a.shape for n, a in arrays.items()}, {n: mybir.dt.from_np(a.dtype) for n, a in arrays.items()})
    r = _run(nc, [arrays], core_ids=[0])
    return r.results[0]["out_x"]
```
